# Optimizing a Trainium2 kernel written in Bass

```python
import math
import jax, jax.numpy as jnp
from jax import lax
import numpy as np

D_MODEL = 1024
BATCH = 1
SEQ = 256
DEPTH = 2

ATTN_HEADS = 8
ATTN_HEAD_DIM = 64
ATTN_WIDTH = ATTN_HEADS * ATTN_HEAD_DIM
POOL_WINDOWS = (2, 4, 8, 16)
POOL_GROUPS = len(POOL_WINDOWS)
POOL_GROUP_DIM = 64
POOL_WIDTH = POOL_GROUPS * POOL_GROUP_DIM
SSM_GROUPS = 16
SSM_GROUP_DIM = 16
SSM_STATE = 64
SSM_WIDTH = SSM_GROUPS * SSM_GROUP_DIM
MIX_WIDTH = ATTN_WIDTH + POOL_WIDTH + SSM_WIDTH
Q_BLOCK = 128

Q_OFF = 0
K_OFF = Q_OFF + ATTN_WIDTH
V_OFF = K_OFF + ATTN_WIDTH
F_OFF = V_OFF + ATTN_WIDTH
P_OFF = F_OFF + ATTN_HEADS
S_OFF = P_OFF + POOL_WIDTH
N_IN = S_OFF + SSM_WIDTH

FFN_DIM = 2816
N_EXPERTS = 8
TOP_K = 2
EXPERT_DIM = 3584
N_DENSE = (DEPTH + 1) // 2
N_MOE = DEPTH // 2

RMS_EPS = 1e-6
DT_MIN = 1e-3
DT_MAX = 1e-1
NEG_INF = -1e30

kernel_name = "hybrid_fox_pool_s5_moe_trunk"

def rmsnorm(x, g):
    xf = x.astype(jnp.float32)
    y = xf * lax.rsqrt(jnp.mean(xf * xf, axis=-1, keepdims=True) + RMS_EPS)
    return (y * g.astype(jnp.float32)).astype(x.dtype)

def forgetting_attention(q, k, v, log_f):
    b, L, H, dh = q.shape
    nb = L // Q_BLOCK
    qf = q.astype(jnp.float32) * (dh ** -0.5)
    kh = k.astype(jnp.float32).transpose(0, 2, 1, 3)
    vh = v.astype(jnp.float32).transpose(0, 2, 1, 3)
    c = jnp.cumsum(log_f.astype(jnp.float32), axis=1)
    ck = c.transpose(0, 2, 1)
    qb = qf.reshape(b, nb, Q_BLOCK, H, dh).transpose(1, 0, 3, 2, 4)
    cb = c.reshape(b, nb, Q_BLOCK, H).transpose(1, 0, 3, 2)
    kpos = jnp.arange(L)

    def block(args):
        q_blk, c_blk, start = args
        s = jnp.einsum('bhqd,bhkd->bhqk', q_blk, kh) + c_blk[..., None] - ck[:, :, None, :]
        qpos = start + jnp.arange(Q_BLOCK)
        s = jnp.where(kpos[None, :] <= qpos[:, None], s, NEG_INF)
        p = jax.nn.softmax(s, axis=-1)
        return jnp.einsum('bhqk,bhkd->bhqd', p, vh)

    o = lax.map(block, (qb, cb, jnp.arange(nb, dtype=jnp.int32) * Q_BLOCK))
    return o.transpose(1, 0, 3, 2, 4).reshape(b, L, H * dh)

def pooling_mixer(u, w, scale):
    b, L, _ = u.shape
    uf = u.astype(jnp.float32).reshape(b, L, POOL_GROUPS, POOL_GROUP_DIM)
    cs = jnp.cumsum(uf, axis=1)
    t = jnp.arange(L, dtype=jnp.float32)
    outs = []
    for g, win in enumerate(POOL_WINDOWS):
        csg = cs[:, :, g]
        prev = jnp.pad(csg, ((0, 0), (win, 0), (0, 0)))[:, :L]
        count = jnp.minimum(t + 1.0, float(win))[None, :, None]
        outs.append((csg - prev) / count - uf[:, :, g])
    d = jnp.stack(outs, axis=2)
    y = jnp.einsum('blgc,gcd->blgd', d, w.astype(jnp.float32)).reshape(b, L, POOL_WIDTH)
    return y * scale.astype(jnp.float32)

def ssm_mixer(u, a_re, a_im, b_re, b_im, c_re, c_im, d, log_dt, w_glu, b_glu):
    bsz, L, _ = u.shape
    uf = u.astype(jnp.float32).reshape(bsz, L, SSM_GROUPS, SSM_GROUP_DIM)
    lam = lax.complex(a_re.astype(jnp.float32), a_im.astype(jnp.float32))
    dt = jnp.exp(log_dt.astype(jnp.float32))[:, None]
    lam_bar = jnp.exp(lam * dt)
    bmat = lax.complex(b_re.astype(jnp.float32), b_im.astype(jnp.float32))
    cmat = lax.complex(c_re.astype(jnp.float32), c_im.astype(jnp.float32))
    b_bar = ((lam_bar - 1.0) / lam)[:, :, None] * bmat
    bu = jnp.einsum('blgh,gph->blgp', uf.astype(jnp.complex64), b_bar)
    a = jnp.broadcast_to(lam_bar, bu.shape)

    def combine(left, right):
        a1, b1 = left
        a2, b2 = right
        return a1 * a2, a2 * b1 + b2

    _, xs = lax.associative_scan(combine, (a, bu), axis=1)
    y = jnp.einsum('blgp,ghp->blgh', xs, cmat).real + d.astype(jnp.float32) * uf
    y = jax.nn.gelu(y.reshape(bsz, L, SSM_WIDTH))
    return y * jax.nn.sigmoid(y @ w_glu.astype(jnp.float32) + b_glu.astype(jnp.float32))

def swiglu(h, wg, wu, wd):
    return (jax.nn.silu(h @ wg) * (h @ wu)) @ wd

def moe_swiglu(h, router, wg, wu, wd):
    b, L, D = h.shape
    t = h.reshape(-1, D)
    logits = t.astype(jnp.float32) @ router.astype(jnp.float32)
    top_v, top_i = lax.top_k(logits, TOP_K)
    gates = jax.nn.softmax(top_v, axis=-1)
    comb = jnp.einsum('nk,nke->ne', gates, jax.nn.one_hot(top_i, N_EXPERTS, dtype=jnp.float32))
    out = jnp.zeros(t.shape, jnp.float32)
    for e in range(N_EXPERTS):
        out = out + comb[:, e:e + 1] * swiglu(t, wg[e], wu[e], wd[e]).astype(jnp.float32)
    return out.astype(h.dtype).reshape(b, L, D)

def setup_inputs(seed: int = 0) -> dict:
    key = jax.random.key(seed)
    ks = list(jax.random.split(key, 40))
    nxt = iter(ks)

    def nrm(shape, scale):
        return jax.random.normal(next(nxt), shape, jnp.float32) * scale

    def gain(shape):
        return 1.0 + nrm(shape, 0.1)

    n_idx = jnp.arange(SSM_STATE, dtype=jnp.float32)
    inp = {}
    inp['x'] = nrm((BATCH, SEQ, D_MODEL), 1.0)
    inp['norm_mix_pre'] = gain((DEPTH, D_MODEL))
    inp['norm_mix_post'] = gain((DEPTH, D_MODEL))
    inp['norm_ffn_pre'] = gain((DEPTH, D_MODEL))
    inp['norm_ffn_post'] = gain((DEPTH, D_MODEL))
    inp['w_in'] = nrm((DEPTH, D_MODEL, N_IN), D_MODEL ** -0.5)
    inp['b_forget'] = nrm((DEPTH, ATTN_HEADS), 0.1)
    inp['pool_w'] = nrm((DEPTH, POOL_GROUPS, POOL_GROUP_DIM, POOL_GROUP_DIM), POOL_GROUP_DIM ** -0.5)
    inp['pool_scale'] = gain((DEPTH, POOL_WIDTH))
    inp['ssm_a_re'] = -0.5 + nrm((DEPTH, SSM_GROUPS, SSM_STATE), 0.01)
    inp['ssm_a_im'] = math.pi * n_idx[None, None, :] + nrm((DEPTH, SSM_GROUPS, SSM_STATE), 0.01)
    inp['ssm_b_re'] = nrm((DEPTH, SSM_GROUPS, SSM_STATE, SSM_GROUP_DIM), (2 * SSM_GROUP_DIM) ** -0.5)
    inp['ssm_b_im'] = nrm((DEPTH, SSM_GROUPS, SSM_STATE, SSM_GROUP_DIM), (2 * SSM_GROUP_DIM) ** -0.5)
    inp['ssm_c_re'] = nrm((DEPTH, SSM_GROUPS, SSM_GROUP_DIM, SSM_STATE), (2 * SSM_STATE) ** -0.5)
    inp['ssm_c_im'] = nrm((DEPTH, SSM_GROUPS, SSM_GROUP_DIM, SSM_STATE), (2 * SSM_STATE) ** -0.5)
    inp['ssm_d'] = nrm((DEPTH, SSM_GROUPS, SSM_GROUP_DIM), 1.0)
    inp['ssm_log_dt'] = jax.random.uniform(next(nxt), (DEPTH, SSM_GROUPS), jnp.float32,
                                           math.log(DT_MIN), math.log(DT_MAX))
    inp['ssm_w_glu'] = nrm((DEPTH, SSM_WIDTH, SSM_WIDTH), SSM_WIDTH ** -0.5)
    inp['ssm_b_glu'] = nrm((DEPTH, SSM_WIDTH), 0.01)
    inp['branch_norm_attn'] = gain((DEPTH, ATTN_WIDTH))
    inp['branch_norm_pool'] = gain((DEPTH, POOL_WIDTH))
    inp['branch_norm_ssm'] = gain((DEPTH, SSM_WIDTH))
    inp['w_out'] = nrm((DEPTH, MIX_WIDTH, D_MODEL), MIX_WIDTH ** -0.5)
    inp['ffn_w_gate'] = nrm((N_DENSE, D_MODEL, FFN_DIM), D_MODEL ** -0.5)
    inp['ffn_w_up'] = nrm((N_DENSE, D_MODEL, FFN_DIM), D_MODEL ** -0.5)
    inp['ffn_w_down'] = nrm((N_DENSE, FFN_DIM, D_MODEL), FFN_DIM ** -0.5)
    inp['moe_router'] = nrm((N_MOE, D_MODEL, N_EXPERTS), D_MODEL ** -0.5)
    inp['moe_w_gate'] = nrm((N_MOE, N_EXPERTS, D_MODEL, EXPERT_DIM), D_MODEL ** -0.5)
    inp['moe_w_up'] = nrm((N_MOE, N_EXPERTS, D_MODEL, EXPERT_DIM), D_MODEL ** -0.5)
    inp['moe_w_down'] = nrm((N_MOE, N_EXPERTS, EXPERT_DIM, D_MODEL), EXPERT_DIM ** -0.5)
    return inp

def reference(x, norm_mix_pre, norm_mix_post, norm_ffn_pre, norm_ffn_post, w_in, b_forget,
              pool_w, pool_scale, ssm_a_re, ssm_a_im, ssm_b_re, ssm_b_im, ssm_c_re, ssm_c_im,
              ssm_d, ssm_log_dt, ssm_w_glu, ssm_b_glu, branch_norm_attn, branch_norm_pool,
              branch_norm_ssm, w_out, ffn_w_gate, ffn_w_up, ffn_w_down, moe_router,
              moe_w_gate, moe_w_up, moe_w_down):
    b, L, _ = x.shape
    for i in range(DEPTH):
        h = rmsnorm(x, norm_mix_pre[i])
        proj = h @ w_in[i]
        q = proj[..., Q_OFF:Q_OFF + ATTN_WIDTH].reshape(b, L, ATTN_HEADS, ATTN_HEAD_DIM)
        k = proj[..., K_OFF:K_OFF + ATTN_WIDTH].reshape(b, L, ATTN_HEADS, ATTN_HEAD_DIM)
        v = proj[..., V_OFF:V_OFF + ATTN_WIDTH].reshape(b, L, ATTN_HEADS, ATTN_HEAD_DIM)
        log_f = jax.nn.log_sigmoid((proj[..., F_OFF:F_OFF + ATTN_HEADS] + b_forget[i]).astype(jnp.float32))
        attn = forgetting_attention(q, k, v, log_f).astype(x.dtype)
        pool = pooling_mixer(proj[..., P_OFF:P_OFF + POOL_WIDTH], pool_w[i], pool_scale[i]).astype(x.dtype)
        ssm = ssm_mixer(proj[..., S_OFF:S_OFF + SSM_WIDTH], ssm_a_re[i], ssm_a_im[i], ssm_b_re[i],
                        ssm_b_im[i], ssm_c_re[i], ssm_c_im[i], ssm_d[i], ssm_log_dt[i],
                        ssm_w_glu[i], ssm_b_glu[i]).astype(x.dtype)
        mixed = jnp.concatenate([rmsnorm(attn, branch_norm_attn[i]),
                                 rmsnorm(pool, branch_norm_pool[i]),
                                 rmsnorm(ssm, branch_norm_ssm[i])], axis=-1)
        x = x + rmsnorm(mixed @ w_out[i], norm_mix_post[i])
        h = rmsnorm(x, norm_ffn_pre[i])
        if i % 2 == 0:
            j = i // 2
            f = swiglu(h, ffn_w_gate[j], ffn_w_up[j], ffn_w_down[j])
        else:
            j = i // 2
            f = moe_swiglu(h, moe_router[j], moe_w_gate[j], moe_w_up[j], moe_w_down[j])
        x = x + rmsnorm(f, norm_ffn_post[i])
    return x


_drawn_inputs = setup_inputs


def setup_inputs(seed=0):
    import zlib

    import numpy as np

    out = dict(_drawn_inputs(seed))
    spreads = {}
    factors = {'ssm_a_re': 8.0, 'ssm_b_glu': 4.009}
    for name, (base, spread) in spreads.items():
        noise = np.random.default_rng([zlib.crc32(name.encode()), seed]).standard_normal(out[name].shape)
        drawn = base * np.exp(spread * noise) if base else spread * noise
        out[name] = __import__('jax').numpy.asarray(drawn.astype(out[name].dtype))
    for name, factor in factors.items():
        out[name] = (out[name] * factor).astype(out[name].dtype)
    return out
```

```python
import math
from contextlib import ExitStack

import numpy as np

import concourse.bass as bass
from concourse import mybir

P = 128
T = 256
TB = T // P
D = 1024
KT = D // P
LAYERS = 2
HEADS, DH = 8, 64
WINDOWS = (2, 4, 8, 16)
NG, GC = 4, 64
SJ = 8
SCH = 32
F_OFF, P_OFF, S_OFF = 1536, 1544, 1800
FFN = 2816
FT_DENSE = FFN // P
NE = 8
EDIM = 3584
FT_MOE = EDIM // P
SLOTS = 128
PASSES = -(-T // SLOTS)
EPS = 1e-6
NEG = -1e30
ROUND = 1.5 * 2.0 ** 23
TURN = 6.283185

SLAB = 2048
NSLOT = 7
W_COLS = 256
MIX_SLABS = 8 + 4
DENSE_SLABS = 3 * (FT_DENSE // 2)
MOE_SLABS = 3 * (FT_MOE // 2)
BASE_MIX = (0, MIX_SLABS + DENSE_SLABS)
BASE_DENSE = MIX_SLABS
BASE_MOE = BASE_MIX[1] + MIX_SLABS
assert MOE_SLABS % NSLOT == 0

_off = {}
_n = 0
for _name, _w in (("g_mix", KT), ("g_ffn", KT), ("g_br", KT), ("pool_scale", 2), ("ssm_d", 2),
                  ("b_glu", 2), ("b_forget", 1), ("a_re", SJ), ("a_im", SJ), ("log_dt", SJ),
                  ("w_f", KT * HEADS), ("router", KT * NE), ("b_re", 2 * P), ("b_im", 2 * P),
                  ("c_re", SJ * SCH), ("c_im", SJ * SCH), ("pool_w", 2 * P), ("w_glu", 2 * T)):
    _off[_name] = (_n, _n + _w)
    _n += _w
NPAR = _n
C_ID, C_MASK, C_TRI, C_ONES, C_IOTA, C_BAND = 0, P, 2 * P, 3 * P, 4 * P, 4 * P + T
NCONST = C_BAND + NG * 3 * P

F32 = mybir.dt.float32
I32 = mybir.dt.int32
U32 = mybir.dt.uint32
ALU = mybir.AluOpType
ACT = mybir.ActivationFunctionType
AX = mybir.AxisListType.X


def build(nc, x, w_in, w_out, ffn_gate, ffn_up, ffn_down, moe_gate, moe_up, moe_down, g_post, params, consts, c_dram, out):
    ctx = ExitStack()
    with ctx:
        def sb(name, shape, dt=F32):
            return ctx.enter_context(nc.sbuf_tensor(name, shape, dt))

        def sem(name):
            return ctx.enter_context(nc.semaphore(name))

        RING = sb("RING", [P, NSLOT, SLAB])
        X = sb("X", [P, TB, D])
        XN = sb("XN", [P, TB, D])
        HT = sb("HT", [P, KT, T])
        SQ = HT
        QA = sb("QA", [DH + 2, HEADS, T])
        KA = sb("KA", [DH + 2, HEADS, T])
        V = sb("V", [P, TB, HEADS * DH])
        MT = sb("MT", [P, KT, T])
        SCR = sb("SCR", [P, 9, 2 * T])
        ROT = SCR[:, 0:2, :]
        ZIN = SCR[:, 2, :]
        Z = SCR[:, 3:5, :]
        ZC = SCR[:, 5:7, :]
        ZS = SCR[:, 7:9, :]
        P0 = SCR[:, 0:2, :].rearrange("p a (h k) -> p (a h) k", k=P)
        P1 = SCR[:, 2:6, :].rearrange("p a (h k) -> p (a h) k", k=T)
        TRIG = sb("TRIG", [P, 2, SJ, T])
        COS = TRIG[:, 0, :, :]
        SIN = TRIG[:, 1, :, :]
        PAR = sb("PAR", [P, LAYERS, NPAR])
        CST = sb("CST", [P, NCONST])
        GB = sb("GB", [P, D])
        TMP = sb("TMP", [P, D])
        UT = sb("UT", [P, 2, T])
        UP = sb("UP", [P, TB, T])
        DT = sb("DT", [P, 2, T])
        GY = sb("GY", [P, 2, T])
        SG = sb("SG", [P, 2, T])
        YS = sb("YS", [P, 2, T])
        PTS = sb("PTS", [P, 2, 3 * P])
        RB = sb("RB", [P, 3, T])
        CC = sb("CC", [P, 3, SJ, SCH])
        CT = sb("CT", [P, 2, SJ, SCH])
        SV = sb("SV", [P, 24, SJ])
        FG = sb("FG", [HEADS, 6, T])
        MX = sb("MX", [P, 16])
        SUM = sb("SUM", [P, 16])
        RS = sb("RS", [P, 16])
        STAT = sb("STAT", [P, 8])
        RSTD = sb("RSTD", [P, 4])
        EXPO = sb("EXPO", [P, 4])
        AT = DT
        SA = GY
        MOEB = TRIG[:, :, :, :].rearrange("p a j t -> p (a j t)")
        XG = MOEB[:, 0:KT * SLOTS].rearrange("p (k s) -> p k s", k=KT)
        at_ = KT * SLOTS
        GM = MOEB[:, at_:at_ + TB * SLOTS].rearrange("p (b s) -> p b s", b=TB)
        at_ += TB * SLOTS
        GW = MOEB[:, at_:at_ + TB * SLOTS].rearrange("p (b s) -> p b s", b=TB)
        at_ += TB * SLOTS
        GT = MOEB[0:SLOTS, at_:at_ + T]
        at_ += T
        YE = MOEB[0:SLOTS, at_:at_ + D]
        LG = sb("LG", [P, TB, NE])
        M8 = sb("M8", [P, TB, 8])
        I8 = sb("I8", [P, TB, 8], U32)
        IF8 = sb("IF8", [P, TB, 8])
        OH = sb("OH", [P, 2, TB, NE])
        SEL = sb("SEL", [P, TB, NE])
        GATE = sb("GATE", [P, TB, 4])
        NI = (PASSES + 1) * NE
        POS = sb("POS", [P, TB, NI])
        CMB = sb("CMB", [P, TB, NI])
        CNT = sb("CNT", [P, 4])
        OVER = sb("OVER", [P, 1], I32)

        bank = [ctx.enter_context(nc.psum_tensor(f"bank{i}", [P, 512], F32)) for i in range(8)]
        ident = CST[:, C_ID:C_ID + P]
        mask = CST[:, C_MASK:C_MASK + P]
        tri = CST[:, C_TRI:C_TRI + P]
        ones = CST[:, C_ONES:C_ONES + P]
        iota = CST[:, C_IOTA:C_IOTA + T]
        band = CST[:, C_BAND:NCONST].rearrange("p (g b t) -> p g b t", g=NG, b=3)

        def par(l, name):
            a, b = _off[name]
            return PAR[:, l, a:b]

        x_in = sem("x_in")
        par_in = sem("par_in")
        cst_in = sem("cst_in")
        gb_in = sem("gb_in")
        slab_in = [sem(f"slab_in{i}") for i in range(NSLOT)]
        slabs_used = sem("slabs_used")
        out_done = sem("out_done")
        sq_done = sem("sq_done")
        var_done = sem("var_done")
        rstd_done = sem("rstd_done")
        xn_done = sem("xn_done")
        ht_tr = sem("ht_tr")
        ht_v = sem("ht_v")
        ht_a = sem("ht_a")
        f_ps = sem("f_ps")
        ut_done = sem("ut_done")
        up_done = sem("up_done")
        qkv_done = sem("qkv_done")
        fz_a = sem("fz_a")
        fz_v = sem("fz_v")
        c_out = sem("c_out")
        c_rows = sem("c_rows")
        aug_ones = sem("aug_ones")
        bu_done = sem("bu_done")
        rot_done = sem("rot_done")
        zin_done = sem("zin_done")
        z_done = sem("z_done")
        zr_done = sem("zr_done")
        y_done = sem("y_done")
        trig_v = sem("trig_v")
        trig_a = sem("trig_a")
        tab_ok = sem("tab_ok")
        dt_ps = sem("dt_ps")
        dt_done = sem("dt_done")
        pl_ps = sem("pl_ps")
        mt_pool = sem("mt_pool")
        ys_done = sem("ys_done")
        gy_done = sem("gy_done")
        glu_ps = sem("glu_ps")
        sg_done = sem("sg_done")
        mt_ssm = sem("mt_ssm")
        sc_ps = sem("sc_ps")
        msk_done = sem("msk_done")
        mx_done = sem("mx_done")
        ex_done = sem("ex_done")
        rs_done = sem("rs_done")
        pn_done = sem("pn_done")
        pt_ps = sem("pt_ps")
        pt_done = sem("pt_done")
        ot_ps = sem("ot_ps")
        ot_done = sem("ot_done")
        bsq = sem("bsq")
        bss_ps = sem("bss_ps")
        bvar = sem("bvar")
        brs = sem("brs")
        mtn = sem("mtn")
        mix_ps = sem("mix_ps")
        up_ps = sem("up_ps")
        silu_d = sem("silu_d")
        act_d = sem("act_d")
        post_tmp = sem("post_tmp")
        x_done = sem("x_done")
        lg_ps = sem("lg_ps")
        gate_d = sem("gate_d")
        gate_e = sem("gate_e")
        sel_done = sem("sel_done")
        pos_ps = sem("pos_ps")
        route_ok = sem("route_ok")
        g_done = sem("g_done")
        ga_ps = sem("ga_ps")
        xg_done = sem("xg_done")
        gu_ps = sem("gu_ps")
        silu_m = sem("silu_m")
        act_m = sem("act_m")
        gt_done = sem("gt_done")
        y_v = sem("y_v")
        y_a = sem("y_a")
        acc_all = sem("acc_all")
        chain = sem("chain")

        block = ctx.enter_context(nc.Block())

        @block.sync
        def _(sp):
            def load(n, src, shape_of):
                slot = n % NSLOT
                if n >= NSLOT:
                    sp.wait_ge(slabs_used, n - NSLOT + 1)
                sp.dma_start(shape_of(slot), src).then_inc(slab_in[slot], 16)

            def cols(slot):
                return RING[:, slot, :].rearrange("p (k n) -> p k n", k=KT)

            def rows(slot):
                return RING[:, slot, :].rearrange("p (k n) -> p k n", k=2)

            w_in_v = w_in.rearrange("l (k p) n -> l p k n", p=P)
            w_out_v = w_out.rearrange("l (b k p) n -> l b p k n", p=P, k=2)
            gate_v = ffn_gate.rearrange("(k p) n -> p k n", p=P)
            up_v = ffn_up.rearrange("(k p) n -> p k n", p=P)
            down_v = ffn_down.rearrange("(u k p) n -> u p k n", p=P, k=2)
            mg_v = moe_gate.rearrange("e (k p) n -> p e k n", p=P)
            mu_v = moe_up.rearrange("e (k p) n -> p e k n", p=P)
            md_v = moe_down.rearrange("e (u k p) n -> p e u k n", p=P, k=2)

            sp.dma_start(X[:, :, :], x.rearrange("(b p) d -> p b d", p=P)).then_inc(x_in, 16)
            sp.dma_start(CST[:, :], consts).then_inc(cst_in, 16)
            sp.dma_start(PAR[:, :, :], params).then_inc(par_in, 16)
            for l in range(LAYERS):
                b = BASE_MIX[l]
                for n, c in enumerate((S_OFF, P_OFF, 0, 256, 512, 768, 1024, 1280)):
                    load(b + n, w_in_v[l, :, :, c:c + W_COLS], cols)
                for n, r in enumerate((2, 3, 0, 1)):
                    load(b + 8 + n, w_out_v[l, r, :, :, :], rows)
                if l == 0:
                    for u in range(FT_DENSE // 2):
                        load(BASE_DENSE + 3 * u, gate_v[:, :, u * W_COLS:(u + 1) * W_COLS], cols)
                        load(BASE_DENSE + 3 * u + 1, up_v[:, :, u * W_COLS:(u + 1) * W_COLS], cols)
                        load(BASE_DENSE + 3 * u + 2, down_v[u, :, :, :], rows)

            def load_expert(i, e):
                for m in range(MOE_SLABS):
                    slot = (BASE_MOE + m) % NSLOT
                    sp.wait_ge(slabs_used, i * MOE_SLABS + (BASE_MOE + m - NSLOT + 1))
                    u, kind = m // 3, m % 3
                    if kind < 2:
                        v = (mg_v, mu_v)[kind]
                        src = v[:, bass.ds(e, 1), :, u * W_COLS:(u + 1) * W_COLS]
                        dst = cols(slot)
                    else:
                        src = md_v[:, bass.ds(e, 1), u, :, :]
                        dst = rows(slot)
                    sp.dma_start(dst.unsqueeze(1), src).then_inc(slab_in[slot], 16)

            with sp.Fori(0, NE) as e:
                load_expert(e, e)
            sp.wait_ge(route_ok, 1)
            over = sp.value_load(OVER[0:1, 0:1], min_val=0, max_val=T)
            with sp.If(over > SLOTS):
                for p in range(1, PASSES):
                    with sp.Fori(0, NE) as e:
                        load_expert(e + p * NE, e)
            sp.wait_ge(x_done, 16)
            sp.dma_start(out.rearrange("(b p) d -> p b d", p=P), X[:, :, :]).then_inc(out_done, 16)
            sp.wait_ge(out_done, 16)

        def arrived(eng, n):
            eng.wait_ge(slab_in[n % NSLOT], 16 * (n // NSLOT + 1))

        @block.tensor
        def _(pe):
            def norm_transpose(i):
                for b in range(TB):
                    pe.wait_ge(xn_done, TB * i + b + 1)
                    for k in range(KT):
                        at = (k % 2) * T + b * P
                        t = nc.tensor.transpose(bank[k // 2][:, at:at + P], XN[:, b, k * P:(k + 1) * P], ident)
                        if b == TB - 1 and k % 2:
                            t.then_inc(ht_tr, 1)

            def tile_of(slot, m, dst):
                w = RING[:, slot, :].rearrange("p (k n) -> p k n", k=KT)
                for k in range(KT):
                    t = nc.tensor.matmul(dst, w[:, k, m * P:(m + 1) * P], HT[:, k, :], start=k == 0, stop=k == KT - 1)
                return t

            def rows_of(slot, b, dst):
                w = RING[:, slot, :].rearrange("p (k n) -> p k n", k=KT)
                for k in range(KT):
                    t = nc.tensor.matmul(dst, HT[:, k, b * P:(b + 1) * P], w[:, k, :], start=k == 0, stop=k == KT - 1)
                return t

            def mixer(l):
                base = BASE_MIX[l]
                norm_transpose(2 * l)
                pe.wait_ge(ht_v, 4 * (2 * l) + 4)
                pe.wait_ge(ht_a, 4 * (2 * l) + 4)

                arrived(pe, base)
                for m in range(2):
                    t = tile_of(base % NSLOT, m, bank[4][:, m * T:(m + 1) * T])
                t.then_inc(slabs_used, 1)
                arrived(pe, base + 1)
                for b in range(TB):
                    t = rows_of((base + 1) % NSLOT, b, bank[5][:, b * T:(b + 1) * T])
                t.then_inc(slabs_used, 1)
                wf = par(l, "w_f").rearrange("p (k h) -> p k h", k=KT)
                for k in range(KT):
                    t = nc.tensor.matmul(bank[6][0:HEADS, 0:T], wf[:, k, :], HT[:, k, :], start=k == 0, stop=k == KT - 1)
                t.then_inc(f_ps, 1)

                def scan_in(j):
                    if j == 0:
                        pe.wait_ge(ut_done, l + 1)
                        pe.wait_ge(up_done, l + 1)
                    if j >= 2:
                        pe.wait_ge(rot_done, 8 * l + j - 1)
                    r = SCH * (j % 4)
                    for c, name in enumerate(("b_re", "b_im")):
                        w = par(l, name)[r:r + SCH, (j // 4) * P:(j // 4 + 1) * P]
                        t = nc.tensor.matmul(bank[4 + j % 2][:, c * T:(c + 1) * T], w, UT[r:r + SCH, j // 4, :],
                                             start=True, stop=True)
                    t.then_inc(bu_done, 1)

                def scan_out(j):
                    if j == 0:
                        pe.wait_ge(tab_ok, l + 1)
                    pe.wait_ge(zr_done, 8 * l + j + 1)
                    if j == 0:
                        pe.wait_ge(fz_a, 3 * l + 3)
                        pe.wait_ge(fz_v, 4 * l + 1)
                    r = SCH * (j % 4)
                    dst = bank[6][r:r + SCH, (j // 4) * T:(j // 4 + 1) * T]
                    parts = ((0, ZC[:, j % 2, 0:T]), (1, ZS[:, j % 2, T:2 * T]),
                             (2, ZS[:, j % 2, 0:T]), (2, ZC[:, j % 2, T:2 * T]))
                    for n, (c, z) in enumerate(parts):
                        t = nc.tensor.matmul(dst, CC[:, c, j, :], z, start=n == 0, stop=n == 3)
                    t.then_inc(y_done, 1)

                def feature_tile(n):
                    s = base + 2 + n // 2
                    arrived(pe, s)
                    t = tile_of(s % NSLOT, n % 2, bank[n // 2][:, (n % 2) * T:(n % 2 + 1) * T])
                    if n % 2:
                        t.then_inc(slabs_used, 1)

                def value_slab(s):
                    n = base + 6 + s
                    arrived(pe, n)
                    if s == 0:
                        pe.wait_ge(mt_pool, l + 1)
                    for b in range(TB):
                        if s == 0 and b == 1:
                            pe.wait_ge(rot_done, 8 * l + 7)
                        t = rows_of(n % NSLOT, b, bank[7 if b == 0 else 4][:, s * T:(s + 1) * T])
                    t.then_inc(slabs_used, 1)

                def pool_band():
                    for g in range(NG):
                        r = (g % 2) * GC
                        dst = bank[7][r:r + GC, (g // 2) * T:(g // 2 + 1) * T]
                        nc.tensor.matmul(dst, UP[:, 0, g * GC:(g + 1) * GC], band[:, g, 0:2, :],
                                         start=True, stop=False)
                        t = nc.tensor.matmul(dst[:, P:T], UP[:, 1, g * GC:(g + 1) * GC], band[:, g, 2, :],
                                             start=False, stop=True)
                    t.then_inc(dt_ps, 1)

                def pool_mix():
                    pe.wait_ge(dt_done, l + 1)
                    w = par(l, "pool_w").rearrange("p (a n) -> p a n", a=2)
                    for a in range(2):
                        t = nc.tensor.matmul(bank[7][:, a * T:(a + 1) * T], w[:, a, :], DT[:, a, :], start=True, stop=True)
                    t.then_inc(pl_ps, 1)

                scan_in(0)
                scan_in(1)
                feature_tile(0)
                pool_band()
                scan_in(2)
                feature_tile(1)
                scan_in(3)
                pool_mix()
                feature_tile(2)
                scan_in(4)
                feature_tile(3)
                scan_out(0)
                scan_in(5)
                scan_out(1)
                feature_tile(4)
                scan_in(6)
                scan_out(2)
                feature_tile(5)
                scan_in(7)
                scan_out(3)
                feature_tile(6)
                scan_out(4)
                feature_tile(7)
                scan_out(5)
                value_slab(0)
                scan_out(6)
                value_slab(1)
                scan_out(7)

                pe.wait_ge(qkv_done, 6 * l + 6)
                pe.wait_ge(c_rows, 32 * (l + 1))
                if l == 0:
                    pe.wait_ge(aug_ones, 2)
                for b in range(2):
                    for h in range(4):
                        t = nc.tensor.matmul(bank[b][:, h * P:(h + 1) * P], QA[:, 4 * b + h, 0:P], KA[:, 4 * b + h, 0:P],
                                             start=True, stop=True)
                    t.then_inc(sc_ps, 1)
                for n, bk in enumerate((2, 3, 4, 7)):
                    for h in range(2):
                        t = nc.tensor.matmul(bank[bk][:, h * T:(h + 1) * T], QA[:, 2 * n + h, P:T], KA[:, 2 * n + h, :],
                                             start=True, stop=True)
                    t.then_inc(sc_ps, 1)

                pe.wait_ge(gy_done, l + 1)
                w = par(l, "w_glu").rearrange("p (a n) -> p a n", a=2)
                for m in range(2):
                    for k in range(2):
                        t = nc.tensor.matmul(bank[5][:, m * T:(m + 1) * T], w[:, k, m * P:(m + 1) * P], GY[:, k, :],
                                             start=k == 0, stop=k == 1)
                t.then_inc(glu_ps, 1)

                def branch_sum(n, tiles, dst):
                    pe.wait_ge(bsq, 3 * l + n + 1)
                    if n == 1:
                        pe.wait_ge(bvar, 3 * l + 1)
                    for i, k in enumerate(tiles):
                        t = nc.tensor.matmul(dst, ones, SQ[:, k, :], start=i == 0, stop=i == len(tiles) - 1)
                    t.then_inc(bss_ps, 1)

                def head_out(h):
                    pe.wait_ge(pt_done, 8 * l + h + 1)
                    r = (h % 2) * DH
                    dst = bank[2 + h // 4][r:r + DH, (h // 2 % 2) * T:(h // 2 % 2 + 1) * T]
                    nc.tensor.matmul(dst, V[:, 0, h * DH:(h + 1) * DH], PTS[:, h % 2, 0:T], start=True, stop=False)
                    t = nc.tensor.matmul(dst[:, P:T], V[:, 1, h * DH:(h + 1) * DH], PTS[:, h % 2, T:3 * P], start=False,
                                         stop=True)
                    if h % 4 == 3:
                        t.then_inc(ot_ps, 1)

                for h in range(HEADS):
                    pe.wait_ge(pn_done, 6 * l + 3 + h // 2)
                    if h >= 2:
                        pe.wait_ge(pt_done, 8 * l + h - 1)
                    dst = bank[h % 2]
                    nc.tensor.transpose(dst[:, 0:P], P0[:, h, :], ident)
                    nc.tensor.transpose(dst[:, P:2 * P], P1[:, h, 0:P], ident)
                    nc.tensor.transpose(dst[:, 2 * P:3 * P], P1[:, h, P:T], ident).then_inc(pt_ps, 1)
                    if h == 2:
                        branch_sum(0, (4, 5), bank[6][:, 0:T])
                    if h == 5:
                        branch_sum(1, (6, 7), bank[6][:, T:2 * T])
                    if h >= 1:
                        head_out(h - 1)
                head_out(HEADS - 1)

                def project(b, slabs):
                    for s in slabs:
                        n = base + 8 + s
                        arrived(pe, n)
                        w = RING[:, n % NSLOT, :].rearrange("p (k n) -> p k n", k=2)
                        for k in range(2):
                            kt = (4, 6, 0, 2)[s] + k
                            pe.wait_ge(mtn, 8 * l + (0, 2, 4, 6)[s] + k + 1)
                            for c in range(2):
                                t = nc.tensor.matmul(bank[(4, 7, 0, 1)[2 * b + c]][:, :], MT[:, kt, b * P:(b + 1) * P],
                                                     w[:, k, c * 512:(c + 1) * 512], start=s == 0 and k == 0,
                                                     stop=s == 3 and k == 1)
                        if b == 1:
                            t.then_inc(slabs_used, 1)
                    return t

                project(0, (0, 1))
                branch_sum(2, (0, 1, 2, 3), bank[5][:, 0:T])
                project(1, (0, 1))
                project(0, (2, 3)).then_inc(mix_ps, 1)
                project(1, (2, 3))

            def dense():
                norm_transpose(1)
                pe.wait_ge(ht_v, 8)
                pe.wait_ge(ht_a, 8)

                def up(ft):
                    g, u = BASE_DENSE + 3 * (ft // 2), BASE_DENSE + 3 * (ft // 2) + 1
                    arrived(pe, g)
                    arrived(pe, u)
                    if ft >= 4:
                        pe.wait_ge(act_d, ft - 3)
                    for c, n in enumerate((g, u)):
                        t = tile_of(n % NSLOT, ft % 2, bank[ft % 4][:, c * T:(c + 1) * T])
                        if c == 0 and ft % 2:
                            t.then_inc(slabs_used, 1)
                    t.then_inc(up_ps, 1)

                def down(ft):
                    n = BASE_DENSE + 3 * (ft // 2) + 2
                    arrived(pe, n)
                    pe.wait_ge(act_d, ft + 1)
                    w = RING[:, n % NSLOT, :].rearrange("p (k n) -> p k n", k=2)
                    for b in range(TB):
                        for c in range(2):
                            t = nc.tensor.matmul(bank[4 + 2 * b + c][:, :], AT[:, ft % 2, b * P:(b + 1) * P],
                                                 w[:, ft % 2, c * 512:(c + 1) * 512], start=ft == 0,
                                                 stop=ft == FT_DENSE - 1)
                            if ft % 2 == 0 and b == 0 and c == 0:
                                t.then_inc(slabs_used, 1)
                    if ft % 2:
                        t.then_inc(slabs_used, 1)
                    return t

                for ft in range(FT_DENSE):
                    up(ft)
                    if ft:
                        down(ft - 1)
                down(FT_DENSE - 1)

            def routing():
                rt = par(1, "router").rearrange("p (k e) -> p k e", k=KT)
                for b in range(TB):
                    for k in range(KT):
                        t = nc.tensor.matmul(bank[4][:, b * NE:(b + 1) * NE], HT[:, k, b * P:(b + 1) * P], rt[:, k, :],
                                             start=k == 0, stop=k == KT - 1)
                t.then_inc(lg_ps, 1)
                pe.wait_ge(sel_done, 1)
                dst = bank[5]
                nc.tensor.matmul(dst[:, 0:NE], tri, SEL[:, 0, :], start=True, stop=True)
                nc.tensor.matmul(dst[:, NE:2 * NE], ones, SEL[:, 0, :], start=True, stop=False)
                nc.tensor.matmul(dst[:, NE:2 * NE], tri, SEL[:, 1, :], start=False, stop=True)
                nc.tensor.matmul(dst[:, 2 * NE:3 * NE], ones, SEL[:, 0, :], start=True, stop=False)
                nc.tensor.matmul(dst[:, 2 * NE:3 * NE], ones, SEL[:, 1, :], start=False, stop=True).then_inc(pos_ps, 1)

            def gather(i, first=False):
                pe.wait_ge(g_done, i + 1)
                for h in range(2):
                    if not first:
                        pe.wait_ge(act_m, i * FT_MOE + (h - 1))
                    for k in range(4):
                        for b in range(TB):
                            t = nc.tensor.matmul(bank[h][:, k * SLOTS:(k + 1) * SLOTS],
                                                 XN[:, b, (4 * h + k) * P:(4 * h + k + 1) * P], GM[:, b, :],
                                                 start=b == 0, stop=b == TB - 1)
                    t.then_inc(ga_ps, 1)

            def scatter_waits(i):
                pe.wait_ge(y_v, i + 1)
                pe.wait_ge(y_a, i + 1)
                pe.wait_ge(gt_done, i + 1)

            def scatter(start=False):
                for b in range(TB):
                    for c in range(2):
                        t = nc.tensor.matmul(bank[4 + 2 * b + c][:, :], GT[:, b * P:(b + 1) * P],
                                             YE[:, c * 512:(c + 1) * 512], start=start, stop=False, skip_group_check=True)
                return t

            def item(i):
                def slot(m):
                    return (BASE_MOE + m) % NSLOT

                def here(m):
                    pe.wait_ge(slab_in[slot(m)], i * (16 * MOE_SLABS // NSLOT) + 16 * ((BASE_MOE + m) // NSLOT + 1))

                def up(ft):
                    m = 3 * (ft // 2)
                    if ft % 2 == 0:
                        here(m)
                        here(m + 1)
                    if ft >= 2:
                        pe.wait_ge(act_m, i * FT_MOE + (ft - 1))
                    if ft == 3:
                        pe.wait_ge(gt_done, i + 2)
                    if ft == 1:
                        for b in range(TB):
                            nc.tensor.transpose(bank[1][0:SLOTS, T + b * P:T + (b + 1) * P], GW[:, b, :], ident)
                    for c in range(2):
                        w = RING[:, slot(m + c), :].rearrange("p (k n) -> p k n", k=KT)
                        for k in range(KT):
                            t = nc.tensor.matmul(bank[ft % 2][:, c * SLOTS:(c + 1) * SLOTS],
                                                 w[:, k, (ft % 2) * P:(ft % 2 + 1) * P], XG[:, k, :],
                                                 start=k == 0, stop=k == KT - 1)
                        if c == 0 and ft % 2:
                            t.then_inc(slabs_used, 1)
                    t.then_inc(gu_ps, 1)

                def down(ft):
                    m = 3 * (ft // 2) + 2
                    if ft % 2 == 0:
                        here(m)
                    pe.wait_ge(act_m, i * FT_MOE + (ft + 1))
                    w = RING[:, slot(m), :].rearrange("p (k n) -> p k n", k=2)
                    for c in range(2):
                        t = nc.tensor.matmul(bank[2 + c][0:SLOTS, :], AT[:, ft % 2, 0:SLOTS],
                                             w[:, ft % 2, c * 512:(c + 1) * 512], start=ft == 0, stop=ft == FT_MOE - 1)
                        if ft % 2 == 0 and c == 0:
                            t.then_inc(slabs_used, 1)
                    if ft % 2:
                        t.then_inc(slabs_used, 1)

                pe.wait_ge(xg_done, i + 1)
                for ft in range(FT_MOE):
                    up(ft)
                    if ft == 0:
                        scatter_waits(i)
                        scatter()
                    if ft:
                        down(ft - 1)
                gather(i + 1)
                down(FT_MOE - 1)

            def experts():
                norm_transpose(3)
                pe.wait_ge(ht_v, 16)
                pe.wait_ge(ht_a, 16)
                routing()
                pe.wait_ge(route_ok, 1)
                scatter_waits(0)
                scatter(start=True)
                gather(0, first=True)
                with pe.Fori(0, NE) as e:
                    item(e)
                scatter_waits(NE)
                over = pe.value_load(OVER[0:1, 0:1], min_val=0, max_val=T)
                with pe.If(over > SLOTS):
                    for p in range(1, PASSES):
                        with pe.Fori(0, NE) as e:
                            item(e + p * NE)
                    scatter_waits(PASSES * NE)
                scatter().then_inc(acc_all, 1)

            pe.wait_ge(cst_in, 16)
            pe.wait_ge(par_in, 16)
            mixer(0)
            dense()
            mixer(1)
            experts()

        @block.scalar
        def _(act):
            def sumsq(n, b, sources):
                for h, (src, dst) in enumerate(sources):
                    t = nc.scalar.activation(dst, src, ACT.Square, accum_out=STAT[:, 2 * b + h:2 * b + h + 1])
                t.then_inc(sq_done, 1)

            def pre_norm(i):
                for b in range(TB):
                    if i == 0 and b == 0:
                        act.wait_ge(x_in, 16)
                    if i:
                        act.wait_ge(x_done, 4 * (i - 1) + 2 * b + 2)
                        act.wait_ge(rstd_done, 4 * i)
                    sumsq(2 * i, b, [(X[:, b, :], XN[:, b, :])])
                gain = par(i // 2, "g_ffn" if i % 2 else "g_mix")
                for k in (2, 3, 6, 7):
                    act.wait_ge(ht_tr, 4 * i + k // 2 + 1)
                    nc.scalar.activation(HT[:, k, :], bank[k // 2][:, (k % 2) * T:(k % 2 + 1) * T], ACT.Identity,
                                         scale=gain[:, k:k + 1]).then_inc(ht_a, 1)

            def post_norm(i, banks, first, second):
                if i:
                    act.wait_ge(x_done, 4 * i)
                act.dma_start(GB[:, :], g_post[i, :, :]).then_inc(gb_in, 16)
                for b, ready in enumerate((first, second)):
                    act.wait_ge(*ready)
                    act.wait_ge(rstd_done, 2 * (2 * i + 1))
                    sumsq(2 * i + 1, b, [(bank[banks[2 * b + h]][:, :], XN[:, b, h * 512:(h + 1) * 512]) for h in range(2)])

            def scan_tables(l, part):
                if part == 0:
                    if l:
                        act.wait_ge(tab_ok, l)
                    nc.scalar.activation(SV[:, 0, :], par(l, "log_dt"), ACT.Tanh, scale=1.0 / 16.0).then_inc(trig_a, 1)
                    return
                act.wait_ge(trig_v, 2 * l + 1)
                nc.scalar.activation(SV[:, 6, :], SV[:, 5, :], ACT.Tanh, scale=0.5).then_inc(trig_a, 1)
                act.wait_ge(trig_v, 2 * l + 2)
                for h in range(2):
                    nc.scalar.activation(COS[:, 4 * h:4 * h + 4, :], SIN[:, 4 * h:4 * h + 4, :], ACT.Sin, scale=TURN / 2)
                for h in range(2):
                    t = nc.scalar.activation(SIN[:, 4 * h:4 * h + 4, :], SIN[:, 4 * h:4 * h + 4, :], ACT.Sin, scale=TURN)
                t.then_inc(trig_a, 1)

            def heads_out(dst, src, scale):
                for o in range(2):
                    t = nc.scalar.activation(dst[:, :, o, :], src[o * DH:(o + 1) * DH, :].rearrange("p (m t) -> p m t", m=2),
                                             ACT.Copy, scale=scale)
                return t

            def mixer(l):
                base = BASE_MIX[l]
                pre_norm(2 * l)
                act.wait_ge(slabs_used, base + 1)
                nc.scalar.copy(UT[:, :, :], bank[4][:, :].rearrange("p (a t) -> p a t", a=2)).then_inc(ut_done, 1)
                act.wait_ge(slabs_used, base + 2)
                nc.scalar.copy(UP[:, :, :], bank[5][:, :].rearrange("p (a t) -> p a t", a=2)).then_inc(up_done, 1)
                act.wait_ge(f_ps, l + 1)
                nc.scalar.activation(FG[:, 0, :], bank[6][0:HEADS, 0:T], ACT.Abs, bias=par(l, "b_forget")[0:HEADS, :])\
                    .then_inc(fz_a, 1)
                act.wait_ge(fz_a, 3 * l + 1)
                nc.scalar.activation(FG[:, 1, :], FG[:, 0, :], ACT.Exp, scale=-1.0).then_inc(fz_a, 1)
                act.wait_ge(fz_a, 3 * l + 2)
                nc.scalar.activation(FG[:, 2, :], FG[:, 1, :], ACT.Ln, bias=1.0).then_inc(fz_a, 1)
                if l == 0:
                    scan_tables(0, 1)
                act.wait_ge(dt_ps, l + 1)
                nc.scalar.copy(DT[:, :, :], bank[7][:, :].rearrange("p (a t) -> p a t", a=2)).then_inc(dt_done, 1)
                qa = QA[0:DH, :, :].rearrange("p (b m o) t -> p b m o t", b=2, m=2)
                ka = KA[0:DH, :, :].rearrange("p (b m o) t -> p b m o t", b=2, m=2)
                act.wait_ge(slabs_used, base + 3)
                heads_out(qa[:, 0, :, :, :], bank[0], DH ** -0.5).then_inc(qkv_done, 1)
                act.wait_ge(pl_ps, l + 1)
                ps = par(l, "pool_scale")
                for a in range(2):
                    t = nc.scalar.activation(MT[:, 4 + a, :], bank[7][:, a * T:(a + 1) * T], ACT.Identity, scale=ps[:, a:a + 1])
                t.then_inc(mt_pool, 1)
                act.wait_ge(slabs_used, base + 4)
                heads_out(qa[:, 1, :, :, :], bank[1], DH ** -0.5).then_inc(qkv_done, 1)
                act.wait_ge(mt_pool, l + 1)
                act.wait_ge(slabs_used, base + 8)
                nc.scalar.activation(SQ[:, 4:6, :], MT[:, 4:6, :], ACT.Square).then_inc(bsq, 1)
                for n in range(2):
                    act.wait_ge(slabs_used, base + 5 + n)
                    heads_out(ka[:, n, :, :, :], bank[2 + n], 1.0).then_inc(qkv_done, 1)
                for n, bk in enumerate((7, 4)):
                    act.wait_ge(slabs_used, base + 8)
                    nc.scalar.copy(V[:, n, :], bank[bk][:, :]).then_inc(qkv_done, 1)
                act.wait_ge(ys_done, l + 1)
                nc.scalar.activation(GY[:, :, :], YS[:, :, :], ACT.Gelu_apprx_tanh).then_inc(gy_done, 1)
                act.wait_ge(glu_ps, l + 1)
                bg = par(l, "b_glu")
                for m in range(2):
                    t = nc.scalar.activation(SG[:, m, :], bank[5][:, m * T:(m + 1) * T], ACT.Sigmoid, bias=bg[:, m:m + 1])
                t.then_inc(sg_done, 1)
                for n in range(6):
                    act.wait_ge(mx_done, 6 * l + n + 1)
                    heads, width = (4, P) if n < 2 else (2, T)
                    for h in range(heads):
                        at = 4 * n + h if n < 2 else 8 + 2 * (n - 2) + h
                        dst = P0[:, at, :] if n < 2 else P1[:, at - 8, :]
                        src = bank[(0, 1, 2, 3, 4, 7)[n]][:, h * width:(h + 1) * width]
                        t = nc.scalar.activation(dst, src, ACT.Exp, bias=MX[:, at:at + 1], accum_out=SUM[:, at:at + 1])
                    t.then_inc(ex_done, 1)
                act.wait_ge(mt_ssm, l + 1)
                nc.scalar.activation(SQ[:, 6:8, :], MT[:, 6:8, :], ACT.Square).then_inc(bsq, 1)
                def branch_rstd(n):
                    act.wait_ge(bvar, 3 * l + n + 1)
                    nc.scalar.activation(RB[:, n, :], RB[:, n, :], ACT.Sqrt).then_inc(brs, 1)

                for h in range(HEADS):
                    if h in (4, 7):
                        branch_rstd((h - 4) // 3)
                    act.wait_ge(pt_ps, 8 * l + h + 1)
                    nc.scalar.copy(PTS[:, h % 2, :], bank[h % 2][:, 0:3 * P]).then_inc(pt_done, 1)
                for m in range(2):
                    act.wait_ge(ot_done, 2 * l + m + 1)
                    t = nc.scalar.activation(SQ[:, 2 * m:2 * m + 2, :], MT[:, 2 * m:2 * m + 2, :], ACT.Square)
                t.then_inc(bsq, 1)
                branch_rstd(2)
                post_norm(2 * l, (4, 7, 0, 1), (mix_ps, l + 1), (slabs_used, base + 12))

            def dense():
                pre_norm(1)
                for ft in range(FT_DENSE):
                    act.wait_ge(up_ps, ft + 1)
                    nc.scalar.activation(SA[:, ft % 2, :], bank[ft % 4][:, 0:T], ACT.Silu).then_inc(silu_d, 1)
                    if ft == 2:
                        scan_tables(1, 0)
                        scan_tables(1, 1)
                post_norm(1, (4, 5, 6, 7), (slabs_used, BASE_MIX[1]), (slabs_used, BASE_MIX[1]))

            def item(i):
                for ft in range(FT_MOE):
                    act.wait_ge(gu_ps, i * FT_MOE + (ft + 1))
                    nc.scalar.activation(SA[:, ft % 2, 0:SLOTS], bank[ft % 2][:, 0:SLOTS], ACT.Silu).then_inc(silu_m, 1)
                act.wait_ge(slabs_used, i * MOE_SLABS + (BASE_MOE + MOE_SLABS))
                nc.scalar.copy(YE[:, 512:D], bank[3][0:SLOTS, :]).then_inc(y_a, 1)

            def experts():
                pre_norm(3)
                act.wait_ge(gate_d, 1)
                nc.scalar.activation(GATE[:, :, 1:2], GATE[:, :, 0:1], ACT.Exp).then_inc(gate_e, 1)
                act.wait_ge(route_ok, 1)
                act.wait_ge(y_a, 1)
                over = act.value_load(OVER[0:1, 0:1], min_val=0, max_val=T)
                with act.Fori(0, NE) as e:
                    item(e)
                with act.If(over > SLOTS):
                    for p in range(1, PASSES):
                        with act.Fori(0, NE) as e:
                            item(e + p * NE)
                post_norm(3, (4, 5, 6, 7), (acc_all, 1), (acc_all, 1))

            act.wait_ge(par_in, 16)
            scan_tables(0, 0)
            mixer(0)
            dense()
            mixer(1)
            experts()

        @block.gpsimd
        def _(pool):
            steps = [0]

            def rstd(n, post):
                for b in range(TB):
                    pool.wait_ge(sq_done, 2 * n + b + 1)
                    v = STAT[:, 2 * b:2 * b + 1]
                    if post:
                        nc.gpsimd.tensor_tensor(STAT[:, 4 + b:5 + b], v, STAT[:, 2 * b + 1:2 * b + 2], ALU.add)\
                            .then_inc(var_done, 1)
                        steps[0] += 1
                        pool.wait_ge(var_done, steps[0])
                        v = STAT[:, 4 + b:5 + b]
                    nc.gpsimd.tensor_scalar(STAT[:, 6 + b:7 + b], v, 1.0 / D, EPS, ALU.mult, ALU.add).then_inc(var_done, 1)
                    steps[0] += 1
                    pool.wait_ge(var_done, steps[0])
                    if n:
                        pool.wait_ge(xn_done if post else x_done, (n + 1) if post else 2 * n)
                    nc.gpsimd.tensor_tensor(RSTD[:, b:b + 1], STAT[:, 6 + b:7 + b], EXPO[:, 0:1], ALU.pow).then_inc(rstd_done, 1)

            def mixer(l):
                rstd(4 * l, False)
                for j in range(SJ):
                    pool.wait_ge(z_done, 8 * l + j + 1)
                    if j >= 2:
                        pool.wait_ge(y_done, 8 * l + j - 1)
                    z = Z[:, j % 2, :].rearrange("p (c t) -> p c t", c=2)
                    for dst, tab in ((ZC, COS), (ZS, SIN)):
                        t = nc.gpsimd.tensor_tensor(dst[:, j % 2, :].rearrange("p (c t) -> p c t", c=2), z,
                                                    tab[:, j, :].unsqueeze(1).to_broadcast([P, 2, T]), ALU.mult)
                    t.then_inc(zr_done, 1)
                    if j == 2:
                        pool.wait_ge(fz_v, 4 * l + 4)
                        pool.dma_start(c_dram[l, :, :, :], FG[:, 4:6, :]).then_inc(c_out, 16)
                    if j == 4:
                        pool.wait_ge(c_out, 16 * (l + 1))
                        for n, dst in enumerate((QA[DH:DH + 1, :, :], KA[DH + 1:DH + 2, :, :])):
                            pool.dma_start(dst, c_dram[l, :, n, :].unsqueeze(0)).then_inc(c_rows, 16)
                rstd(4 * l + 1, True)

            for n, m in enumerate((QA, KA)):
                if n:
                    pool.wait_ge(aug_ones, n)
                nc.gpsimd.memset(m[DH:DH + 2, :, :], 1.0).then_inc(aug_ones, 1)
            pool.wait_ge(aug_ones, 2)
            nc.gpsimd.memset(EXPO[:, :], -0.5).then_inc(aug_ones, 1)
            pool.wait_ge(aug_ones, 3)
            mixer(0)
            rstd(2, False)
            rstd(3, True)
            mixer(1)
            rstd(6, False)
            rstd(7, True)

        @block.vector
        def _(dve):
            links = [0]

            def link(t):
                t.then_inc(chain, 1)
                links[0] += 1
                dve.wait_ge(chain, links[0])

            TT, TS, STT = nc.vector.tensor_tensor, nc.vector.tensor_scalar, nc.vector.scalar_tensor_tensor

            def pre_norm(i):
                for b in range(TB):
                    dve.wait_ge(rstd_done, 4 * i + b + 1)
                    if i:
                        dve.wait_ge(ht_tr, 4 * i)
                    TS(XN[:, b, :], X[:, b, :], RSTD[:, b:b + 1], None, ALU.mult).then_inc(xn_done, 1)
                gain = par(i // 2, "g_ffn" if i % 2 else "g_mix")
                for k in (0, 1, 4, 5):
                    dve.wait_ge(ht_tr, 4 * i + k // 2 + 1)
                    TS(HT[:, k, :], bank[k // 2][:, (k % 2) * T:(k % 2 + 1) * T], gain[:, k:k + 1], None, ALU.mult)\
                        .then_inc(ht_v, 1)

            def post_norm(i, banks):
                dve.wait_ge(gb_in, 16 * (i + 1))
                for b in range(TB):
                    dve.wait_ge(rstd_done, 4 * i + 2 + b + 1)
                    for h in range(2):
                        if b:
                            dve.wait_ge(x_done, 4 * i + h + 1)
                        STT(TMP[:, h * 512:(h + 1) * 512], bank[banks[2 * b + h]][:, :], RSTD[:, b:b + 1],
                            GB[:, h * 512:(h + 1) * 512], ALU.mult, ALU.mult).then_inc(post_tmp, 1)
                    for h in range(2):
                        dve.wait_ge(post_tmp, 4 * i + 2 * b + h + 1)
                        TT(X[:, b, h * 512:(h + 1) * 512], X[:, b, h * 512:(h + 1) * 512],
                           TMP[:, h * 512:(h + 1) * 512], ALU.add).then_inc(x_done, 1)

            def s(n):
                return SV[:, n, :]

            def scan_steps(l):
                a_re = par(l, "a_re")
                dve.wait_ge(trig_a, 3 * l + 1)
                if l:
                    dve.wait_ge(y_done, 8 * l)
                link(TS(s(1), s(0), 1.0, None, ALU.add))
                link(TS(s(2), s(0), -1.0, 1.0, ALU.mult, ALU.add))
                link(nc.vector.reciprocal(s(2), s(2)))
                link(TT(s(3), s(1), s(2), ALU.mult))
                for _ in range(3):
                    link(TT(s(3), s(3), s(3), ALU.mult))
                TT(s(5), a_re, s(3), ALU.mult).then_inc(trig_v, 1)

            def scan_tables(l):
                a_re, a_im = par(l, "a_re"), par(l, "a_im")
                link(TT(s(9), a_im, s(3), ALU.mult))
                link(TS(s(10), s(9), 1.0 / (2.0 * math.pi), None, ALU.mult))
                link(TS(s(11), s(10), ROUND, None, ALU.add))
                link(TS(s(11), s(11), -ROUND, None, ALU.add))
                link(TT(s(10), s(10), s(11), ALU.subtract))
                for j in range(SJ):
                    t = TS(COS[:, j, :], iota, s(10)[:, j:j + 1], ROUND, ALU.mult, ALU.add)
                link(t)
                link(TS(COS, COS, -ROUND, None, ALU.add))
                for j in range(SJ):
                    t = STT(SIN[:, j, :], iota, s(10)[:, j:j + 1], COS[:, j, :], ALU.mult, ALU.subtract)
                t.then_inc(trig_v, 1)
                dve.wait_ge(trig_a, 3 * l + 2)
                link(TS(s(7), s(6), -1.0, 1.0, ALU.mult, ALU.add))
                link(nc.vector.reciprocal(s(7), s(7)))
                link(STT(s(7), s(7), 2.0, s(6), ALU.mult, ALU.mult))
                link(TS(s(8), s(7), 1.0, None, ALU.add))
                dve.wait_ge(trig_a, 3 * l + 3)
                for h in range(2):
                    c = COS[:, 4 * h:4 * h + 4, :]
                    link(TT(c, c, c, ALU.mult))
                sin1 = SIN[:, :, 1]
                link(TS(s(12), COS[:, :, 1], -2.0, None, ALU.mult))
                link(TS(s(13), s(12), 1.0, None, ALU.add))
                link(TT(s(13), s(13), s(7), ALU.mult))
                link(TT(s(13), s(13), s(12), ALU.add))
                link(TT(s(14), s(8), sin1, ALU.mult))
                link(TT(s(15), a_re, a_re, ALU.mult))
                link(TT(s(16), a_im, a_im, ALU.mult))
                link(TT(s(15), s(15), s(16), ALU.add))
                link(nc.vector.reciprocal(s(15), s(15)))
                link(TT(s(16), s(13), a_re, ALU.mult))
                link(TT(s(17), s(14), a_im, ALU.mult))
                link(TT(s(16), s(16), s(17), ALU.add))
                link(TT(s(16), s(16), s(15), ALU.mult))
                link(TT(s(17), s(14), a_re, ALU.mult))
                link(TT(s(18), s(13), a_im, ALU.mult))
                link(TT(s(17), s(17), s(18), ALU.subtract))
                link(TT(s(17), s(17), s(15), ALU.mult))
                for h in range(2):
                    c = COS[:, 4 * h:4 * h + 4, :]
                    link(TS(c, c, -2.0, 1.0, ALU.mult, ALU.add))
                cr = par(l, "c_re").rearrange("p (j c) -> p j c", j=SJ)
                ci = par(l, "c_im").rearrange("p (j c) -> p j c", j=SJ)
                re = s(16).unsqueeze(2).to_broadcast([P, SJ, SCH])
                im = s(17).unsqueeze(2).to_broadcast([P, SJ, SCH])
                link(TT(CT[:, 0, :, :], cr, re, ALU.mult))
                link(TT(CT[:, 1, :, :], ci, im, ALU.mult))
                link(TT(CC[:, 0, :, :], CT[:, 0, :, :], CT[:, 1, :, :], ALU.subtract))
                link(TT(CT[:, 0, :, :], cr, im, ALU.mult))
                link(TT(CT[:, 1, :, :], ci, re, ALU.mult))
                link(TT(CT[:, 0, :, :], CT[:, 0, :, :], CT[:, 1, :, :], ALU.add))
                link(TS(CC[:, 2, :, :], CT[:, 0, :, :], -1.0, None, ALU.mult))
                TS(CC[:, 1, :, :], CC[:, 0, :, :], -1.0, None, ALU.mult).then_inc(tab_ok, 1)

            def scan_tile(l, j):
                dve.wait_ge(bu_done, 8 * l + j + 1)
                bu = bank[4 + j % 2][:, :].rearrange("p (c t) -> p c t", c=2)
                for n, tab in enumerate((COS, SIN)):
                    t = TT(ROT[:, n, :].rearrange("p (c t) -> p c t", c=2), bu,
                           tab[:, j, :].unsqueeze(1).to_broadcast([P, 2, T]), ALU.mult)
                t.then_inc(rot_done, 1)
                dve.wait_ge(rot_done, 8 * l + j + 1)
                TT(ZIN[:, 0:T], ROT[:, 0, 0:T], ROT[:, 1, T:2 * T], ALU.add)
                TT(ZIN[:, T:2 * T], ROT[:, 0, T:2 * T], ROT[:, 1, 0:T], ALU.subtract).then_inc(zin_done, 1)
                dve.wait_ge(zin_done, 8 * l + j + 1)
                if j >= 2:
                    dve.wait_ge(zr_done, 8 * l + j - 1)
                r = SV[:, 8, j:j + 1].to_broadcast([P, T])
                for c in range(2):
                    t = nc.vector.tensor_tensor_scan(Z[:, j % 2, c * T:(c + 1) * T], r, ZIN[:, c * T:(c + 1) * T], 0.0,
                                                     ALU.mult, ALU.add)
                t.then_inc(z_done, 1)

            def branch_norm(l, n, src, width):
                dve.wait_ge(bss_ps, 3 * l + n + 1)
                link(TS(RB[:, n, :], src, 1.0 / width, EPS, ALU.mult, ALU.add))
                nc.vector.reciprocal(RB[:, n, :], RB[:, n, :]).then_inc(bvar, 1)

            def branch_scale(l, n, tiles):
                dve.wait_ge(brs, 3 * l + n + 1)
                dve.wait_ge(bsq, 3 * l + n + 1)
                g = par(l, "g_br")
                for k in tiles:
                    STT(MT[:, k, :], MT[:, k, :], g[:, k:k + 1], RB[:, n, :], ALU.mult, ALU.mult).then_inc(mtn, 1)

            def softmax_max(l, n):
                dve.wait_ge(sc_ps, 6 * l + n + 1)
                bk = bank[(0, 1, 2, 3, 4, 7)[n]]
                heads, width = (4, P) if n < 2 else (2, T)
                at = 4 * n if n < 2 else 8 + 2 * (n - 2)
                sc = bk[:, :].rearrange("p (h k) -> p h k", h=heads)
                diag = sc[:, :, width - P:width]
                TT(diag, diag, mask.unsqueeze(1).to_broadcast([P, heads, P]), ALU.add).then_inc(msk_done, 1)
                dve.wait_ge(msk_done, 6 * l + n + 1)
                nc.vector.tensor_reduce(MX[:, at:at + heads], sc, AX, ALU.max, negate=True).then_inc(mx_done, 1)

            def softmax_scale(l, n):
                dve.wait_ge(ex_done, 6 * l + n + 1)
                heads, width = (4, P) if n < 2 else (2, T)
                at = 4 * n if n < 2 else 8 + 2 * (n - 2)
                nc.vector.reciprocal(RS[:, at:at + heads], SUM[:, at:at + heads]).then_inc(rs_done, 1)
                dve.wait_ge(rs_done, 6 * l + n + 1)
                p = P0[:, at:at + heads, :] if n < 2 else P1[:, at - 8:at - 8 + heads, :]
                TT(p, p, RS[:, at:at + heads].unsqueeze(2).to_broadcast([P, heads, width]), ALU.mult).then_inc(pn_done, 1)

            def mixer(l):
                pre_norm(2 * l)
                if l == 0:
                    scan_tables(0)
                scan_tile(l, 0)
                dve.wait_ge(fz_a, 3 * l + 1)
                TS(FG[:, 3, :], bank[6][0:HEADS, 0:T], par(l, "b_forget")[0:HEADS, :], 0.0, ALU.add, ALU.min)\
                    .then_inc(fz_v, 1)
                scan_tile(l, 1)
                dve.wait_ge(fz_a, 3 * l + 3)
                dve.wait_ge(fz_v, 4 * l + 1)
                TT(FG[:, 3, :], FG[:, 3, :], FG[:, 2, :], ALU.subtract).then_inc(fz_v, 1)
                dve.wait_ge(fz_v, 4 * l + 2)
                nc.vector.tensor_tensor_scan(FG[:, 4, :], ones[0:HEADS, 0:1].to_broadcast([HEADS, T]), FG[:, 3, :], 0.0,
                                             ALU.mult, ALU.add).then_inc(fz_v, 1)
                dve.wait_ge(fz_v, 4 * l + 3)
                TS(FG[:, 5, :], FG[:, 4, :], -1.0, None, ALU.mult).then_inc(fz_v, 1)
                for j in range(2, SJ):
                    scan_tile(l, j)
                dve.wait_ge(y_done, 8 * (l + 1))
                d = par(l, "ssm_d")
                for a in range(2):
                    t = STT(YS[:, a, :], UT[:, a, :], d[:, a:a + 1], bank[6][:, a * T:(a + 1) * T], ALU.mult, ALU.add)
                t.then_inc(ys_done, 1)
                for n in range(6):
                    softmax_max(l, n)
                dve.wait_ge(sg_done, l + 1)
                TT(MT[:, 6:8, :], GY[:, :, :], SG[:, :, :], ALU.mult).then_inc(mt_ssm, 1)
                for n in range(6):
                    softmax_scale(l, n)
                branch_norm(l, 0, bank[6][:, 0:T], NG * GC)
                branch_scale(l, 0, (4, 5))
                for m in range(2):
                    if m == 1:
                        branch_norm(l, 1, bank[6][:, T:2 * T], SJ * SCH)
                        branch_scale(l, 1, (6, 7))
                    dve.wait_ge(ot_ps, 2 * l + m + 1)
                    nc.vector.tensor_copy(MT[:, 2 * m:2 * m + 2, :], bank[2 + m][:, :].rearrange("p (a t) -> p a t", a=2))\
                        .then_inc(ot_done, 1)
                branch_norm(l, 2, bank[5][:, 0:T], HEADS * DH)
                branch_scale(l, 2, (0, 1, 2, 3))
                post_norm(2 * l, (4, 7, 0, 1))

            def dense():
                pre_norm(1)
                for ft in range(FT_DENSE):
                    dve.wait_ge(silu_d, ft + 1)
                    TT(AT[:, ft % 2, :], SA[:, ft % 2, :], bank[ft % 4][:, T:2 * T], ALU.mult).then_inc(act_d, 1)
                    if ft == 2:
                        scan_steps(1)
                        scan_tables(1)
                post_norm(1, (4, 5, 6, 7))

            def routing():
                dve.wait_ge(lg_ps, 1)
                link(nc.vector.tensor_copy(LG[:, :, :], bank[4][:, 0:TB * NE].rearrange("p (b e) -> p b e", b=TB)))
                for b in range(TB):
                    link(nc.vector.max(M8[:, b, :], LG[:, b, :]))
                    link(nc.vector.max_index(I8[:, b, :], M8[:, b, :], LG[:, b, :]))
                TT(GATE[:, :, 0:1], M8[:, :, 1:2], M8[:, :, 0:1], ALU.subtract).then_inc(gate_d, 1)
                link(nc.vector.tensor_copy(IF8[:, :, :], I8[:, :, :]))
                for c in range(2):
                    for b in range(TB):
                        link(TS(OH[:, c, b, :], iota[:, 0:NE], IF8[:, b, c:c + 1], None, ALU.is_equal))
                TT(SEL[:, :, :], OH[:, 0, :, :], OH[:, 1, :, :], ALU.add).then_inc(sel_done, 1)
                dve.wait_ge(gate_e, 1)
                link(TS(GATE[:, :, 2:3], GATE[:, :, 1:2], 1.0, None, ALU.add))
                link(nc.vector.reciprocal(GATE[:, :, 2:3], GATE[:, :, 2:3]))
                link(TT(GATE[:, :, 3:4], GATE[:, :, 1:2], GATE[:, :, 2:3], ALU.mult))
                for b in range(TB):
                    link(TS(CMB[:, b, 0:NE], OH[:, 0, b, :], GATE[:, b, 2:3], None, ALU.mult))
                    link(STT(CMB[:, b, 0:NE], OH[:, 1, b, :], GATE[:, b, 3:4], CMB[:, b, 0:NE], ALU.mult, ALU.add))
                dve.wait_ge(pos_ps, 1)
                dve.wait_ge(sel_done, 1)
                link(STT(POS[:, :, 0:NE], bank[5][:, 0:TB * NE].rearrange("p (b e) -> p b e", b=TB), 1.0, SEL[:, :, :],
                         ALU.add, ALU.mult))
                link(TS(POS[:, :, 0:NE], POS[:, :, 0:NE], -1.0, None, ALU.add))
                for p in range(1, PASSES + 1):
                    TS(POS[:, :, p * NE:(p + 1) * NE], POS[:, :, 0:NE], -float(p * SLOTS), None, ALU.add)
                    nc.vector.tensor_copy(CMB[:, :, p * NE:(p + 1) * NE], CMB[:, :, 0:NE])
                link(nc.vector.tensor_reduce(CNT[:, 0:1], bank[5][:, 2 * NE:3 * NE], AX, ALU.max))
                nc.vector.tensor_copy(OVER[:, :], CNT[:, 0:1]).then_inc(route_ok, 1)

            def one_hot(i):
                for b in range(TB):
                    pos = POS[:, b, bass.ds(i, 1)]
                    TS(GM[:, b, :], iota[:, 0:SLOTS], pos, None, ALU.is_equal)
                    t = TS(GW[:, b, :], iota[:, 0:SLOTS], pos, CMB[:, b, bass.ds(i, 1)], ALU.is_equal, ALU.mult)
                t.then_inc(g_done, 1)

            def gathered(i):
                gain = par(1, "g_ffn")
                for h in range(2):
                    dve.wait_ge(ga_ps, i * 2 + (h + 1))
                    t = TT(XG[:, 4 * h:4 * h + 4, :], bank[h][:, 0:4 * SLOTS].rearrange("p (k s) -> p k s", k=4),
                           gain[:, 4 * h:4 * h + 4].unsqueeze(2).to_broadcast([P, 4, SLOTS]), ALU.mult)
                t.then_inc(xg_done, 1)

            def item(i):
                for ft in range(FT_MOE):
                    dve.wait_ge(silu_m, i * FT_MOE + (ft + 1))
                    TT(AT[:, ft % 2, 0:SLOTS], SA[:, ft % 2, 0:SLOTS], bank[ft % 2][:, SLOTS:2 * SLOTS], ALU.mult)\
                        .then_inc(act_m, 1)
                    if ft == 1:
                        nc.vector.tensor_copy(GT[:, :], bank[1][0:SLOTS, T:2 * T]).then_inc(gt_done, 1)
                    if ft == 2:
                        one_hot(i + 1)
                gathered(i + 1)
                dve.wait_ge(slabs_used, i * MOE_SLABS + (BASE_MOE + MOE_SLABS))
                nc.vector.tensor_copy(YE[:, 0:512], bank[2][0:SLOTS, :]).then_inc(y_v, 1)

            def experts():
                pre_norm(3)
                routing()
                dve.wait_ge(route_ok, 1)
                nc.vector.memset(GT[:, :], 0.0).then_inc(gt_done, 1)
                nc.vector.memset(YE[:, 0:512], 0.0).then_inc(y_v, 1)
                nc.vector.memset(YE[:, 512:D], 0.0).then_inc(y_a, 1)
                over = dve.value_load(OVER[0:1, 0:1], min_val=0, max_val=T)
                one_hot(0)
                gathered(0)
                with dve.Fori(0, NE) as e:
                    item(e)
                with dve.If(over > SLOTS):
                    for p in range(1, PASSES):
                        with dve.Fori(0, NE) as e:
                            item(e + p * NE)
                post_norm(3, (4, 5, 6, 7))

            dve.wait_ge(par_in, 16)
            dve.wait_ge(cst_in, 16)
            scan_steps(0)
            dve.wait_ge(x_in, 16)
            mixer(0)
            dense()
            mixer(1)
            experts()


def shape_constants():
    c = np.zeros((P, NCONST), np.float32)
    c[:, C_ID:C_ID + P] = np.eye(P)
    c[:, C_MASK:C_MASK + P] = np.triu(np.full((P, P), NEG), 1)
    c[:, C_TRI:C_TRI + P] = np.triu(np.ones((P, P)), 1)
    c[:, C_ONES:C_ONES + P] = 1.0
    c[:, C_IOTA:C_IOTA + T] = np.arange(T)
    t = np.arange(T)
    for g, w in enumerate(WINDOWS):
        inside = (t[None, :] >= t[:, None]) & (t[None, :] - t[:, None] < w)
        a = inside / np.minimum(t + 1.0, w)[None, :] - np.eye(T)
        for n, (s, u) in enumerate(((0, 0), (0, 1), (1, 1))):
            at = C_BAND + (3 * g + n) * P
            c[:, at:at + P] = a[s * P:(s + 1) * P, u * P:(u + 1) * P]
    return c


def pack_params(a):
    out = np.zeros((P, LAYERS, NPAR), np.float32)
    for l in range(LAYERS):
        def put(name, v):
            lo, hi = _off[name]
            out[:v.shape[0], l, lo:hi] = v

        def columns(v):
            return v.reshape(-1, P).T

        put("g_mix", columns(a["norm_mix_pre"][l]))
        put("g_ffn", columns(a["norm_ffn_pre"][l]))
        put("g_br", columns(np.concatenate([a["branch_norm_attn"][l], a["branch_norm_pool"][l], a["branch_norm_ssm"][l]])))
        put("pool_scale", columns(a["pool_scale"][l]))
        put("ssm_d", columns(a["ssm_d"][l].reshape(-1)))
        put("b_glu", columns(a["ssm_b_glu"][l]))
        put("b_forget", a["b_forget"][l].reshape(HEADS, 1))
        put("a_re", columns(a["ssm_a_re"][l].reshape(-1)))
        put("a_im", columns(a["ssm_a_im"][l].reshape(-1)))
        put("log_dt", columns(np.repeat(a["ssm_log_dt"][l], 64)))
        put("w_f", a["w_in"][l][:, F_OFF:P_OFF].reshape(KT, P, HEADS).transpose(1, 0, 2).reshape(P, -1))
        put("router", a["moe_router"][l // 2].reshape(KT, P, NE).transpose(1, 0, 2).reshape(P, -1))
        for name, key in (("b_re", "ssm_b_re"), ("b_im", "ssm_b_im")):
            m = np.zeros((P, 2, P), np.float32)
            for g in range(16):
                j, o = g // 2, g % 2
                r = SCH * (j % 4) + 16 * o
                m[r:r + 16, j // 4, 64 * o:64 * o + 64] = a[key][l, g].T
            put(name, m.reshape(P, -1))
        for name, key in (("c_re", "ssm_c_re"), ("c_im", "ssm_c_im")):
            m = np.zeros((P, SJ, SCH), np.float32)
            for g in range(16):
                j, o = g // 2, g % 2
                m[64 * o:64 * o + 64, j, 16 * o:16 * o + 16] = a[key][l, g].T
            put(name, m.reshape(P, -1))
        m = np.zeros((P, 2, P), np.float32)
        for g in range(NG):
            o = GC * (g % 2)
            m[o:o + GC, g // 2, o:o + GC] = a["pool_w"][l, g]
        put("pool_w", m.reshape(P, -1))
        put("w_glu", a["ssm_w_glu"][l].reshape(2, P, T).transpose(1, 0, 2).reshape(P, -1))
    return out


def kernel(**inputs):
    from concourse import bacc
    from concourse.bass_utils import run_bass_kernel_spmd

    a = {k: np.asarray(v) for k, v in inputs.items()}
    post = np.stack([a["norm_mix_post"][0], a["norm_ffn_post"][0], a["norm_mix_post"][1], a["norm_ffn_post"][1]])
    arrays = {
        "x": a["x"][0], "w_in": a["w_in"], "w_out": a["w_out"],
        "ffn_gate": a["ffn_w_gate"][0], "ffn_up": a["ffn_w_up"][0], "ffn_down": a["ffn_w_down"][0],
        "moe_gate": a["moe_w_gate"][0], "moe_up": a["moe_w_up"][0], "moe_down": a["moe_w_down"][0],
        "g_post": np.broadcast_to(post[:, None, :], (4, P, D)),
        "params": pack_params(a), "consts": shape_constants(),
    }
    arrays = {k: np.ascontiguousarray(v) for k, v in arrays.items()}
    nc = bacc.Bacc("TRN2", target_bir_lowering=False, num_devices=1)
    args = [nc.dram_tensor(k, v.shape, F32, kind="ExternalInput").ap() for k, v in arrays.items()]
    args.append(nc.dram_tensor("c_scratch", (LAYERS, HEADS, 2, T), F32, kind="Internal").ap())
    out = nc.dram_tensor("out", (T, D), F32, kind="ExternalOutput").ap()
    build(nc, *args, out)
    r = run_bass_kernel_spmd(nc, [arrays], core_ids=[0])
    return r.results[0]["out"].reshape(1, T, D)
```

```python
import math
from contextlib import ExitStack

import numpy as np

import concourse.bass as bass
from concourse import mybir

P = 128
T = 256
TB = T // P
D = 1024
KT = D // P
LAYERS = 2
HEADS, DH = 8, 64
WINDOWS = (2, 4, 8, 16)
NG, GC = 4, 64
SJ = 8
SCH = 32
F_OFF, P_OFF, S_OFF = 1536, 1544, 1800
FFN = 2816
FT_DENSE = FFN // P
NE = 8
EDIM = 3584
FT_MOE = EDIM // P
SLOTS = 128
CAP = SLOTS
PASSES = -(-T // CAP)
EPS = 1e-6
NEG = -1e30
ROUND = 1.5 * 2.0 ** 23
TURN = 6.283185

SLAB = 2048
NSLOT = 7
W_COLS = 256
MIX_SLABS = 8 + 4
DENSE_SLABS = 3 * (FT_DENSE // 2)
UNITS = FT_MOE // 2
MOE_SLABS = 3 * UNITS
NSPLIT = 3
BASE_MIX = (0, MIX_SLABS + DENSE_SLABS)
BASE_DENSE = MIX_SLABS
BASE_MOE = BASE_MIX[1] + MIX_SLABS
assert MOE_SLABS % NSLOT == 0 and MOE_SLABS % NSPLIT == 0


def moe_order():
    seq = [("a", 0), ("b", 0)]
    for u in range(1, UNITS):
        seq += [("a", u), ("b", u), ("d", u - 1)]
    return seq + [("d", UNITS - 1)]


MOE_ORDER = moe_order()
AT_SLAB = {key: m for m, key in enumerate(MOE_ORDER)}


_off = {}
_n = 0
for _name, _w in (("g_mix", KT), ("g_ffn", KT), ("g_br", KT), ("pool_scale", 2), ("ssm_d", 2),
                  ("b_glu", 2), ("b_forget", 1), ("a_re", SJ), ("a_im", SJ), ("log_dt", SJ),
                  ("w_f", KT * HEADS), ("router", KT * NE), ("b_re", 2 * P), ("b_im", 2 * P),
                  ("c_re", SJ * SCH), ("c_im", SJ * SCH), ("pool_w", 2 * P), ("w_glu", 2 * T)):
    _off[_name] = (_n, _n + _w)
    _n += _w
NPAR = _n
NVEC = _off["log_dt"][1]
C_ID, C_IOTA, C_MASK = 0, P, P + T
C_TRI, C_ONES, C_SLOT = C_MASK + P, C_MASK + 2 * P, C_MASK + 3 * P
C_BAND = C_SLOT + SLOTS
NCONST = C_BAND + NG * 3 * P

F32 = mybir.dt.float32
F32R = mybir.dt.float32r
I32 = mybir.dt.int32
U32 = mybir.dt.uint32
ALU = mybir.AluOpType
ACT = mybir.ActivationFunctionType
AX = mybir.AxisListType.X


def build(nc, x, w_in, w_out, ffn_gate, ffn_up, ffn_down, moe_gate, moe_up, moe_down, g_post, params, consts, c_dram, out):
    ctx = ExitStack()
    with ctx:
        def sb(name, shape, dt=F32):
            return ctx.enter_context(nc.sbuf_tensor(name, shape, dt))

        def sem(name):
            return ctx.enter_context(nc.semaphore(name))

        RING = sb("RING", [P, NSLOT, SLAB])
        X = sb("X", [P, TB, D])
        XN = sb("XN", [P, TB, D])
        HT = sb("HT", [P, KT, T])
        SQ = HT
        PAR = sb("PAR", [P, LAYERS, NPAR])
        CST = sb("CST", [P, NCONST])
        GB = sb("GB", [P, D])
        TMP = sb("TMP", [P, D])
        STAT = sb("STAT", [P, 8])
        RSTD = sb("RSTD", [P, 4])
        EXPO = sb("EXPO", [P, 4])
        LG = sb("LG", [P, TB, NE])
        M8 = sb("M8", [P, TB, 8])
        I8 = sb("I8", [P, TB, 8], U32)
        IF8 = sb("IF8", [P, TB, 8])
        OH = sb("OH", [P, 2, TB, NE])
        SEL = sb("SEL", [P, TB, NE])
        GATE = sb("GATE", [P, TB, 4])
        NI = (PASSES + 1) * NE
        POS = sb("POS", [P, TB, NI])
        CMB = sb("CMB", [P, TB, NI])
        CNT = sb("CNT", [P, 4])
        OVER = sb("OVER", [P, 1], I32)

        mix = ExitStack()

        def mb(name, shape, dt=F32):
            return mix.enter_context(nc.sbuf_tensor(name, shape, dt))

        QA = mb("QA", [DH + 2, HEADS, T])
        KA = mb("KA", [DH + 2, HEADS, T])
        V = mb("V", [P, TB, HEADS * DH])
        MT = mb("MT", [P, KT, T])
        SCR = mb("SCR", [P, 9, 2 * T])
        ROT = SCR[:, 0:2, :]
        ZIN = SCR[:, 2, :]
        Z = SCR[:, 3:5, :]
        ZC = SCR[:, 5:7, :]
        ZS = SCR[:, 7:9, :]
        P0 = SCR[:, 0:2, :].rearrange("p a (h k) -> p (a h) k", k=P)
        P1 = SCR[:, 2:6, :].rearrange("p a (h k) -> p (a h) k", k=T)
        TRIG = mb("TRIG", [P, 2, SJ, T])
        COS = TRIG[:, 0, :, :]
        SIN = TRIG[:, 1, :, :]
        UT = mb("UT", [P, 2, T])
        UP = mb("UP", [P, TB, T])
        DT = mb("DT", [P, 2, T])
        GY = mb("GY", [P, 2, T])
        SG = mb("SG", [P, 2, T])
        YS = mb("YS", [P, 2, T])
        PTS = mb("PTS", [P, 2, 3 * P])
        RB = mb("RB", [P, 3, T])
        CC = mb("CC", [P, 3, SJ, SCH])
        CT = mb("CT", [P, 2, SJ, SCH])
        SV = mb("SV", [P, 24, SJ])
        FG = mb("FG", [HEADS, 6, T])
        MX = mb("MX", [P, 16])
        SUM = mb("SUM", [P, 16])
        RS = mb("RS", [P, 16])
        AT = DT
        SA = GY
        mix.close()

        WH = sb("WH", [P, NSPLIT, SLAB], F32R)
        WL = sb("WL", [P, NSPLIT, SLAB], F32R)
        XGH = sb("XGH", [P, KT, SLOTS], F32R)
        XGL = sb("XGL", [P, KT, SLOTS], F32R)
        ATH = sb("ATH", [P, 2, SLOTS], F32R)
        ATL = sb("ATL", [P, 2, SLOTS], F32R)
        SM = sb("SM", [SLOTS, W_COLS])
        HM = sb("HM", [SLOTS, W_COLS])
        GM = sb("GM", [P, TB, SLOTS])
        GW = sb("GW", [P, TB, SLOTS])
        GT = sb("GT", [SLOTS, T])
        YE = sb("YE", [SLOTS, D])

        bank = [ctx.enter_context(nc.psum_tensor(f"bank{i}", [P, 512], F32)) for i in range(8)]
        ident = CST[:, C_ID:C_ID + P]
        mask = CST[:, C_MASK:C_MASK + P]
        tri = CST[:, C_TRI:C_TRI + P]
        ones = CST[:, C_ONES:C_ONES + P]
        iota = CST[:, C_IOTA:C_IOTA + T]
        slots = CST[:, C_SLOT:C_SLOT + SLOTS]
        band = CST[:, C_BAND:NCONST].rearrange("p (g b t) -> p g b t", g=NG, b=3)

        SCORE_BANK = (0, 1, 2, 3, 0, 1)
        PT_BANK = (7, 4)
        MIX_BANKS = (0, 1, 4, 7)

        def par(l, name):
            a, b = _off[name]
            return PAR[:, l, a:b]

        x_in = [sem(f"x_in{b}") for b in range(TB)]
        vec_in = sem("vec_in")
        par_in = sem("par_in")
        id_in = sem("id_in")
        cst_in = sem("cst_in")
        gb_in = sem("gb_in")
        slab_in = [sem(f"slab_in{i}") for i in range(NSLOT)]
        slabs_used = sem("slabs_used")
        out_done = sem("out_done")
        sq_done = sem("sq_done")
        var_done = sem("var_done")
        rstd_done = sem("rstd_done")
        xn_done = sem("xn_done")
        ht_tr = sem("ht_tr")
        ht_v = sem("ht_v")
        ht_a = sem("ht_a")
        f_ps = sem("f_ps")
        ut_done = sem("ut_done")
        up_done = sem("up_done")
        qkv_done = sem("qkv_done")
        fz_a = sem("fz_a")
        fz_v = sem("fz_v")
        c_out = sem("c_out")
        c_rows = sem("c_rows")
        aug_ones = sem("aug_ones")
        bu_done = sem("bu_done")
        rot_done = sem("rot_done")
        zin_done = sem("zin_done")
        z_done = sem("z_done")
        zr_done = sem("zr_done")
        y_done = sem("y_done")
        trig_v = sem("trig_v")
        trig_a = sem("trig_a")
        tab_ok = sem("tab_ok")
        dt_ps = sem("dt_ps")
        dt_done = sem("dt_done")
        pl_ps = sem("pl_ps")
        mt_pool = sem("mt_pool")
        ys_done = sem("ys_done")
        gy_done = sem("gy_done")
        glu_ps = sem("glu_ps")
        sg_done = sem("sg_done")
        mt_ssm = sem("mt_ssm")
        sc_ps = sem("sc_ps")
        msk_done = sem("msk_done")
        mx_done = sem("mx_done")
        ex_done = sem("ex_done")
        rs_done = sem("rs_done")
        pn_done = sem("pn_done")
        pt_ps = sem("pt_ps")
        pt_done = sem("pt_done")
        ot_ps = sem("ot_ps")
        ot_done = sem("ot_done")
        bsq = sem("bsq")
        bss_ps = sem("bss_ps")
        bvar = sem("bvar")
        brs = sem("brs")
        mtn = sem("mtn")
        mix_ps = sem("mix_ps")
        up_ps = sem("up_ps")
        ffn_ps = sem("ffn_ps")
        silu_d = sem("silu_d")
        act_d = sem("act_d")
        post_tmp = sem("post_tmp")
        x_done = sem("x_done")
        lg_ps = sem("lg_ps")
        gate_d = sem("gate_d")
        gate_e = sem("gate_e")
        sel_done = sem("sel_done")
        pos_ps = sem("pos_ps")
        route_ok = sem("route_ok")
        g_done = sem("g_done")
        gw_done = sem("gw_done")
        ga_ps = sem("ga_ps")
        xgh_done = sem("xgh_done")
        xg_done = sem("xg_done")
        wh_done = sem("wh_done")
        mm_used = sem("mm_used")
        silu_m = sem("silu_m")
        h_done = sem("h_done")
        t_ps = sem("t_ps")
        ath_done = sem("ath_done")
        at_done = sem("at_done")
        gt_ps = sem("gt_ps")
        gt_done = sem("gt_done")
        y_v = sem("y_v")
        y_a = sem("y_a")
        acc_ps = sem("acc_ps")
        chain = sem("chain")

        block = ctx.enter_context(nc.Block())

        @block.sync
        def _(sp):
            def load(n, src, shape_of):
                slot = n % NSLOT
                if n >= NSLOT:
                    sp.wait_ge(slabs_used, n - NSLOT + 1)
                sp.dma_start(shape_of(slot), src).then_inc(slab_in[slot], 16)

            def cols(slot):
                return RING[:, slot, :].rearrange("p (k n) -> p k n", k=KT)

            def rows(slot):
                return RING[:, slot, :].rearrange("p (k n) -> p k n", k=2)

            def halves(slot):
                return RING[:, slot, :].rearrange("p (k c n) -> p k c n", k=4, c=2)

            w_in_v = w_in.rearrange("l (k p) n -> l p k n", p=P)
            w_out_v = w_out.rearrange("l (b k p) n -> l b p k n", p=P, k=2)
            gate_v = ffn_gate.rearrange("(k p) n -> p k n", p=P)
            up_v = ffn_up.rearrange("(k p) n -> p k n", p=P)
            down_v = ffn_down.rearrange("(u k p) n -> u p k n", p=P, k=2)
            mg_v = moe_gate.rearrange("e (h k p) n -> p e h k n", p=P, k=4)
            mu_v = moe_up.rearrange("e (h k p) n -> p e h k n", p=P, k=4)
            md_v = moe_down.rearrange("e (u k p) n -> p e u k n", p=P, k=2)

            sp.dma_start(PAR[:, :, 0:NVEC], params[:, :, 0:NVEC]).then_inc(vec_in, 16)
            sp.dma_start(CST[:, 0:C_MASK], consts[:, 0:C_MASK]).then_inc(id_in, 16)
            for n in range(TB):
                sp.dma_start(X[:, n, :], x[n * P:(n + 1) * P, :]).then_inc(x_in[n], 16)
            for l in range(LAYERS):
                b = BASE_MIX[l]
                for n, c in enumerate((S_OFF, P_OFF, 0, 256, 512, 768, 1024, 1280)):
                    load(b + n, w_in_v[l, :, :, c:c + W_COLS], cols)
                    if l == 0 and n == 1:
                        sp.dma_start(PAR[:, :, NVEC:NPAR], params[:, :, NVEC:NPAR]).then_inc(par_in, 16)
                        sp.dma_start(CST[:, C_MASK:NCONST], consts[:, C_MASK:NCONST]).then_inc(cst_in, 16)
                for n, r in enumerate((2, 3, 0, 1)):
                    load(b + 8 + n, w_out_v[l, r, :, :, :], rows)
                if l == 0:
                    for u in range(FT_DENSE // 2):
                        load(BASE_DENSE + 3 * u, gate_v[:, :, u * W_COLS:(u + 1) * W_COLS], cols)
                        load(BASE_DENSE + 3 * u + 1, up_v[:, :, u * W_COLS:(u + 1) * W_COLS], cols)
                        load(BASE_DENSE + 3 * u + 2, down_v[u, :, :, :], rows)

            def load_expert(i, e):
                for m, (kind, u) in enumerate(MOE_ORDER):
                    slot = (BASE_MOE + m) % NSLOT
                    sp.wait_ge(slabs_used, i * MOE_SLABS + (BASE_MOE + m - NSLOT + 1))
                    for c in range(2):
                        if kind == "d":
                            src = md_v[:, bass.ds(e, 1), u, c, :]
                            dst = rows(slot)[:, c, :]
                        else:
                            src = (mg_v, mu_v)[c][:, bass.ds(e, 1), "ab".index(kind), :, u * W_COLS:(u + 1) * W_COLS]
                            dst = halves(slot)[:, :, c, :]
                        sp.dma_start(dst.unsqueeze(1), src).then_inc(slab_in[slot], 16)

            with sp.Fori(0, NE) as e:
                load_expert(e, e)
            sp.wait_ge(route_ok, 1)
            over = sp.value_load(OVER[0:1, 0:1], min_val=0, max_val=T)
            with sp.If(over > CAP):
                for p in range(1, PASSES):
                    with sp.Fori(0, NE) as e:
                        load_expert(e + p * NE, e)
            sp.wait_ge(x_done, 16)
            sp.dma_start(out.rearrange("(b p) d -> p b d", p=P), X[:, :, :]).then_inc(out_done, 16)
            sp.wait_ge(out_done, 16)

        def arrived(eng, n):
            eng.wait_ge(slab_in[n % NSLOT], 16 * (n // NSLOT + 1))

        def moe_arrived(eng, i, m):
            slot = (BASE_MOE + m) % NSLOT
            before = len(range(slot, BASE_MOE, NSLOT))
            eng.wait_ge(slab_in[slot], i * (32 * MOE_SLABS // NSLOT) + (16 * before + 32 * (m // NSLOT + 1)))

        @block.tensor
        def _(pe):
            def norm_transpose(i):
                for b in range(TB):
                    pe.wait_ge(xn_done, TB * i + b + 1)
                    for k in range(KT):
                        at = (k % 2) * T + b * P
                        t = nc.tensor.transpose(bank[k // 2][:, at:at + P], XN[:, b, k * P:(k + 1) * P], ident)
                        if b == TB - 1 and k % 2:
                            t.then_inc(ht_tr, 1)

            def tile_of(slot, m, dst):
                w = RING[:, slot, :].rearrange("p (k n) -> p k n", k=KT)
                for k in range(KT):
                    t = nc.tensor.matmul(dst, w[:, k, m * P:(m + 1) * P], HT[:, k, :], start=k == 0, stop=k == KT - 1)
                return t

            def rows_of(slot, b, dst):
                w = RING[:, slot, :].rearrange("p (k n) -> p k n", k=KT)
                for k in range(KT):
                    t = nc.tensor.matmul(dst, HT[:, k, b * P:(b + 1) * P], w[:, k, :], start=k == 0, stop=k == KT - 1)
                return t

            def mixer(l):
                base = BASE_MIX[l]
                norm_transpose(2 * l)
                pe.wait_ge(ht_v, 4 * (2 * l) + 4)
                pe.wait_ge(ht_a, 4 * (2 * l) + 4)

                arrived(pe, base)
                for m in range(2):
                    t = tile_of(base % NSLOT, m, bank[4][:, m * T:(m + 1) * T])
                t.then_inc(slabs_used, 1)
                arrived(pe, base + 1)
                for b in range(TB):
                    t = rows_of((base + 1) % NSLOT, b, bank[5][:, b * T:(b + 1) * T])
                t.then_inc(slabs_used, 1)
                if l == 0:
                    pe.wait_ge(par_in, 16)
                    pe.wait_ge(cst_in, 16)
                wf = par(l, "w_f").rearrange("p (k h) -> p k h", k=KT)
                for k in range(KT):
                    t = nc.tensor.matmul(bank[6][0:HEADS, 0:T], wf[:, k, :], HT[:, k, :], start=k == 0, stop=k == KT - 1)
                t.then_inc(f_ps, 1)

                def scan_in(j):
                    if j == 0:
                        pe.wait_ge(ut_done, l + 1)
                        pe.wait_ge(up_done, l + 1)
                    if j >= 2:
                        pe.wait_ge(rot_done, 8 * l + j - 1)
                    r = SCH * (j % 4)
                    for c, name in enumerate(("b_re", "b_im")):
                        w = par(l, name)[r:r + SCH, (j // 4) * P:(j // 4 + 1) * P]
                        t = nc.tensor.matmul(bank[4 + j % 2][:, c * T:(c + 1) * T], w, UT[r:r + SCH, j // 4, :],
                                             start=True, stop=True)
                    t.then_inc(bu_done, 1)

                def scan_out(j):
                    if j == 0:
                        pe.wait_ge(tab_ok, l + 1)
                    pe.wait_ge(zr_done, 8 * l + j + 1)
                    if j == 0:
                        pe.wait_ge(fz_a, 3 * l + 3)
                        pe.wait_ge(fz_v, 4 * l + 1)
                    r = SCH * (j % 4)
                    dst = bank[6][r:r + SCH, (j // 4) * T:(j // 4 + 1) * T]
                    parts = ((0, ZC[:, j % 2, 0:T]), (1, ZS[:, j % 2, T:2 * T]),
                             (2, ZS[:, j % 2, 0:T]), (2, ZC[:, j % 2, T:2 * T]))
                    for n, (c, z) in enumerate(parts):
                        t = nc.tensor.matmul(dst, CC[:, c, j, :], z, start=n == 0, stop=n == 3)
                    t.then_inc(y_done, 1)

                def feature_tile(n):
                    s = base + 2 + n // 2
                    arrived(pe, s)
                    t = tile_of(s % NSLOT, n % 2, bank[n // 2][:, (n % 2) * T:(n % 2 + 1) * T])
                    if n % 2:
                        t.then_inc(slabs_used, 1)

                def value_slab(s):
                    n = base + 6 + s
                    arrived(pe, n)
                    if s == 0:
                        pe.wait_ge(mt_pool, l + 1)
                    for b in range(TB):
                        if s == 0 and b == 1:
                            pe.wait_ge(rot_done, 8 * l + 7)
                        t = rows_of(n % NSLOT, b, bank[7 if b == 0 else 4][:, s * T:(s + 1) * T])
                    t.then_inc(slabs_used, 1)

                def pool_band():
                    for g in range(NG):
                        r = (g % 2) * GC
                        dst = bank[7][r:r + GC, (g // 2) * T:(g // 2 + 1) * T]
                        nc.tensor.matmul(dst, UP[:, 0, g * GC:(g + 1) * GC], band[:, g, 0:2, :],
                                         start=True, stop=False)
                        t = nc.tensor.matmul(dst[:, P:T], UP[:, 1, g * GC:(g + 1) * GC], band[:, g, 2, :],
                                             start=False, stop=True)
                    t.then_inc(dt_ps, 1)

                def pool_mix():
                    pe.wait_ge(dt_done, l + 1)
                    w = par(l, "pool_w").rearrange("p (a n) -> p a n", a=2)
                    for a in range(2):
                        t = nc.tensor.matmul(bank[7][:, a * T:(a + 1) * T], w[:, a, :], DT[:, a, :], start=True, stop=True)
                    t.then_inc(pl_ps, 1)

                scan_in(0)
                scan_in(1)
                feature_tile(0)
                pool_band()
                scan_in(2)
                feature_tile(1)
                scan_in(3)
                pool_mix()
                feature_tile(2)
                scan_in(4)
                feature_tile(3)
                scan_out(0)
                scan_in(5)
                scan_out(1)
                feature_tile(4)
                scan_in(6)
                scan_out(2)
                feature_tile(5)
                scan_in(7)
                scan_out(3)
                feature_tile(6)
                scan_out(4)
                feature_tile(7)
                scan_out(5)
                value_slab(0)

                def scores(n):
                    pe.wait_ge(qkv_done, 6 * l + 4)
                    pe.wait_ge(c_rows, 32 * (l + 1))
                    if l == 0:
                        pe.wait_ge(aug_ones, 2)
                    if n >= 4:
                        pe.wait_ge(ex_done, 6 * l + n - 3)
                    heads, width = (4, P) if n < 2 else (2, T)
                    h0 = 4 * n if n < 2 else 2 * (n - 2)
                    q = QA[:, :, 0:P] if n < 2 else QA[:, :, P:T]
                    for h in range(heads):
                        t = nc.tensor.matmul(bank[SCORE_BANK[n]][:, h * width:(h + 1) * width], q[:, h0 + h, :],
                                             KA[:, h0 + h, 0:width], start=True, stop=True)
                    t.then_inc(sc_ps, 1)

                for n in range(4):
                    scores(n)
                scan_out(6)
                value_slab(1)
                scan_out(7)
                for n in (4, 5):
                    scores(n)

                pe.wait_ge(gy_done, l + 1)
                w = par(l, "w_glu").rearrange("p (a n) -> p a n", a=2)
                for m in range(2):
                    for k in range(2):
                        t = nc.tensor.matmul(bank[5][:, m * T:(m + 1) * T], w[:, k, m * P:(m + 1) * P], GY[:, k, :],
                                             start=k == 0, stop=k == 1)
                t.then_inc(glu_ps, 1)

                def branch_sum(n, tiles, dst):
                    pe.wait_ge(bsq, 3 * l + n + 1)
                    if n == 1:
                        pe.wait_ge(bvar, 3 * l + 1)
                    for i, k in enumerate(tiles):
                        t = nc.tensor.matmul(dst, ones, SQ[:, k, :], start=i == 0, stop=i == len(tiles) - 1)
                    t.then_inc(bss_ps, 1)

                def head_out(h):
                    pe.wait_ge(pt_done, 8 * l + h + 1)
                    r = (h % 2) * DH
                    dst = bank[2 + h // 4][r:r + DH, (h // 2 % 2) * T:(h // 2 % 2 + 1) * T]
                    nc.tensor.matmul(dst, V[:, 0, h * DH:(h + 1) * DH], PTS[:, h % 2, 0:T], start=True, stop=False)
                    t = nc.tensor.matmul(dst[:, P:T], V[:, 1, h * DH:(h + 1) * DH], PTS[:, h % 2, T:3 * P], start=False,
                                         stop=True)
                    if h % 4 == 3:
                        t.then_inc(ot_ps, 1)

                for h in range(HEADS):
                    pe.wait_ge(pn_done, 6 * l + 3 + h // 2)
                    if h >= 2:
                        pe.wait_ge(pt_done, 8 * l + h - 1)
                    if h == 0:
                        pe.wait_ge(qkv_done, 6 * l + 6)
                    dst = bank[PT_BANK[h % 2]]
                    nc.tensor.transpose(dst[:, 0:P], P0[:, h, :], ident)
                    nc.tensor.transpose(dst[:, P:2 * P], P1[:, h, 0:P], ident)
                    nc.tensor.transpose(dst[:, 2 * P:3 * P], P1[:, h, P:T], ident).then_inc(pt_ps, 1)
                    if h == 2:
                        branch_sum(0, (4, 5), bank[6][:, 0:T])
                    if h == 5:
                        branch_sum(1, (6, 7), bank[6][:, T:2 * T])
                    if h >= 1:
                        head_out(h - 1)
                head_out(HEADS - 1)

                def project(b, slabs):
                    for s in slabs:
                        n = base + 8 + s
                        arrived(pe, n)
                        w = RING[:, n % NSLOT, :].rearrange("p (k n) -> p k n", k=2)
                        for k in range(2):
                            kt = (4, 6, 0, 2)[s] + k
                            pe.wait_ge(mtn, 8 * l + (0, 2, 4, 6)[s] + k + 1)
                            for c in range(2):
                                t = nc.tensor.matmul(bank[MIX_BANKS[2 * b + c]][:, :], MT[:, kt, b * P:(b + 1) * P],
                                                     w[:, k, c * 512:(c + 1) * 512], start=s == 0 and k == 0,
                                                     stop=s == 3 and k == 1)
                        if b == 1:
                            t.then_inc(slabs_used, 1)
                    return t

                project(0, (0, 1))
                branch_sum(2, (0, 1, 2, 3), bank[5][:, 0:T])
                project(1, (0, 1))
                project(0, (2, 3)).then_inc(mix_ps, 1)
                project(1, (2, 3))

            def dense():
                norm_transpose(1)
                pe.wait_ge(ht_v, 8)
                pe.wait_ge(ht_a, 8)

                def up(ft):
                    g, u = BASE_DENSE + 3 * (ft // 2), BASE_DENSE + 3 * (ft // 2) + 1
                    arrived(pe, g)
                    arrived(pe, u)
                    if ft >= 4:
                        pe.wait_ge(act_d, ft - 3)
                    for c, n in enumerate((g, u)):
                        t = tile_of(n % NSLOT, ft % 2, bank[ft % 4][:, c * T:(c + 1) * T])
                        if c == 0 and ft % 2:
                            t.then_inc(slabs_used, 1)
                    t.then_inc(up_ps, 1)

                def down(ft):
                    n = BASE_DENSE + 3 * (ft // 2) + 2
                    arrived(pe, n)
                    pe.wait_ge(act_d, ft + 1)
                    w = RING[:, n % NSLOT, :].rearrange("p (k n) -> p k n", k=2)
                    for b in range(TB):
                        for c in range(2):
                            t = nc.tensor.matmul(bank[4 + 2 * b + c][:, :], AT[:, ft % 2, b * P:(b + 1) * P],
                                                 w[:, ft % 2, c * 512:(c + 1) * 512], start=ft == 0,
                                                 stop=ft == FT_DENSE - 1)
                            if ft % 2 == 0 and b == 0 and c == 0:
                                t.then_inc(slabs_used, 1)
                            if ft == FT_DENSE - 1 and b == 0 and c == 1:
                                t.then_inc(ffn_ps, 1)
                    if ft % 2:
                        t.then_inc(slabs_used, 1)
                    return t

                for ft in range(FT_DENSE):
                    up(ft)
                    if ft:
                        down(ft - 1)
                down(FT_DENSE - 1)

            def routing():
                rt = par(1, "router").rearrange("p (k e) -> p k e", k=KT)
                for b in range(TB):
                    for k in range(KT):
                        t = nc.tensor.matmul(bank[4][:, b * NE:(b + 1) * NE], HT[:, k, b * P:(b + 1) * P], rt[:, k, :],
                                             start=k == 0, stop=k == KT - 1)
                t.then_inc(lg_ps, 1)
                pe.wait_ge(sel_done, 1)
                dst = bank[5]
                nc.tensor.matmul(dst[:, 0:NE], tri, SEL[:, 0, :], start=True, stop=True)
                nc.tensor.matmul(dst[:, NE:2 * NE], ones, SEL[:, 0, :], start=True, stop=False)
                nc.tensor.matmul(dst[:, NE:2 * NE], tri, SEL[:, 1, :], start=False, stop=True)
                nc.tensor.matmul(dst[:, 2 * NE:3 * NE], ones, SEL[:, 0, :], start=True, stop=False)
                nc.tensor.matmul(dst[:, 2 * NE:3 * NE], ones, SEL[:, 1, :], start=False, stop=True).then_inc(pos_ps, 1)

            def gather(i, h):
                for k in range(4):
                    for b in range(TB):
                        t = nc.tensor.matmul(bank[h][:, k * SLOTS:(k + 1) * SLOTS],
                                             XN[:, b, (4 * h + k) * P:(4 * h + k + 1) * P], GM[:, b, :],
                                             start=b == 0, stop=b == TB - 1)
                t.then_inc(ga_ps, 1)

            def scatter_waits(i):
                pe.wait_ge(y_v, i + 1)
                pe.wait_ge(y_a, i + 1)
                pe.wait_ge(gt_done, i + 1)

            def item(i):
                pe.wait_ge(xg_done, i * 2 + 2)
                for m, (kind, u) in enumerate(MOE_ORDER):
                    if m == MOE_SLABS - 1:
                        pe.wait_ge(g_done, i + 2)
                        gather(i + 1, 0)
                        transpose_unit(i, UNITS - 1)
                        pe.wait_ge(xgh_done, i * 2 + 3)
                        pe.wait_ge(xg_done, i * 2 + 3)
                        pe.wait_ge(gw_done, i + 1)
                        for b in range(TB):
                            t = nc.tensor.transpose(bank[0][0:SLOTS, b * P:(b + 1) * P], GW[:, b, :], ident)
                        t.then_inc(gt_ps, 1)
                    pe.wait_ge(slabs_used, i * MOE_SLABS + (BASE_MOE + m + 1))
                    hi, lo = WH[:, m % NSPLIT, :], WL[:, m % NSPLIT, :]
                    if kind == "d":
                        pe.wait_ge(at_done, i * UNITS + (u + 1))
                        wh = hi.rearrange("p (j c n) -> p j c n", j=2, c=2)
                        wl = lo.rearrange("p (j c n) -> p j c n", j=2, c=2)
                        for j in range(2):
                            for n, (x_, w_) in enumerate(((ATH, wh), (ATH, wl), (ATL, wh))):
                                for c in range(2):
                                    t = nc.tensor.matmul(bank[2 + c][0:SLOTS, :], x_[:, j, :], w_[:, j, c, :],
                                                         start=u == 0 and j == 0 and n == 0,
                                                         stop=u == UNITS - 1 and j == 1 and n == 2)
                    else:
                        if kind == "a" and u >= 2:
                            pe.wait_ge(at_done, i * UNITS + (u - 1))
                        wh = hi.rearrange("p (k n) -> p k n", k=4)
                        wl = lo.rearrange("p (k n) -> p k n", k=4)
                        for k in range(4):
                            kt = 4 * "ab".index(kind) + k
                            for n, (x_, w_) in enumerate(((XGH, wh), (XGH, wl), (XGL, wh))):
                                t = nc.tensor.matmul(bank[u % 2][0:SLOTS, :], x_[:, kt, :], w_[:, k, :],
                                                     start=kt == 0 and n == 0, stop=kt == KT - 1 and n == 2)
                    t.then_inc(mm_used, 1)
                    if kind == "a" and u >= 1:
                        transpose_unit(i, u - 1)
                gather(i + 1, 1)
                scatter_waits(i + 1)
                for b in range(TB):
                    for c in range(2):
                        t = nc.tensor.matmul(bank[4 + 2 * b + c][:, :], GT[:, b * P:(b + 1) * P],
                                             YE[:, c * 512:(c + 1) * 512], start=False, stop=False, skip_group_check=True)
                t.then_inc(acc_ps, 1)

            def transpose_unit(i, u):
                pe.wait_ge(h_done, i * UNITS + (u + 1))
                for j in range(2):
                    t = nc.tensor.transpose(bank[u % 2][:, j * SLOTS:(j + 1) * SLOTS], HM[:, j * P:(j + 1) * P],
                                            ident[0:SLOTS, 0:SLOTS])
                t.then_inc(t_ps, 1)

            def experts():
                norm_transpose(3)
                pe.wait_ge(ht_v, 16)
                pe.wait_ge(ht_a, 16)
                routing()
                pe.wait_ge(route_ok, 1)
                scatter_waits(0)
                for c in range(4):
                    t = nc.tensor.matmul(bank[4 + c][:, :], GT[:, 0:P], YE[:, 0:512], start=True, stop=False,
                                         skip_group_check=True)
                    if c < 2:
                        t.then_inc(mm_used, 1)
                pe.wait_ge(g_done, 1)
                gather(0, 0)
                gather(0, 1)
                with pe.Fori(0, NE) as e:
                    item(e)
                over = pe.value_load(OVER[0:1, 0:1], min_val=0, max_val=T)
                with pe.If(over > CAP):
                    for p in range(1, PASSES):
                        with pe.Fori(0, NE) as e:
                            item(e + p * NE)

            pe.wait_ge(id_in, 16)
            mixer(0)
            dense()
            mixer(1)
            experts()

        @block.scalar
        def _(act):
            def sumsq(n, b, sources):
                for h, (src, dst) in enumerate(sources):
                    t = nc.scalar.activation(dst, src, ACT.Square, accum_out=STAT[:, 2 * b + h:2 * b + h + 1])
                t.then_inc(sq_done, 1)

            def pre_norm(i):
                for b in range(TB):
                    if i == 0:
                        act.wait_ge(x_in[b], 16)
                    if i:
                        act.wait_ge(x_done, 4 * (i - 1) + 2 * b + 2)
                        act.wait_ge(rstd_done, 4 * i)
                    sumsq(2 * i, b, [(X[:, b, :], XN[:, b, :])])
                gain = par(i // 2, "g_ffn" if i % 2 else "g_mix")
                for k in (2, 3, 6, 7):
                    act.wait_ge(ht_tr, 4 * i + k // 2 + 1)
                    nc.scalar.activation(HT[:, k, :], bank[k // 2][:, (k % 2) * T:(k % 2 + 1) * T], ACT.Identity,
                                         scale=gain[:, k:k + 1]).then_inc(ht_a, 1)

            def post_norm(i, banks, first, second):
                if i:
                    act.wait_ge(x_done, 4 * i)
                act.dma_start(GB[:, :], g_post[i, :, :]).then_inc(gb_in, 16)
                for b, ready in enumerate((first, second)):
                    act.wait_ge(*ready)
                    act.wait_ge(rstd_done, 2 * (2 * i + 1))
                    sumsq(2 * i + 1, b, [(bank[banks[2 * b + h]][:, :], XN[:, b, h * 512:(h + 1) * 512]) for h in range(2)])

            def scan_tables(l, part):
                if part == 0:
                    if l:
                        act.wait_ge(tab_ok, l)
                    nc.scalar.activation(SV[:, 0, :], par(l, "log_dt"), ACT.Tanh, scale=1.0 / 16.0).then_inc(trig_a, 1)
                    return
                if part == 1:
                    act.wait_ge(trig_v, 2 * l + 1)
                    nc.scalar.activation(SV[:, 6, :], SV[:, 5, :], ACT.Tanh, scale=0.5).then_inc(trig_a, 1)
                    return
                act.wait_ge(trig_v, 2 * l + 2)
                for h in range(2):
                    nc.scalar.activation(COS[:, 4 * h:4 * h + 4, :], SIN[:, 4 * h:4 * h + 4, :], ACT.Sin, scale=TURN / 2)
                for h in range(2):
                    t = nc.scalar.activation(SIN[:, 4 * h:4 * h + 4, :], SIN[:, 4 * h:4 * h + 4, :], ACT.Sin, scale=TURN)
                t.then_inc(trig_a, 1)

            def heads_out(dst, src, scale):
                for o in range(2):
                    t = nc.scalar.activation(dst[:, :, o, :], src[o * DH:(o + 1) * DH, :].rearrange("p (m t) -> p m t", m=2),
                                             ACT.Copy, scale=scale)
                return t

            def mixer(l):
                base = BASE_MIX[l]
                pre_norm(2 * l)
                if l == 0:
                    scan_tables(0, 2)
                act.wait_ge(slabs_used, base + 1)
                nc.scalar.copy(UT[:, :, :], bank[4][:, :].rearrange("p (a t) -> p a t", a=2)).then_inc(ut_done, 1)
                act.wait_ge(slabs_used, base + 2)
                nc.scalar.copy(UP[:, :, :], bank[5][:, :].rearrange("p (a t) -> p a t", a=2)).then_inc(up_done, 1)
                act.wait_ge(f_ps, l + 1)
                nc.scalar.activation(FG[:, 0, :], bank[6][0:HEADS, 0:T], ACT.Abs, bias=par(l, "b_forget")[0:HEADS, :])\
                    .then_inc(fz_a, 1)
                act.wait_ge(fz_a, 3 * l + 1)
                nc.scalar.activation(FG[:, 1, :], FG[:, 0, :], ACT.Exp, scale=-1.0).then_inc(fz_a, 1)
                act.wait_ge(fz_a, 3 * l + 2)
                nc.scalar.activation(FG[:, 2, :], FG[:, 1, :], ACT.Ln, bias=1.0).then_inc(fz_a, 1)
                act.wait_ge(dt_ps, l + 1)
                nc.scalar.copy(DT[:, :, :], bank[7][:, :].rearrange("p (a t) -> p a t", a=2)).then_inc(dt_done, 1)
                qa = QA[0:DH, :, :].rearrange("p (b m o) t -> p b m o t", b=2, m=2)
                ka = KA[0:DH, :, :].rearrange("p (b m o) t -> p b m o t", b=2, m=2)
                act.wait_ge(slabs_used, base + 3)
                heads_out(qa[:, 0, :, :, :], bank[0], DH ** -0.5).then_inc(qkv_done, 1)
                act.wait_ge(pl_ps, l + 1)
                ps = par(l, "pool_scale")
                for a in range(2):
                    t = nc.scalar.activation(MT[:, 4 + a, :], bank[7][:, a * T:(a + 1) * T], ACT.Identity, scale=ps[:, a:a + 1])
                t.then_inc(mt_pool, 1)
                act.wait_ge(slabs_used, base + 4)
                heads_out(qa[:, 1, :, :, :], bank[1], DH ** -0.5).then_inc(qkv_done, 1)
                for n in range(2):
                    act.wait_ge(slabs_used, base + 5 + n)
                    heads_out(ka[:, n, :, :, :], bank[2 + n], 1.0).then_inc(qkv_done, 1)
                def numerators(n):
                    act.wait_ge(mx_done, 6 * l + n + 1)
                    if n == 2:
                        act.wait_ge(zr_done, 8 * l + 8)
                    heads, width = (4, P) if n < 2 else (2, T)
                    at = 4 * n if n < 2 else 8 + 2 * (n - 2)
                    for h in range(heads):
                        dst = P0[:, at + h, :] if n < 2 else P1[:, at + h - 8, :]
                        t = nc.scalar.activation(dst, bank[SCORE_BANK[n]][:, h * width:(h + 1) * width], ACT.Exp,
                                                 bias=MX[:, at + h:at + h + 1], accum_out=SUM[:, at + h:at + h + 1])
                    t.then_inc(ex_done, 1)

                for n in range(4):
                    numerators(n)
                for n, bk in enumerate((7, 4)):
                    act.wait_ge(slabs_used, base + 8)
                    nc.scalar.copy(V[:, n, :], bank[bk][:, :]).then_inc(qkv_done, 1)
                nc.scalar.activation(SQ[:, 4:6, :], MT[:, 4:6, :], ACT.Square).then_inc(bsq, 1)
                for n in (4, 5):
                    numerators(n)
                act.wait_ge(ys_done, l + 1)
                nc.scalar.activation(GY[:, :, :], YS[:, :, :], ACT.Gelu_apprx_tanh).then_inc(gy_done, 1)
                act.wait_ge(glu_ps, l + 1)
                bg = par(l, "b_glu")
                for m in range(2):
                    t = nc.scalar.activation(SG[:, m, :], bank[5][:, m * T:(m + 1) * T], ACT.Sigmoid, bias=bg[:, m:m + 1])
                t.then_inc(sg_done, 1)
                act.wait_ge(mt_ssm, l + 1)
                nc.scalar.activation(SQ[:, 6:8, :], MT[:, 6:8, :], ACT.Square).then_inc(bsq, 1)
                def branch_rstd(n):
                    act.wait_ge(bvar, 3 * l + n + 1)
                    nc.scalar.activation(RB[:, n, :], RB[:, n, :], ACT.Sqrt).then_inc(brs, 1)

                for h in range(HEADS):
                    if h in (4, 7):
                        branch_rstd((h - 4) // 3)
                    act.wait_ge(pt_ps, 8 * l + h + 1)
                    nc.scalar.copy(PTS[:, h % 2, :], bank[PT_BANK[h % 2]][:, 0:3 * P]).then_inc(pt_done, 1)
                for m in range(2):
                    act.wait_ge(ot_done, 2 * l + m + 1)
                    t = nc.scalar.activation(SQ[:, 2 * m:2 * m + 2, :], MT[:, 2 * m:2 * m + 2, :], ACT.Square)
                t.then_inc(bsq, 1)
                branch_rstd(2)
                post_norm(2 * l, MIX_BANKS, (mix_ps, l + 1), (slabs_used, base + 12))

            def dense():
                pre_norm(1)
                for ft in range(FT_DENSE):
                    act.wait_ge(up_ps, ft + 1)
                    nc.scalar.activation(SA[:, ft % 2, :], bank[ft % 4][:, 0:T], ACT.Silu).then_inc(silu_d, 1)
                    if ft == 0:
                        scan_tables(1, 0)
                    if ft == 2:
                        scan_tables(1, 1)
                    if ft == 5:
                        scan_tables(1, 2)
                post_norm(1, (4, 5, 6, 7), (ffn_ps, 1), (slabs_used, BASE_MIX[1]))

            def silu(i, u):
                act.wait_ge(mm_used, i * MOE_SLABS + (AT_SLAB["b", u] + 3))
                nc.scalar.activation(SM[:, :], bank[u % 2][0:SLOTS, 0:W_COLS], ACT.Silu).then_inc(silu_m, 1)

            def high_part(i, m):
                moe_arrived(act, i, m)
                nc.scalar.copy(WH[:, m % NSPLIT, :], RING[:, (BASE_MOE + m) % NSLOT, :]).then_inc(wh_done, 1)

            def item(i, first=0):
                for m in range(first, MOE_SLABS):
                    if m >= 1:
                        act.wait_ge(mm_used, i * MOE_SLABS + m)
                    high_part(i, m)
                    if m >= 3 and m % 3 == 0:
                        silu(i, m // 3 - 1)
                silu(i, UNITS - 1)
                act.wait_ge(mm_used, i * MOE_SLABS + (MOE_SLABS + 2))
                nc.scalar.copy(YE[:, 512:D], bank[3][0:SLOTS, :]).then_inc(y_a, 1)

            def experts():
                pre_norm(3)
                for m in range(NSPLIT):
                    high_part(0, m)
                act.wait_ge(gate_d, 1)
                nc.scalar.activation(GATE[:, :, 1:2], GATE[:, :, 0:1], ACT.Exp).then_inc(gate_e, 1)
                act.wait_ge(y_a, 1)
                item(0, NSPLIT)
                with act.Fori(1, NE) as e:
                    item(e)
                act.wait_ge(acc_ps, NE)
                over = act.value_load(OVER[0:1, 0:1], min_val=0, max_val=T)
                with act.If(over > CAP):
                    for p in range(1, PASSES):
                        with act.Fori(0, NE) as e:
                            item(e + p * NE)
                    act.wait_ge(acc_ps, PASSES * NE)
                post_norm(3, (4, 5, 6, 7), (acc_ps, NE), (acc_ps, NE))

            act.wait_ge(vec_in, 16)
            scan_tables(0, 0)
            scan_tables(0, 1)
            mixer(0)
            dense()
            mixer(1)
            experts()

        @block.gpsimd
        def _(pool):
            steps = [0]

            def rstd(n, post):
                for b in range(TB):
                    pool.wait_ge(sq_done, 2 * n + b + 1)
                    v = STAT[:, 2 * b:2 * b + 1]
                    if post:
                        nc.gpsimd.tensor_tensor(STAT[:, 4 + b:5 + b], v, STAT[:, 2 * b + 1:2 * b + 2], ALU.add)\
                            .then_inc(var_done, 1)
                        steps[0] += 1
                        pool.wait_ge(var_done, steps[0])
                        v = STAT[:, 4 + b:5 + b]
                    nc.gpsimd.tensor_scalar(STAT[:, 6 + b:7 + b], v, 1.0 / D, EPS, ALU.mult, ALU.add).then_inc(var_done, 1)
                    steps[0] += 1
                    pool.wait_ge(var_done, steps[0])
                    if n:
                        pool.wait_ge(xn_done if post else x_done, (n + 1) if post else 2 * n)
                    nc.gpsimd.tensor_tensor(RSTD[:, b:b + 1], STAT[:, 6 + b:7 + b], EXPO[:, 0:1], ALU.pow).then_inc(rstd_done, 1)

            def mixer(l):
                rstd(4 * l, False)
                for j in range(SJ):
                    pool.wait_ge(z_done, 8 * l + j + 1)
                    if j >= 2:
                        pool.wait_ge(y_done, 8 * l + j - 1)
                    z = Z[:, j % 2, :].rearrange("p (c t) -> p c t", c=2)
                    for dst, tab in ((ZC, COS), (ZS, SIN)):
                        t = nc.gpsimd.tensor_tensor(dst[:, j % 2, :].rearrange("p (c t) -> p c t", c=2), z,
                                                    tab[:, j, :].unsqueeze(1).to_broadcast([P, 2, T]), ALU.mult)
                    t.then_inc(zr_done, 1)
                    if j == 2:
                        pool.wait_ge(fz_v, 4 * l + 4)
                        pool.dma_start(c_dram[l, :, :, :], FG[:, 4:6, :]).then_inc(c_out, 16)
                    if j == 4:
                        pool.wait_ge(c_out, 16 * (l + 1))
                        for n, dst in enumerate((QA[DH:DH + 1, :, :], KA[DH + 1:DH + 2, :, :])):
                            pool.dma_start(dst, c_dram[l, :, n, :].unsqueeze(0)).then_inc(c_rows, 16)
                rstd(4 * l + 1, True)

            for n, m in enumerate((QA, KA)):
                if n:
                    pool.wait_ge(aug_ones, n)
                nc.gpsimd.memset(m[DH:DH + 2, :, :], 1.0).then_inc(aug_ones, 1)
            pool.wait_ge(aug_ones, 2)
            nc.gpsimd.memset(EXPO[:, :], -0.5).then_inc(aug_ones, 1)
            pool.wait_ge(aug_ones, 3)
            mixer(0)
            rstd(2, False)
            rstd(3, True)
            mixer(1)
            rstd(6, False)
            rstd(7, True)

        @block.vector
        def _(dve):
            links = [0]

            def link(t):
                t.then_inc(chain, 1)
                links[0] += 1
                dve.wait_ge(chain, links[0])

            TT, TS, STT = nc.vector.tensor_tensor, nc.vector.tensor_scalar, nc.vector.scalar_tensor_tensor

            def pre_norm(i):
                for b in range(TB):
                    dve.wait_ge(rstd_done, 4 * i + b + 1)
                    if i:
                        dve.wait_ge(ht_tr, 4 * i)
                    if i == 0:
                        dve.wait_ge(x_in[b], 16)
                    TS(XN[:, b, :], X[:, b, :], RSTD[:, b:b + 1], None, ALU.mult).then_inc(xn_done, 1)
                gain = par(i // 2, "g_ffn" if i % 2 else "g_mix")
                for k in (0, 1, 4, 5):
                    dve.wait_ge(ht_tr, 4 * i + k // 2 + 1)
                    TS(HT[:, k, :], bank[k // 2][:, (k % 2) * T:(k % 2 + 1) * T], gain[:, k:k + 1], None, ALU.mult)\
                        .then_inc(ht_v, 1)

            def post_norm(i, banks):
                dve.wait_ge(gb_in, 16 * (i + 1))
                for b in range(TB):
                    dve.wait_ge(rstd_done, 4 * i + 2 + b + 1)
                    for h in range(2):
                        if b:
                            dve.wait_ge(x_done, 4 * i + h + 1)
                        STT(TMP[:, h * 512:(h + 1) * 512], bank[banks[2 * b + h]][:, :], RSTD[:, b:b + 1],
                            GB[:, h * 512:(h + 1) * 512], ALU.mult, ALU.mult).then_inc(post_tmp, 1)
                    for h in range(2):
                        dve.wait_ge(post_tmp, 4 * i + 2 * b + h + 1)
                        TT(X[:, b, h * 512:(h + 1) * 512], X[:, b, h * 512:(h + 1) * 512],
                           TMP[:, h * 512:(h + 1) * 512], ALU.add).then_inc(x_done, 1)

            def s(n):
                return SV[:, n, :]

            def scan_steps(l):
                a_re = par(l, "a_re")
                dve.wait_ge(trig_a, 3 * l + 1)
                if l:
                    dve.wait_ge(y_done, 8 * l)
                link(TS(s(1), s(0), 1.0, None, ALU.add))
                link(TS(s(2), s(0), -1.0, 1.0, ALU.mult, ALU.add))
                link(nc.vector.reciprocal(s(2), s(2)))
                link(TT(s(3), s(1), s(2), ALU.mult))
                for _ in range(3):
                    link(TT(s(3), s(3), s(3), ALU.mult))
                TT(s(5), a_re, s(3), ALU.mult).then_inc(trig_v, 1)

            def scan_phases(l):
                a_im = par(l, "a_im")
                link(TT(s(9), a_im, s(3), ALU.mult))
                link(TS(s(10), s(9), 1.0 / (2.0 * math.pi), None, ALU.mult))
                link(TS(s(11), s(10), ROUND, None, ALU.add))
                link(TS(s(11), s(11), -ROUND, None, ALU.add))
                link(TT(s(10), s(10), s(11), ALU.subtract))
                for j in range(SJ):
                    t = TS(COS[:, j, :], iota, s(10)[:, j:j + 1], ROUND, ALU.mult, ALU.add)
                link(t)
                link(TS(COS, COS, -ROUND, None, ALU.add))
                for j in range(SJ):
                    t = STT(SIN[:, j, :], iota, s(10)[:, j:j + 1], COS[:, j, :], ALU.mult, ALU.subtract)
                t.then_inc(trig_v, 1)

            def scan_coefs(l):
                a_re, a_im = par(l, "a_re"), par(l, "a_im")
                dve.wait_ge(trig_a, 3 * l + 2)
                link(TS(s(7), s(6), -1.0, 1.0, ALU.mult, ALU.add))
                link(nc.vector.reciprocal(s(7), s(7)))
                link(STT(s(7), s(7), 2.0, s(6), ALU.mult, ALU.mult))
                link(TS(s(8), s(7), 1.0, None, ALU.add))
                dve.wait_ge(trig_a, 3 * l + 3)
                for h in range(2):
                    c = COS[:, 4 * h:4 * h + 4, :]
                    link(TT(c, c, c, ALU.mult))
                sin1 = SIN[:, :, 1]
                link(TS(s(12), COS[:, :, 1], -2.0, None, ALU.mult))
                link(TS(s(13), s(12), 1.0, None, ALU.add))
                link(TT(s(13), s(13), s(7), ALU.mult))
                link(TT(s(13), s(13), s(12), ALU.add))
                link(TT(s(14), s(8), sin1, ALU.mult))
                link(TT(s(15), a_re, a_re, ALU.mult))
                link(TT(s(16), a_im, a_im, ALU.mult))
                link(TT(s(15), s(15), s(16), ALU.add))
                link(nc.vector.reciprocal(s(15), s(15)))
                link(TT(s(16), s(13), a_re, ALU.mult))
                link(TT(s(17), s(14), a_im, ALU.mult))
                link(TT(s(16), s(16), s(17), ALU.add))
                link(TT(s(16), s(16), s(15), ALU.mult))
                link(TT(s(17), s(14), a_re, ALU.mult))
                link(TT(s(18), s(13), a_im, ALU.mult))
                link(TT(s(17), s(17), s(18), ALU.subtract))
                link(TT(s(17), s(17), s(15), ALU.mult))
                for h in range(2):
                    c = COS[:, 4 * h:4 * h + 4, :]
                    link(TS(c, c, -2.0, 1.0, ALU.mult, ALU.add))
                cr = par(l, "c_re").rearrange("p (j c) -> p j c", j=SJ)
                ci = par(l, "c_im").rearrange("p (j c) -> p j c", j=SJ)
                re = s(16).unsqueeze(2).to_broadcast([P, SJ, SCH])
                im = s(17).unsqueeze(2).to_broadcast([P, SJ, SCH])
                link(TT(CT[:, 0, :, :], cr, re, ALU.mult))
                link(TT(CT[:, 1, :, :], ci, im, ALU.mult))
                link(TT(CC[:, 0, :, :], CT[:, 0, :, :], CT[:, 1, :, :], ALU.subtract))
                link(TT(CT[:, 0, :, :], cr, im, ALU.mult))
                link(TT(CT[:, 1, :, :], ci, re, ALU.mult))
                link(TT(CT[:, 0, :, :], CT[:, 0, :, :], CT[:, 1, :, :], ALU.add))
                link(TS(CC[:, 2, :, :], CT[:, 0, :, :], -1.0, None, ALU.mult))
                TS(CC[:, 1, :, :], CC[:, 0, :, :], -1.0, None, ALU.mult).then_inc(tab_ok, 1)

            def scan_tile(l, j):
                dve.wait_ge(bu_done, 8 * l + j + 1)
                bu = bank[4 + j % 2][:, :].rearrange("p (c t) -> p c t", c=2)
                for n, tab in enumerate((COS, SIN)):
                    t = TT(ROT[:, n, :].rearrange("p (c t) -> p c t", c=2), bu,
                           tab[:, j, :].unsqueeze(1).to_broadcast([P, 2, T]), ALU.mult)
                t.then_inc(rot_done, 1)
                dve.wait_ge(rot_done, 8 * l + j + 1)
                TT(ZIN[:, 0:T], ROT[:, 0, 0:T], ROT[:, 1, T:2 * T], ALU.add)
                TT(ZIN[:, T:2 * T], ROT[:, 0, T:2 * T], ROT[:, 1, 0:T], ALU.subtract).then_inc(zin_done, 1)
                dve.wait_ge(zin_done, 8 * l + j + 1)
                if j >= 2:
                    dve.wait_ge(zr_done, 8 * l + j - 1)
                r = SV[:, 8, j:j + 1].to_broadcast([P, T])
                for c in range(2):
                    t = nc.vector.tensor_tensor_scan(Z[:, j % 2, c * T:(c + 1) * T], r, ZIN[:, c * T:(c + 1) * T], 0.0,
                                                     ALU.mult, ALU.add)
                t.then_inc(z_done, 1)

            def branch_norm(l, n, src, width):
                dve.wait_ge(bss_ps, 3 * l + n + 1)
                link(TS(RB[:, n, :], src, 1.0 / width, EPS, ALU.mult, ALU.add))
                nc.vector.reciprocal(RB[:, n, :], RB[:, n, :]).then_inc(bvar, 1)

            def branch_scale(l, n, tiles):
                dve.wait_ge(brs, 3 * l + n + 1)
                dve.wait_ge(bsq, 3 * l + n + 1)
                g = par(l, "g_br")
                for k in tiles:
                    STT(MT[:, k, :], MT[:, k, :], g[:, k:k + 1], RB[:, n, :], ALU.mult, ALU.mult).then_inc(mtn, 1)

            def softmax_max(l, n):
                dve.wait_ge(sc_ps, 6 * l + n + 1)
                bk = bank[SCORE_BANK[n]]
                heads, width = (4, P) if n < 2 else (2, T)
                at = 4 * n if n < 2 else 8 + 2 * (n - 2)
                sc = bk[:, :].rearrange("p (h k) -> p h k", h=heads)
                diag = sc[:, :, width - P:width]
                TT(diag, diag, mask.unsqueeze(1).to_broadcast([P, heads, P]), ALU.add).then_inc(msk_done, 1)
                dve.wait_ge(msk_done, 6 * l + n + 1)
                nc.vector.tensor_reduce(MX[:, at:at + heads], sc, AX, ALU.max, negate=True).then_inc(mx_done, 1)

            def softmax_scale(l, n):
                dve.wait_ge(ex_done, 6 * l + n + 1)
                heads, width = (4, P) if n < 2 else (2, T)
                at = 4 * n if n < 2 else 8 + 2 * (n - 2)
                nc.vector.reciprocal(RS[:, at:at + heads], SUM[:, at:at + heads]).then_inc(rs_done, 1)
                dve.wait_ge(rs_done, 6 * l + n + 1)
                p = P0[:, at:at + heads, :] if n < 2 else P1[:, at - 8:at - 8 + heads, :]
                TT(p, p, RS[:, at:at + heads].unsqueeze(2).to_broadcast([P, heads, width]), ALU.mult).then_inc(pn_done, 1)

            def mixer(l):
                pre_norm(2 * l)
                if l == 0:
                    dve.wait_ge(par_in, 16)
                    dve.wait_ge(cst_in, 16)
                    scan_coefs(0)
                scan_tile(l, 0)
                dve.wait_ge(fz_a, 3 * l + 1)
                TS(FG[:, 3, :], bank[6][0:HEADS, 0:T], par(l, "b_forget")[0:HEADS, :], 0.0, ALU.add, ALU.min)\
                    .then_inc(fz_v, 1)
                scan_tile(l, 1)
                dve.wait_ge(fz_a, 3 * l + 3)
                dve.wait_ge(fz_v, 4 * l + 1)
                TT(FG[:, 3, :], FG[:, 3, :], FG[:, 2, :], ALU.subtract).then_inc(fz_v, 1)
                dve.wait_ge(fz_v, 4 * l + 2)
                nc.vector.tensor_tensor_scan(FG[:, 4, :], ones[0:HEADS, 0:1].to_broadcast([HEADS, T]), FG[:, 3, :], 0.0,
                                             ALU.mult, ALU.add).then_inc(fz_v, 1)
                dve.wait_ge(fz_v, 4 * l + 3)
                TS(FG[:, 5, :], FG[:, 4, :], -1.0, None, ALU.mult).then_inc(fz_v, 1)
                for j in range(2, SJ):
                    scan_tile(l, j)
                for n in range(4):
                    softmax_max(l, n)
                dve.wait_ge(y_done, 8 * (l + 1))
                d = par(l, "ssm_d")
                for a in range(2):
                    t = STT(YS[:, a, :], UT[:, a, :], d[:, a:a + 1], bank[6][:, a * T:(a + 1) * T], ALU.mult, ALU.add)
                t.then_inc(ys_done, 1)
                for n in range(4):
                    softmax_scale(l, n)
                for n in (4, 5):
                    softmax_max(l, n)
                for n in (4, 5):
                    softmax_scale(l, n)
                dve.wait_ge(sg_done, l + 1)
                TT(MT[:, 6:8, :], GY[:, :, :], SG[:, :, :], ALU.mult).then_inc(mt_ssm, 1)
                branch_norm(l, 0, bank[6][:, 0:T], NG * GC)
                branch_scale(l, 0, (4, 5))
                for m in range(2):
                    if m == 1:
                        branch_norm(l, 1, bank[6][:, T:2 * T], SJ * SCH)
                        branch_scale(l, 1, (6, 7))
                    dve.wait_ge(ot_ps, 2 * l + m + 1)
                    nc.vector.tensor_copy(MT[:, 2 * m:2 * m + 2, :], bank[2 + m][:, :].rearrange("p (a t) -> p a t", a=2))\
                        .then_inc(ot_done, 1)
                branch_norm(l, 2, bank[5][:, 0:T], HEADS * DH)
                branch_scale(l, 2, (0, 1, 2, 3))
                post_norm(2 * l, MIX_BANKS)

            def dense():
                pre_norm(1)
                for ft in range(FT_DENSE):
                    dve.wait_ge(silu_d, ft + 1)
                    TT(AT[:, ft % 2, :], SA[:, ft % 2, :], bank[ft % 4][:, T:2 * T], ALU.mult).then_inc(act_d, 1)
                    if ft == 1:
                        scan_steps(1)
                    if ft == 3:
                        scan_phases(1)
                    if ft == 7:
                        scan_coefs(1)
                post_norm(1, (4, 5, 6, 7))

            def routing():
                dve.wait_ge(lg_ps, 1)
                link(nc.vector.tensor_copy(LG[:, :, :], bank[4][:, 0:TB * NE].rearrange("p (b e) -> p b e", b=TB)))
                for b in range(TB):
                    link(nc.vector.max(M8[:, b, :], LG[:, b, :]))
                    link(nc.vector.max_index(I8[:, b, :], M8[:, b, :], LG[:, b, :]))
                TT(GATE[:, :, 0:1], M8[:, :, 1:2], M8[:, :, 0:1], ALU.subtract).then_inc(gate_d, 1)
                link(nc.vector.tensor_copy(IF8[:, :, :], I8[:, :, :]))
                for c in range(2):
                    for b in range(TB):
                        link(TS(OH[:, c, b, :], iota[:, 0:NE], IF8[:, b, c:c + 1], None, ALU.is_equal))
                TT(SEL[:, :, :], OH[:, 0, :, :], OH[:, 1, :, :], ALU.add).then_inc(sel_done, 1)
                dve.wait_ge(gate_e, 1)
                link(TS(GATE[:, :, 2:3], GATE[:, :, 1:2], 1.0, None, ALU.add))
                link(nc.vector.reciprocal(GATE[:, :, 2:3], GATE[:, :, 2:3]))
                link(TT(GATE[:, :, 3:4], GATE[:, :, 1:2], GATE[:, :, 2:3], ALU.mult))
                for b in range(TB):
                    link(TS(CMB[:, b, 0:NE], OH[:, 0, b, :], GATE[:, b, 2:3], None, ALU.mult))
                    link(STT(CMB[:, b, 0:NE], OH[:, 1, b, :], GATE[:, b, 3:4], CMB[:, b, 0:NE], ALU.mult, ALU.add))
                dve.wait_ge(pos_ps, 1)
                dve.wait_ge(sel_done, 1)
                link(STT(POS[:, :, 0:NE], bank[5][:, 0:TB * NE].rearrange("p (b e) -> p b e", b=TB), 1.0, SEL[:, :, :],
                         ALU.add, ALU.mult))
                link(TS(POS[:, :, 0:NE], POS[:, :, 0:NE], -1.0, None, ALU.add))
                for p in range(1, PASSES + 1):
                    TS(POS[:, :, p * NE:(p + 1) * NE], POS[:, :, 0:NE], -float(p * CAP), None, ALU.add)
                    nc.vector.tensor_copy(CMB[:, :, p * NE:(p + 1) * NE], CMB[:, :, 0:NE])
                link(nc.vector.tensor_reduce(CNT[:, 0:1], bank[5][:, 2 * NE:3 * NE], AX, ALU.max))
                nc.vector.tensor_copy(OVER[:, :], CNT[:, 0:1]).then_inc(route_ok, 1)

            def one_hot(dst, i, weighted):
                for b in range(TB):
                    pos = POS[:, b, bass.ds(i, 1)]
                    if weighted:
                        t = TS(dst[:, b, :], slots, pos, CMB[:, b, bass.ds(i, 1)], ALU.is_equal, ALU.mult)
                    else:
                        t = TS(dst[:, b, :], slots, pos, None, ALU.is_equal)
                return t

            def gathered(i, h):
                gain = par(1, "g_ffn")
                src = bank[h][:, 0:4 * SLOTS].rearrange("p (k s) -> p k s", k=4)
                dve.wait_ge(ga_ps, i * 2 + (h + 1))
                TT(XGH[:, 4 * h:4 * h + 4, :], src, gain[:, 4 * h:4 * h + 4].unsqueeze(2).to_broadcast([P, 4, SLOTS]),
                   ALU.mult).then_inc(xgh_done, 1)
                dve.wait_ge(xgh_done, i * 2 + (h + 1))
                for k in range(4):
                    kt = 4 * h + k
                    t = STT(XGL[:, kt, :], src[:, k, :], gain[:, kt:kt + 1], XGH[:, kt, :].bitcast(F32),
                            ALU.mult, ALU.subtract)
                t.then_inc(xg_done, 1)

            def product(i, u):
                dve.wait_ge(silu_m, i * UNITS + (u + 1))
                TT(HM[:, :], SM[:, :], bank[u % 2][0:SLOTS, W_COLS:2 * W_COLS], ALU.mult).then_inc(h_done, 1)

            def activations(i, u):
                dve.wait_ge(t_ps, i * UNITS + (u + 1))
                src = bank[u % 2][:, 0:2 * SLOTS].rearrange("p (j s) -> p j s", j=2)
                nc.vector.tensor_copy(ATH[:, :, :], src).then_inc(ath_done, 1)
                dve.wait_ge(ath_done, i * UNITS + (u + 1))
                TT(ATL[:, :, :], src, ATH[:, :, :].bitcast(F32), ALU.subtract).then_inc(at_done, 1)

            def rest_part(i, m):
                dve.wait_ge(wh_done, i * MOE_SLABS + (m + 1))
                TT(WL[:, m % NSPLIT, :], RING[:, (BASE_MOE + m) % NSLOT, :], WH[:, m % NSPLIT, :].bitcast(F32),
                   ALU.subtract).then_inc(slabs_used, 1)

            def item(i, first=0):
                for m in range(MOE_SLABS):
                    if m >= first:
                        rest_part(i, m)
                    if m >= 3 and m % 3 == 0:
                        product(i, m // 3 - 1)
                    if m >= 4 and m % 3 == 1:
                        activations(i, (m - 4) // 3)
                    if m == 11:
                        one_hot(GM, i + 1, False).then_inc(g_done, 1)
                        one_hot(GW, i, True).then_inc(gw_done, 1)
                product(i, UNITS - 1)
                gathered(i + 1, 0)
                activations(i, UNITS - 1)
                dve.wait_ge(gt_ps, i + 1)
                nc.vector.tensor_copy(GT[:, :], bank[0][0:SLOTS, 0:T]).then_inc(gt_done, 1)
                dve.wait_ge(mm_used, i * MOE_SLABS + (MOE_SLABS + 2))
                nc.vector.tensor_copy(YE[:, 0:512], bank[2][0:SLOTS, :]).then_inc(y_v, 1)
                gathered(i + 1, 1)

            def experts():
                pre_norm(3)
                for m in range(NSPLIT):
                    rest_part(0, m)
                routing()
                dve.wait_ge(route_ok, 1)
                nc.vector.memset(GT[:, :], 0.0).then_inc(gt_done, 1)
                nc.vector.memset(YE[:, 0:512], 0.0).then_inc(y_v, 1)
                nc.vector.memset(YE[:, 512:D], 0.0).then_inc(y_a, 1)
                one_hot(GM, 0, False).then_inc(g_done, 1)
                gathered(0, 0)
                gathered(0, 1)
                item(0, NSPLIT)
                with dve.Fori(1, NE) as e:
                    item(e)
                dve.wait_ge(acc_ps, NE)
                over = dve.value_load(OVER[0:1, 0:1], min_val=0, max_val=T)
                with dve.If(over > CAP):
                    for p in range(1, PASSES):
                        with dve.Fori(0, NE) as e:
                            item(e + p * NE)
                    dve.wait_ge(acc_ps, PASSES * NE)
                post_norm(3, (4, 5, 6, 7))

            dve.wait_ge(vec_in, 16)
            dve.wait_ge(id_in, 16)
            scan_steps(0)
            scan_phases(0)
            mixer(0)
            dense()
            mixer(1)
            experts()


def shape_constants():
    c = np.zeros((P, NCONST), np.float32)
    c[:, C_ID:C_ID + P] = np.eye(P)
    c[:, C_MASK:C_MASK + P] = np.triu(np.full((P, P), NEG), 1)
    c[:, C_TRI:C_TRI + P] = np.triu(np.ones((P, P)), 1)
    c[:, C_ONES:C_ONES + P] = 1.0
    c[:, C_IOTA:C_IOTA + T] = np.arange(T)
    c[:, C_SLOT:C_SLOT + SLOTS] = np.where(np.arange(SLOTS) < CAP, np.arange(SLOTS), -9.0 * T)
    t = np.arange(T)
    for g, w in enumerate(WINDOWS):
        inside = (t[None, :] >= t[:, None]) & (t[None, :] - t[:, None] < w)
        a = inside / np.minimum(t + 1.0, w)[None, :] - np.eye(T)
        for n, (s, u) in enumerate(((0, 0), (0, 1), (1, 1))):
            at = C_BAND + (3 * g + n) * P
            c[:, at:at + P] = a[s * P:(s + 1) * P, u * P:(u + 1) * P]
    return c


def pack_params(a):
    out = np.zeros((P, LAYERS, NPAR), np.float32)
    for l in range(LAYERS):
        def put(name, v):
            lo, hi = _off[name]
            out[:v.shape[0], l, lo:hi] = v

        def columns(v):
            return v.reshape(-1, P).T

        put("g_mix", columns(a["norm_mix_pre"][l]))
        put("g_ffn", columns(a["norm_ffn_pre"][l]))
        put("g_br", columns(np.concatenate([a["branch_norm_attn"][l], a["branch_norm_pool"][l], a["branch_norm_ssm"][l]])))
        put("pool_scale", columns(a["pool_scale"][l]))
        put("ssm_d", columns(a["ssm_d"][l].reshape(-1)))
        put("b_glu", columns(a["ssm_b_glu"][l]))
        put("b_forget", a["b_forget"][l].reshape(HEADS, 1))
        put("a_re", columns(a["ssm_a_re"][l].reshape(-1)))
        put("a_im", columns(a["ssm_a_im"][l].reshape(-1)))
        put("log_dt", columns(np.repeat(a["ssm_log_dt"][l], 64)))
        put("w_f", a["w_in"][l][:, F_OFF:P_OFF].reshape(KT, P, HEADS).transpose(1, 0, 2).reshape(P, -1))
        put("router", a["moe_router"][l // 2].reshape(KT, P, NE).transpose(1, 0, 2).reshape(P, -1))
        for name, key in (("b_re", "ssm_b_re"), ("b_im", "ssm_b_im")):
            m = np.zeros((P, 2, P), np.float32)
            for g in range(16):
                j, o = g // 2, g % 2
                r = SCH * (j % 4) + 16 * o
                m[r:r + 16, j // 4, 64 * o:64 * o + 64] = a[key][l, g].T
            put(name, m.reshape(P, -1))
        for name, key in (("c_re", "ssm_c_re"), ("c_im", "ssm_c_im")):
            m = np.zeros((P, SJ, SCH), np.float32)
            for g in range(16):
                j, o = g // 2, g % 2
                m[64 * o:64 * o + 64, j, 16 * o:16 * o + 16] = a[key][l, g].T
            put(name, m.reshape(P, -1))
        m = np.zeros((P, 2, P), np.float32)
        for g in range(NG):
            o = GC * (g % 2)
            m[o:o + GC, g // 2, o:o + GC] = a["pool_w"][l, g]
        put("pool_w", m.reshape(P, -1))
        put("w_glu", a["ssm_w_glu"][l].reshape(2, P, T).transpose(1, 0, 2).reshape(P, -1))
    return out


def kernel(**inputs):
    from concourse import bacc
    from concourse.bass_utils import run_bass_kernel_spmd

    a = {k: np.asarray(v) for k, v in inputs.items()}
    post = np.stack([a["norm_mix_post"][0], a["norm_ffn_post"][0], a["norm_mix_post"][1], a["norm_ffn_post"][1]])
    arrays = {
        "x": a["x"][0], "w_in": a["w_in"], "w_out": a["w_out"],
        "ffn_gate": a["ffn_w_gate"][0], "ffn_up": a["ffn_w_up"][0], "ffn_down": a["ffn_w_down"][0],
        "moe_gate": a["moe_w_gate"][0], "moe_up": a["moe_w_up"][0], "moe_down": a["moe_w_down"][0],
        "g_post": np.broadcast_to(post[:, None, :], (4, P, D)),
        "params": pack_params(a), "consts": shape_constants(),
    }
    arrays = {k: np.ascontiguousarray(v) for k, v in arrays.items()}
    nc = bacc.Bacc("TRN2", target_bir_lowering=False, num_devices=1)
    args = [nc.dram_tensor(k, v.shape, F32, kind="ExternalInput").ap() for k, v in arrays.items()]
    args.append(nc.dram_tensor("c_scratch", (LAYERS, HEADS, 2, T), F32, kind="Internal").ap())
    out = nc.dram_tensor("out", (T, D), F32, kind="ExternalOutput").ap()
    build(nc, *args, out)
    r = run_bass_kernel_spmd(nc, [arrays], core_ids=[0])
    return r.results[0]["out"].reshape(1, T, D)
```

```python
import math
from contextlib import ExitStack

import numpy as np

import concourse.bass as bass
from concourse import mybir

P = 128
T = 256
TB = T // P
D = 1024
KT = D // P
LAYERS = 2
HEADS, DH = 8, 64
WINDOWS = (2, 4, 8, 16)
NG, GC = 4, 64
SJ = 8
SCH = 32
F_OFF, P_OFF, S_OFF = 1536, 1544, 1800
FFN = 2816
FT_DENSE = FFN // P
NE = 8
EDIM = 3584
FT_MOE = EDIM // P
SLOTS = 128
CAP = SLOTS
PASSES = -(-T // CAP)
EPS = 1e-6
NEG = -1e30
ROUND = 1.5 * 2.0 ** 23
TURN = 6.283185

SLAB = 2048
NSLOT = 7
W_COLS = 256
MIX_SLABS = 8 + 4
DENSE_UNITS = FT_DENSE // 2
DENSE_SLABS = 3 * DENSE_UNITS
UNITS = FT_MOE // 2
MOE_SLABS = 3 * UNITS
NSPLIT = 3
AHEAD = 2
BASE_MIX = (0, MIX_SLABS + DENSE_SLABS)
BASE_DENSE = MIX_SLABS
BASE_MOE = BASE_MIX[1] + MIX_SLABS
assert MOE_SLABS % NSLOT == 0 and MOE_SLABS % NSPLIT == 0 and DENSE_SLABS % NSPLIT == 0


def slab_order(units):
    seq = [("a", 0), ("b", 0)]
    for u in range(1, units):
        seq += [("a", u), ("b", u), ("d", u - 1)]
    return seq + [("d", units - 1)]


MOE_ORDER = slab_order(UNITS)
DENSE_ORDER = slab_order(DENSE_UNITS)
AT_SLAB = {key: m for m, key in enumerate(MOE_ORDER)}
AT_DENSE = {key: m for m, key in enumerate(DENSE_ORDER)}


_off = {}
_n = 0
for _name, _w in (("g_mix", KT), ("g_ffn", KT), ("g_br", KT), ("pool_scale", 2), ("ssm_d", 2),
                  ("b_glu", 2), ("b_forget", 1), ("a_re", SJ), ("a_im", SJ), ("log_dt", SJ),
                  ("w_f", KT * HEADS), ("router", KT * NE), ("b_re", 2 * P), ("b_im", 2 * P),
                  ("c_re", SJ * SCH), ("c_im", SJ * SCH), ("pool_w", 2 * P), ("w_glu", 2 * T)):
    _off[_name] = (_n, _n + _w)
    _n += _w
NPAR = _n
NVEC = _off["log_dt"][1]
C_ID, C_IOTA, C_MASK = 0, P, P + T
C_TRI, C_ONES, C_SLOT = C_MASK + P, C_MASK + 2 * P, C_MASK + 3 * P
C_BAND = C_SLOT + SLOTS
NCONST = C_BAND + NG * 3 * P

F32 = mybir.dt.float32
F32R = mybir.dt.float32r
I32 = mybir.dt.int32
U32 = mybir.dt.uint32
ALU = mybir.AluOpType
ACT = mybir.ActivationFunctionType
AX = mybir.AxisListType.X


def build(nc, x, w_in, w_out, ffn_gate, ffn_up, ffn_down, moe_gate, moe_up, moe_down, g_post, params, consts, c_dram, out):
    ctx = ExitStack()
    with ctx:
        def sb(name, shape, dt=F32):
            return ctx.enter_context(nc.sbuf_tensor(name, shape, dt))

        def sem(name):
            return ctx.enter_context(nc.semaphore(name))

        RING = sb("RING", [P, NSLOT, SLAB])
        X = sb("X", [P, TB, D])
        XN = sb("XN", [P, TB, D])
        HT = sb("HT", [P, KT, T])
        SQ = HT
        PAR = sb("PAR", [P, LAYERS, NPAR])
        CST = sb("CST", [P, NCONST])
        GB = sb("GB", [P, D])
        TMP = sb("TMP", [P, D])
        STAT = sb("STAT", [P, 8])
        RSTD = sb("RSTD", [P, 4])
        EXPO = sb("EXPO", [P, 1])
        LG = sb("LG", [P, TB, NE])
        M8 = sb("M8", [P, TB, 8])
        I8 = sb("I8", [P, TB, 8], U32)
        IF8 = sb("IF8", [P, TB, 8])
        OH = sb("OH", [P, 2, TB, NE])
        SEL = sb("SEL", [P, TB, NE])
        GATE = sb("GATE", [P, TB, 4])
        NI = PASSES * NE
        POS = sb("POS", [P, TB, NI])
        CMB = sb("CMB", [P, TB, NI])
        CNT = sb("CNT", [P, 4])
        OVER = sb("OVER", [P, 1], I32)

        TRIG = sb("TRIG", [P, 2, SJ, T])
        COS = TRIG[:, 0, :, :]
        SIN = TRIG[:, 1, :, :]
        CC = sb("CC", [P, 3, SJ, SCH])
        CT = sb("CT", [P, 2, SJ, SCH])
        SV = sb("SV", [P, 24, SJ])

        mix = ExitStack()

        def mb(name, shape, dt=F32):
            return mix.enter_context(nc.sbuf_tensor(name, shape, dt))

        QA = mb("QA", [DH + 2, HEADS, T])
        KA = mb("KA", [DH + 2, HEADS, T])
        V = mb("V", [P, TB, HEADS * DH])
        MT = mb("MT", [P, KT, T])
        SCR = mb("SCR", [P, 9, 2 * T])
        ROT = SCR[:, 0:2, :]
        ZIN = SCR[:, 2, :]
        Z = SCR[:, 3:5, :]
        ZC = SCR[:, 5:7, :]
        ZS = SCR[:, 7:9, :]
        P0 = SCR[:, 0:2, :].rearrange("p a (h k) -> p (a h) k", k=P)
        P1 = SCR[:, 2:6, :].rearrange("p a (h k) -> p (a h) k", k=T)
        UT = mb("UT", [P, 2, T])
        UP = mb("UP", [P, TB, T])
        DT = mb("DT", [P, 2, T])
        GY = mb("GY", [P, 2, T])
        SG = mb("SG", [P, 2, T])
        YS = mb("YS", [P, 2, T])
        PTS = mb("PTS", [P, 2, 3 * P])
        RB = mb("RB", [P, 3, T])
        FG = mb("FG", [HEADS, 6, T])
        MX = mb("MX", [P, 16])
        SUM = mb("SUM", [P, 16])
        RS = mb("RS", [P, 16])
        mix.close()

        WH = sb("WH", [P, NSPLIT, SLAB], F32R)
        WL = sb("WL", [P, NSPLIT, SLAB], F32R)

        ffn = ExitStack()

        def fb(name, shape, dt):
            return ffn.enter_context(nc.sbuf_tensor(name, shape, dt))

        HTH = fb("HTH", [P, KT, T], F32R)
        HTL = fb("HTL", [P, KT, T], F32R)
        DAH = fb("DAH", [P, 2, T], F32R)
        DAL = fb("DAL", [P, 2, T], F32R)
        SA = fb("SA", [P, 2, T], F32)
        ffn.close()

        XGH = sb("XGH", [P, KT, SLOTS], F32R)
        XGL = sb("XGL", [P, KT, SLOTS], F32R)
        ATH = sb("ATH", [P, 2, SLOTS], F32R)
        ATL = sb("ATL", [P, 2, SLOTS], F32R)
        SM = sb("SM", [SLOTS, W_COLS])
        HM = sb("HM", [SLOTS, W_COLS])
        GM = sb("GM", [P, TB, SLOTS])
        GW = sb("GW", [P, TB, SLOTS])
        GT = sb("GT", [SLOTS, T])
        YE = sb("YE", [SLOTS, D])

        bank = [ctx.enter_context(nc.psum_tensor(f"bank{i}", [P, 512], F32)) for i in range(8)]
        ident = CST[:, C_ID:C_ID + P]
        mask = CST[:, C_MASK:C_MASK + P]
        tri = CST[:, C_TRI:C_TRI + P]
        ones = CST[:, C_ONES:C_ONES + P]
        iota = CST[:, C_IOTA:C_IOTA + T]
        slots = CST[:, C_SLOT:C_SLOT + SLOTS]
        band = CST[:, C_BAND:NCONST].rearrange("p (g b t) -> p g b t", g=NG, b=3)

        SCORE_BANK = (0, 1, 2, 3, 0, 1)
        PT_BANK = (7, 4)
        MIX_BANKS = (0, 1, 4, 7)

        def par(l, name):
            a, b = _off[name]
            return PAR[:, l, a:b]

        x_in = [sem(f"x_in{b}") for b in range(TB)]
        vec_in = sem("vec_in")
        par_in = sem("par_in")
        id_in = sem("id_in")
        cst_in = sem("cst_in")
        gb_in = sem("gb_in")
        slab_in = [sem(f"slab_in{i}") for i in range(NSLOT)]
        slabs_used = sem("slabs_used")
        out_done = sem("out_done")
        sq_done = sem("sq_done")
        var_done = sem("var_done")
        rstd_done = sem("rstd_done")
        xn_done = sem("xn_done")
        ht_tr = sem("ht_tr")
        ht_v = sem("ht_v")
        ht_a = sem("ht_a")
        hth_done = sem("hth_done")
        htl_done = sem("htl_done")
        f_ps = sem("f_ps")
        ut_done = sem("ut_done")
        up_done = sem("up_done")
        qkv_done = sem("qkv_done")
        fz_a = sem("fz_a")
        fz_v = sem("fz_v")
        c_out = sem("c_out")
        c_rows = sem("c_rows")
        aug_ones = sem("aug_ones")
        expo_set = sem("expo_set")
        bu_done = sem("bu_done")
        rot_done = sem("rot_done")
        zin_done = sem("zin_done")
        z_done = sem("z_done")
        zr_done = sem("zr_done")
        y_done = sem("y_done")
        trig_v = sem("trig_v")
        trig_a = sem("trig_a")
        tab_ok = sem("tab_ok")
        dt_ps = sem("dt_ps")
        dt_done = sem("dt_done")
        pl_ps = sem("pl_ps")
        mt_pool = sem("mt_pool")
        ys_done = sem("ys_done")
        gy_done = sem("gy_done")
        glu_ps = sem("glu_ps")
        sg_done = sem("sg_done")
        mt_ssm = sem("mt_ssm")
        sc_ps = sem("sc_ps")
        msk_done = sem("msk_done")
        mx_done = sem("mx_done")
        ex_done = sem("ex_done")
        rs_done = sem("rs_done")
        pn_done = sem("pn_done")
        pt_ps = sem("pt_ps")
        pt_done = sem("pt_done")
        ot_ps = sem("ot_ps")
        ot_done = sem("ot_done")
        bsq = sem("bsq")
        bss_ps = sem("bss_ps")
        bvar = sem("bvar")
        brs = sem("brs")
        mtn = sem("mtn")
        mix_ps = sem("mix_ps")
        dh_done = sem("dh_done")
        dm_used = sem("dm_used")
        ffn_ps = sem("ffn_ps")
        silu_d = sem("silu_d")
        prod_d = sem("prod_d")
        dah_d = sem("dah_d")
        dal_d = sem("dal_d")
        post_tmp = sem("post_tmp")
        x_done = sem("x_done")
        lg_ps = sem("lg_ps")
        gate_d = sem("gate_d")
        gate_e = sem("gate_e")
        sel_done = sem("sel_done")
        pos_ps = sem("pos_ps")
        route_ok = sem("route_ok")
        g_done = sem("g_done")
        gw_done = sem("gw_done")
        ga_ps = sem("ga_ps")
        xgh_done = sem("xgh_done")
        xg_done = sem("xg_done")
        wh_done = sem("wh_done")
        mm_used = sem("mm_used")
        silu_m = sem("silu_m")
        h_done = sem("h_done")
        t_ps = sem("t_ps")
        ath_done = sem("ath_done")
        at_done = sem("at_done")
        gt_done = sem("gt_done")
        ye_done = sem("ye_done")
        acc_ps = sem("acc_ps")
        chain = sem("chain")

        block = ctx.enter_context(nc.Block())

        @block.sync
        def _(sp):
            def load(n, src, shape_of):
                slot = n % NSLOT
                if n >= NSLOT:
                    sp.wait_ge(slabs_used, n - NSLOT + 1)
                sp.dma_start(shape_of(slot), src).then_inc(slab_in[slot], 16)

            def cols(slot):
                return RING[:, slot, :].rearrange("p (k n) -> p k n", k=KT)

            def rows(slot):
                return RING[:, slot, :].rearrange("p (k n) -> p k n", k=2)

            def halves(slot):
                return RING[:, slot, :].rearrange("p (k c n) -> p k c n", k=4, c=2)

            w_in_v = w_in.rearrange("l (k p) n -> l p k n", p=P)
            w_out_v = w_out.rearrange("l (b k p) n -> l b p k n", p=P, k=2)
            gate_v = ffn_gate.rearrange("(k p) n -> p k n", p=P)
            up_v = ffn_up.rearrange("(k p) n -> p k n", p=P)
            down_v = ffn_down.rearrange("(u k p) n -> u p k n", p=P, k=2)
            mg_v = moe_gate.rearrange("e (h k p) n -> p e h k n", p=P, k=4)
            mu_v = moe_up.rearrange("e (h k p) n -> p e h k n", p=P, k=4)
            md_v = moe_down.rearrange("e (u k p) n -> p e u k n", p=P, k=2)

            sp.dma_start(PAR[:, :, 0:NVEC], params[:, :, 0:NVEC]).then_inc(vec_in, 16)
            sp.dma_start(CST[:, 0:C_MASK], consts[:, 0:C_MASK]).then_inc(id_in, 16)
            for n in range(TB):
                sp.dma_start(X[:, n, :], x[n * P:(n + 1) * P, :]).then_inc(x_in[n], 16)
            for l in range(LAYERS):
                b = BASE_MIX[l]
                for n, c in enumerate((S_OFF, P_OFF, 0, 256, 512, 768, 1024, 1280)):
                    load(b + n, w_in_v[l, :, :, c:c + W_COLS], cols)
                    if l == 0 and n == 1:
                        sp.dma_start(PAR[:, :, NVEC:NPAR], params[:, :, NVEC:NPAR]).then_inc(par_in, 16)
                        sp.dma_start(CST[:, C_MASK:NCONST], consts[:, C_MASK:NCONST]).then_inc(cst_in, 16)
                for n, r in enumerate((2, 3, 0, 1)):
                    load(b + 8 + n, w_out_v[l, r, :, :, :], rows)
                if l == 0:
                    for m, (kind, u) in enumerate(DENSE_ORDER):
                        if kind == "d":
                            load(BASE_DENSE + m, down_v[u, :, :, :], rows)
                        else:
                            src = gate_v if kind == "a" else up_v
                            load(BASE_DENSE + m, src[:, :, u * W_COLS:(u + 1) * W_COLS], cols)

            def load_expert(i, e):
                for m, (kind, u) in enumerate(MOE_ORDER):
                    slot = (BASE_MOE + m) % NSLOT
                    sp.wait_ge(slabs_used, i * MOE_SLABS + (BASE_MOE + m - NSLOT + 1))
                    for c in range(2):
                        if kind == "d":
                            src = md_v[:, bass.ds(e, 1), u, c, :]
                            dst = rows(slot)[:, c, :]
                        else:
                            src = (mg_v, mu_v)[c][:, bass.ds(e, 1), "ab".index(kind), :, u * W_COLS:(u + 1) * W_COLS]
                            dst = halves(slot)[:, :, c, :]
                        sp.dma_start(dst.unsqueeze(1), src).then_inc(slab_in[slot], 16)

            with sp.Fori(0, NE) as e:
                load_expert(e, e)
            sp.wait_ge(route_ok, 1)
            over = sp.value_load(OVER[0:1, 0:1], min_val=0, max_val=T)
            with sp.If(over > CAP):
                for p in range(1, PASSES):
                    with sp.Fori(0, NE) as e:
                        load_expert(e + p * NE, e)
            for b in range(TB):
                sp.wait_ge(x_done, 12 + 2 * (b + 1))
                sp.dma_start(out[b * P:(b + 1) * P, :], X[:, b, :]).then_inc(out_done, 16)
            sp.wait_ge(out_done, 16 * TB)

        def arrived(eng, n):
            eng.wait_ge(slab_in[n % NSLOT], 16 * (n // NSLOT + 1))

        def moe_arrived(eng, i, m):
            slot = (BASE_MOE + m) % NSLOT
            before = len(range(slot, BASE_MOE, NSLOT))
            eng.wait_ge(slab_in[slot], i * (32 * MOE_SLABS // NSLOT) + (16 * before + 32 * (m // NSLOT + 1)))

        boundary = [[(post, i + (not post), b) for post, b in
                     (((True, 0), (True, 1), (False, 0), (False, 1)) if i == 1 else
                      ((True, 0), (False, 0), (True, 1), (False, 1)))] for i in range(3)]
        norm_order = [(False, 0, 0), (False, 0, 1)] + sum(boundary, []) + [(True, 3, 0), (True, 3, 1)]

        def norm_count(post, i, b):
            return norm_order.index((post, i, b)) + 1

        def ht_before(i):
            return i - (i > 1)

        @block.tensor
        def _(pe):
            def norm_transpose(i):
                for b in range(TB):
                    pe.wait_ge(xn_done, TB * i + b + 1)
                    for k in range(KT):
                        at = (k % 2) * T + b * P
                        t = nc.tensor.transpose(bank[k // 2][:, at:at + P], XN[:, b, k * P:(k + 1) * P], ident)
                        if b == TB - 1 and k % 2:
                            t.then_inc(ht_tr, 1)

            def ht_ready(i, k):
                pe.wait_ge(ht_a if k % 4 >= 2 else ht_v, 4 * ht_before(i) + 2 * (k // 4) + k % 2 + 1)

            def tile_of(slot, m, dst, norm=None):
                w = RING[:, slot, :].rearrange("p (k n) -> p k n", k=KT)
                for k in range(KT):
                    if norm is not None:
                        ht_ready(norm, k)
                    t = nc.tensor.matmul(dst, w[:, k, m * P:(m + 1) * P], HT[:, k, :], start=k == 0, stop=k == KT - 1)
                return t

            def rows_of(slot, b, dst):
                w = RING[:, slot, :].rearrange("p (k n) -> p k n", k=KT)
                for k in range(KT):
                    t = nc.tensor.matmul(dst, HT[:, k, b * P:(b + 1) * P], w[:, k, :], start=k == 0, stop=k == KT - 1)
                return t

            def mixer(l):
                base = BASE_MIX[l]
                norm_transpose(2 * l)

                arrived(pe, base)
                for m in range(2):
                    t = tile_of(base % NSLOT, m, bank[4][:, m * T:(m + 1) * T], None if m else 2 * l)
                t.then_inc(slabs_used, 1)
                arrived(pe, base + 1)
                for b in range(TB):
                    t = rows_of((base + 1) % NSLOT, b, bank[5][:, b * T:(b + 1) * T])
                t.then_inc(slabs_used, 1)
                if l == 0:
                    pe.wait_ge(par_in, 16)
                    pe.wait_ge(cst_in, 16)
                wf = par(l, "w_f").rearrange("p (k h) -> p k h", k=KT)
                for k in range(KT):
                    t = nc.tensor.matmul(bank[6][0:HEADS, 0:T], wf[:, k, :], HT[:, k, :], start=k == 0, stop=k == KT - 1)
                t.then_inc(f_ps, 1)

                def scan_in(j):
                    if j == 0:
                        pe.wait_ge(ut_done, l + 1)
                        pe.wait_ge(up_done, l + 1)
                    if j >= 2:
                        pe.wait_ge(rot_done, 8 * l + j - 1)
                    r = SCH * (j % 4)
                    for c, name in enumerate(("b_re", "b_im")):
                        w = par(l, name)[r:r + SCH, (j // 4) * P:(j // 4 + 1) * P]
                        t = nc.tensor.matmul(bank[4 + j % 2][:, c * T:(c + 1) * T], w, UT[r:r + SCH, j // 4, :],
                                             start=True, stop=True)
                    t.then_inc(bu_done, 1)

                def scan_out(j):
                    if j == 0:
                        pe.wait_ge(tab_ok, l + 1)
                    pe.wait_ge(zr_done, 8 * l + j + 1)
                    if j == 0:
                        pe.wait_ge(fz_a, 3 * l + 3)
                        pe.wait_ge(fz_v, 4 * l + 1)
                    r = SCH * (j % 4)
                    dst = bank[6][r:r + SCH, (j // 4) * T:(j // 4 + 1) * T]
                    parts = ((0, ZC[:, j % 2, 0:T]), (1, ZS[:, j % 2, T:2 * T]),
                             (2, ZS[:, j % 2, 0:T]), (2, ZC[:, j % 2, T:2 * T]))
                    for n, (c, z) in enumerate(parts):
                        t = nc.tensor.matmul(dst, CC[:, c, j, :], z, start=n == 0, stop=n == 3)
                    t.then_inc(y_done, 1)

                def feature_tile(n):
                    s = base + 2 + n // 2
                    arrived(pe, s)
                    t = tile_of(s % NSLOT, n % 2, bank[n // 2][:, (n % 2) * T:(n % 2 + 1) * T])
                    if n % 2:
                        t.then_inc(slabs_used, 1)

                def value_slab(s):
                    n = base + 6 + s
                    arrived(pe, n)
                    if s == 0:
                        pe.wait_ge(mt_pool, l + 1)
                    for b in range(TB):
                        if s == 0 and b == 1:
                            pe.wait_ge(rot_done, 8 * l + 7)
                        t = rows_of(n % NSLOT, b, bank[7 if b == 0 else 4][:, s * T:(s + 1) * T])
                    t.then_inc(slabs_used, 1)

                def pool_band():
                    for g in range(NG):
                        r = (g % 2) * GC
                        dst = bank[7][r:r + GC, (g // 2) * T:(g // 2 + 1) * T]
                        nc.tensor.matmul(dst, UP[:, 0, g * GC:(g + 1) * GC], band[:, g, 0:2, :],
                                         start=True, stop=False)
                        t = nc.tensor.matmul(dst[:, P:T], UP[:, 1, g * GC:(g + 1) * GC], band[:, g, 2, :],
                                             start=False, stop=True)
                    t.then_inc(dt_ps, 1)

                def pool_mix():
                    pe.wait_ge(dt_done, l + 1)
                    w = par(l, "pool_w").rearrange("p (a n) -> p a n", a=2)
                    for a in range(2):
                        t = nc.tensor.matmul(bank[7][:, a * T:(a + 1) * T], w[:, a, :], DT[:, a, :], start=True, stop=True)
                    t.then_inc(pl_ps, 1)

                scan_in(0)
                scan_in(1)
                feature_tile(0)
                pool_band()
                scan_in(2)
                feature_tile(1)
                scan_in(3)
                pool_mix()
                feature_tile(2)
                scan_in(4)
                feature_tile(3)
                scan_out(0)
                scan_in(5)
                scan_out(1)
                feature_tile(4)
                scan_in(6)
                scan_out(2)
                feature_tile(5)
                scan_in(7)
                scan_out(3)
                feature_tile(6)
                scan_out(4)
                feature_tile(7)
                scan_out(5)
                value_slab(0)

                def scores(n):
                    pe.wait_ge(qkv_done, 6 * l + 4)
                    pe.wait_ge(c_rows, 32 * (l + 1))
                    pe.wait_ge(aug_ones, 2 * (l + 1))
                    if n >= 4:
                        pe.wait_ge(ex_done, 6 * l + n - 3)
                    heads, width = (4, P) if n < 2 else (2, T)
                    h0 = 4 * n if n < 2 else 2 * (n - 2)
                    q = QA[:, :, 0:P] if n < 2 else QA[:, :, P:T]
                    for h in range(heads):
                        t = nc.tensor.matmul(bank[SCORE_BANK[n]][:, h * width:(h + 1) * width], q[:, h0 + h, :],
                                             KA[:, h0 + h, 0:width], start=True, stop=True)
                    t.then_inc(sc_ps, 1)

                for n in range(4):
                    scores(n)
                scan_out(6)
                value_slab(1)
                scan_out(7)
                for n in (4, 5):
                    scores(n)

                pe.wait_ge(gy_done, l + 1)
                w = par(l, "w_glu").rearrange("p (a n) -> p a n", a=2)
                for m in range(2):
                    for k in range(2):
                        t = nc.tensor.matmul(bank[5][:, m * T:(m + 1) * T], w[:, k, m * P:(m + 1) * P], GY[:, k, :],
                                             start=k == 0, stop=k == 1)
                t.then_inc(glu_ps, 1)

                def branch_sum(n, tiles, dst):
                    pe.wait_ge(bsq, 3 * l + n + 1)
                    if n == 1:
                        pe.wait_ge(bvar, 3 * l + 1)
                    for i, k in enumerate(tiles):
                        t = nc.tensor.matmul(dst, ones, SQ[:, k, :], start=i == 0, stop=i == len(tiles) - 1)
                    t.then_inc(bss_ps, 1)

                def head_out(h):
                    pe.wait_ge(pt_done, 8 * l + h + 1)
                    r = (h % 2) * DH
                    dst = bank[2 + h // 4][r:r + DH, (h // 2 % 2) * T:(h // 2 % 2 + 1) * T]
                    nc.tensor.matmul(dst, V[:, 0, h * DH:(h + 1) * DH], PTS[:, h % 2, 0:T], start=True, stop=False)
                    t = nc.tensor.matmul(dst[:, P:T], V[:, 1, h * DH:(h + 1) * DH], PTS[:, h % 2, T:3 * P], start=False,
                                         stop=True)
                    if h % 4 == 3:
                        t.then_inc(ot_ps, 1)

                for h in range(HEADS):
                    pe.wait_ge(pn_done, 6 * l + 3 + h // 2)
                    if h >= 2:
                        pe.wait_ge(pt_done, 8 * l + h - 1)
                    if h == 0:
                        pe.wait_ge(qkv_done, 6 * l + 6)
                    dst = bank[PT_BANK[h % 2]]
                    nc.tensor.transpose(dst[:, 0:P], P0[:, h, :], ident)
                    nc.tensor.transpose(dst[:, P:2 * P], P1[:, h, 0:P], ident)
                    nc.tensor.transpose(dst[:, 2 * P:3 * P], P1[:, h, P:T], ident).then_inc(pt_ps, 1)
                    if h == 2:
                        branch_sum(0, (4, 5), bank[6][:, 0:T])
                    if h == 5:
                        branch_sum(1, (6, 7), bank[6][:, T:2 * T])
                    if h >= 1:
                        head_out(h - 1)
                head_out(HEADS - 1)

                def project(b, slabs):
                    for s in slabs:
                        n = base + 8 + s
                        arrived(pe, n)
                        w = RING[:, n % NSLOT, :].rearrange("p (k n) -> p k n", k=2)
                        for k in range(2):
                            kt = (4, 6, 0, 2)[s] + k
                            pe.wait_ge(mtn, 8 * l + (0, 2, 4, 6)[s] + k + 1)
                            for c in range(2):
                                t = nc.tensor.matmul(bank[MIX_BANKS[2 * b + c]][:, :], MT[:, kt, b * P:(b + 1) * P],
                                                     w[:, k, c * 512:(c + 1) * 512], start=s == 0 and k == 0,
                                                     stop=s == 3 and k == 1)
                        if b == 1:
                            t.then_inc(slabs_used, 1)
                    return t

                project(0, (0, 1))
                branch_sum(2, (0, 1, 2, 3), bank[5][:, 0:T])
                project(1, (0, 1))
                project(0, (2, 3)).then_inc(mix_ps, 1)
                project(1, (2, 3))

            def dense():
                norm_transpose(1)
                for m, (kind, u) in enumerate(DENSE_ORDER):
                    pe.wait_ge(slabs_used, BASE_DENSE + m + 1)
                    hi, lo = WH[:, m % NSPLIT, :], WL[:, m % NSPLIT, :]
                    if kind == "d":
                        pe.wait_ge(dal_d, u + 1)
                        wh = hi.rearrange("p (j n) -> p j n", j=2)
                        wl = lo.rearrange("p (j n) -> p j n", j=2)
                        for b in range(TB):
                            for j in range(2):
                                for n, (x_, w_) in enumerate(((DAH, wh), (DAH, wl), (DAL, wh))):
                                    for c in range(2):
                                        t = nc.tensor.matmul(bank[4 + 2 * b + c][:, :], x_[:, j, b * P:(b + 1) * P],
                                                             w_[:, j, c * 512:(c + 1) * 512],
                                                             start=u == 0 and j == 0 and n == 0,
                                                             stop=u == DENSE_UNITS - 1 and j == 1 and n == 2)
                            if u == DENSE_UNITS - 1:
                                t.then_inc(ffn_ps, 1)
                        if u < DENSE_UNITS - 1:
                            t.then_inc(dm_used, 1)
                        continue
                    wh = hi.rearrange("p (k n) -> p k n", k=KT)
                    wl = lo.rearrange("p (k n) -> p k n", k=KT)
                    c = "ab".index(kind)
                    for j in range(2):
                        dst = bank[2 * (u % 2) + j][:, c * T:(c + 1) * T]
                        for k in range(KT):
                            if m == 0 and j == 0:
                                pe.wait_ge(htl_done, k // 2 + 1)
                            for n, (w_, x_) in enumerate(((wh, HTH), (wh, HTL), (wl, HTH))):
                                t = nc.tensor.matmul(dst, w_[:, k, j * P:(j + 1) * P], x_[:, k, :],
                                                     start=k == 0 and n == 0, stop=k == KT - 1 and n == 2)
                    t.then_inc(dm_used, 1)

            def routing():
                rt = par(1, "router").rearrange("p (k e) -> p k e", k=KT)
                for b in range(TB):
                    for k in range(KT):
                        if b == 0:
                            ht_ready(3, k)
                            if k == 0:
                                ht_ready(3, 1)
                        t = nc.tensor.matmul(bank[0][:, b * NE:(b + 1) * NE], HT[:, k, b * P:(b + 1) * P], rt[:, k, :],
                                             start=k == 0, stop=k == KT - 1)
                t.then_inc(lg_ps, 1)
                gt_waits(0)
                ye_waits(0)
                for c in range(4):
                    t = nc.tensor.matmul(bank[4 + c][:, :], GT[:, 0:P], YE[:, 0:512], start=True, stop=False,
                                         skip_group_check=True)
                    if c < 2:
                        t.then_inc(mm_used, 1)
                pe.wait_ge(sel_done, 1)
                dst = bank[3]
                nc.tensor.matmul(dst[:, 0:NE], tri, SEL[:, 0, :], start=True, stop=True)
                nc.tensor.matmul(dst[:, NE:2 * NE], ones, SEL[:, 0, :], start=True, stop=False)
                nc.tensor.matmul(dst[:, NE:2 * NE], tri, SEL[:, 1, :], start=False, stop=True)
                nc.tensor.matmul(dst[:, 2 * NE:3 * NE], ones, SEL[:, 0, :], start=True, stop=False)
                nc.tensor.matmul(dst[:, 2 * NE:3 * NE], ones, SEL[:, 1, :], start=False, stop=True).then_inc(pos_ps, 1)

            def gather(i, h):
                pe.wait_ge(g_done, i + 1)
                for k in range(4):
                    for b in range(TB):
                        t = nc.tensor.matmul(bank[h][:, k * SLOTS:(k + 1) * SLOTS],
                                             XN[:, b, (4 * h + k) * P:(4 * h + k + 1) * P], GM[:, b, :],
                                             start=b == 0, stop=b == TB - 1)
                t.then_inc(ga_ps, 1)

            def gt_waits(i):
                pe.wait_ge(gt_done, i + 1)

            def ye_waits(i):
                pe.wait_ge(ye_done, i + 1)

            def item(i, ahead):
                for m, (kind, u) in enumerate(MOE_ORDER):
                    if m < 2:
                        pe.wait_ge(xg_done, i * 2 + (m + 1))
                    if m == MOE_SLABS - 1:
                        transpose_unit(i, UNITS - 1)
                        if ahead:
                            gather(i + 1, 0)
                    pe.wait_ge(slabs_used, i * MOE_SLABS + (BASE_MOE + m + 1))
                    hi, lo = WH[:, m % NSPLIT, :], WL[:, m % NSPLIT, :]
                    if kind == "d":
                        pe.wait_ge(at_done, i * UNITS + (u + 1))
                        wh = hi.rearrange("p (j c n) -> p j c n", j=2, c=2)
                        wl = lo.rearrange("p (j c n) -> p j c n", j=2, c=2)
                        for j in range(2):
                            for n, (x_, w_) in enumerate(((ATH, wh), (ATH, wl), (ATL, wh))):
                                for c in range(2):
                                    t = nc.tensor.matmul(bank[2 + c][0:SLOTS, :], x_[:, j, :], w_[:, j, c, :],
                                                         start=u == 0 and j == 0 and n == 0,
                                                         stop=u == UNITS - 1 and j == 1 and n == 2)
                    else:
                        if kind == "a" and u >= 2:
                            pe.wait_ge(at_done, i * UNITS + (u - 1))
                        wh = hi.rearrange("p (k n) -> p k n", k=4)
                        wl = lo.rearrange("p (k n) -> p k n", k=4)
                        for k in range(4):
                            kt = 4 * "ab".index(kind) + k
                            for n, (x_, w_) in enumerate(((XGH, wh), (XGH, wl), (XGL, wh))):
                                t = nc.tensor.matmul(bank[u % 2][0:SLOTS, :], x_[:, kt, :], w_[:, k, :],
                                                     start=kt == 0 and n == 0, stop=kt == KT - 1 and n == 2)
                    t.then_inc(mm_used, 1)
                    if kind == "a" and u >= 1:
                        transpose_unit(i, u - 1)
                gt_waits(i + 1)
                if ahead:
                    gather(i + 1, 1)
                ye_waits(i + 1)
                for b in range(TB):
                    for c in range(2):
                        t = nc.tensor.matmul(bank[4 + 2 * b + c][:, :], GT[:, b * P:(b + 1) * P],
                                             YE[:, c * 512:(c + 1) * 512], start=False, stop=False, skip_group_check=True)
                    t.then_inc(acc_ps, 1)

            def transpose_unit(i, u):
                pe.wait_ge(h_done, i * UNITS + (u + 1))
                for j in range(2):
                    t = nc.tensor.transpose(bank[u % 2][:, j * SLOTS:(j + 1) * SLOTS], HM[:, j * P:(j + 1) * P],
                                            ident[0:SLOTS, 0:SLOTS])
                if u == UNITS - 1:
                    pe.wait_ge(gw_done, i + 1)
                    for b in range(TB):
                        t = nc.tensor.transpose(bank[u % 2][0:SLOTS, T + b * P:T + (b + 1) * P], GW[:, b, :], ident)
                t.then_inc(t_ps, 1)

            def experts():
                norm_transpose(3)
                routing()
                gather(0, 0)
                gather(0, 1)
                with pe.Fori(0, NE - 1) as e:
                    item(e, True)
                item(NE - 1, False)
                pe.wait_ge(route_ok, 1)
                over = pe.value_load(OVER[0:1, 0:1], min_val=0, max_val=T)
                with pe.If(over > CAP):
                    for p in range(1, PASSES):
                        gather(p * NE, 0)
                        gather(p * NE, 1)
                        with pe.Fori(0, NE - 1) as e:
                            item(e + p * NE, True)
                        item(p * NE + NE - 1, False)

            pe.wait_ge(id_in, 16)
            mixer(0)
            dense()
            mixer(1)
            experts()

        @block.scalar
        def _(act):
            def sumsq(b, sources):
                for h, (src, dst) in enumerate(sources):
                    t = nc.scalar.activation(dst, src, ACT.Square, accum_out=STAT[:, 2 * b + h:2 * b + h + 1])
                t.then_inc(sq_done, 1)

            def square_x(i, b):
                if i == 0:
                    act.wait_ge(x_in[b], 16)
                else:
                    act.wait_ge(x_done, 4 * (i - 1) + 2 * b + 2)
                    act.wait_ge(rstd_done, norm_count(True, i - 1, b))
                sumsq(b, [(X[:, b, :], XN[:, b, :])])

            def square_out(i, banks, b, ready):
                act.wait_ge(*ready)
                act.wait_ge(rstd_done, norm_count(False, i, b))
                sumsq(b, [(bank[banks[2 * b + h]][:, :], XN[:, b, h * 512:(h + 1) * 512]) for h in range(2)])

            def load_gain(i):
                if i:
                    act.wait_ge(x_done, 4 * i)
                act.dma_start(GB[:, :], g_post[i, :, :]).then_inc(gb_in, 16)

            def between(i, banks, ready, meanwhile=None):
                load_gain(i)
                for post, _, b in boundary[i]:
                    if post:
                        square_out(i, banks, b, ready[b])
                    else:
                        if b and meanwhile:
                            meanwhile()
                        square_x(i + 1, b)

            def tiles(i):
                gain = par(i // 2, "g_ffn" if i % 2 else "g_mix")
                for k in (2, 3, 6, 7):
                    act.wait_ge(ht_tr, 4 * i + k // 2 + 1)
                    nc.scalar.activation(HT[:, k, :], bank[k // 2][:, (k % 2) * T:(k % 2 + 1) * T], ACT.Identity,
                                         scale=gain[:, k:k + 1]).then_inc(ht_a, 1)

            def scan_tables(l, part):
                if part == 0:
                    if l:
                        act.wait_ge(tab_ok, l)
                    nc.scalar.activation(SV[:, 0, :], par(l, "log_dt"), ACT.Tanh, scale=1.0 / 16.0).then_inc(trig_a, 1)
                    return
                if part == 1:
                    act.wait_ge(trig_v, 2 * l + 1)
                    nc.scalar.activation(SV[:, 6, :], SV[:, 5, :], ACT.Tanh, scale=0.5).then_inc(trig_a, 1)
                    return
                act.wait_ge(trig_v, 2 * l + 2)
                if part == 2:
                    for h in range(2):
                        t = nc.scalar.activation(COS[:, 4 * h:4 * h + 4, :], SIN[:, 4 * h:4 * h + 4, :], ACT.Sin,
                                                 scale=TURN / 2)
                    t.then_inc(trig_a, 1)
                    return
                for h in range(2):
                    t = nc.scalar.activation(SIN[:, 4 * h:4 * h + 4, :], SIN[:, 4 * h:4 * h + 4, :], ACT.Sin, scale=TURN)
                t.then_inc(trig_a, 1)

            def heads_out(dst, src, scale):
                for o in range(2):
                    t = nc.scalar.activation(dst[:, :, o, :], src[o * DH:(o + 1) * DH, :].rearrange("p (m t) -> p m t", m=2),
                                             ACT.Copy, scale=scale)
                return t

            def high(m):
                arrived(act, BASE_DENSE + m)
                if m >= NSPLIT:
                    act.wait_ge(dm_used, m - NSPLIT + 1)
                nc.scalar.copy(WH[:, m % NSPLIT, :], RING[:, (BASE_DENSE + m) % NSLOT, :]).then_inc(dh_done, 1)

            def mixer(l):
                base = BASE_MIX[l]
                if l == 0:
                    square_x(0, 0)
                    square_x(0, 1)
                tiles(2 * l)
                if l == 0:
                    scan_tables(0, 2)
                    scan_tables(0, 3)
                act.wait_ge(slabs_used, base + 1)
                nc.scalar.copy(UT[:, :, :], bank[4][:, :].rearrange("p (a t) -> p a t", a=2)).then_inc(ut_done, 1)
                act.wait_ge(slabs_used, base + 2)
                nc.scalar.copy(UP[:, :, :], bank[5][:, :].rearrange("p (a t) -> p a t", a=2)).then_inc(up_done, 1)
                act.wait_ge(f_ps, l + 1)
                nc.scalar.activation(FG[:, 0, :], bank[6][0:HEADS, 0:T], ACT.Abs, bias=par(l, "b_forget")[0:HEADS, :])\
                    .then_inc(fz_a, 1)
                act.wait_ge(fz_a, 3 * l + 1)
                nc.scalar.activation(FG[:, 1, :], FG[:, 0, :], ACT.Exp, scale=-1.0).then_inc(fz_a, 1)
                act.wait_ge(fz_a, 3 * l + 2)
                nc.scalar.activation(FG[:, 2, :], FG[:, 1, :], ACT.Ln, bias=1.0).then_inc(fz_a, 1)
                act.wait_ge(dt_ps, l + 1)
                nc.scalar.copy(DT[:, :, :], bank[7][:, :].rearrange("p (a t) -> p a t", a=2)).then_inc(dt_done, 1)
                qa = QA[0:DH, :, :].rearrange("p (b m o) t -> p b m o t", b=2, m=2)
                ka = KA[0:DH, :, :].rearrange("p (b m o) t -> p b m o t", b=2, m=2)
                act.wait_ge(slabs_used, base + 3)
                heads_out(qa[:, 0, :, :, :], bank[0], DH ** -0.5).then_inc(qkv_done, 1)
                act.wait_ge(pl_ps, l + 1)
                ps = par(l, "pool_scale")
                for a in range(2):
                    t = nc.scalar.activation(MT[:, 4 + a, :], bank[7][:, a * T:(a + 1) * T], ACT.Identity, scale=ps[:, a:a + 1])
                t.then_inc(mt_pool, 1)
                act.wait_ge(slabs_used, base + 4)
                heads_out(qa[:, 1, :, :, :], bank[1], DH ** -0.5).then_inc(qkv_done, 1)
                for n in range(2):
                    act.wait_ge(slabs_used, base + 5 + n)
                    heads_out(ka[:, n, :, :, :], bank[2 + n], 1.0).then_inc(qkv_done, 1)
                def numerators(n):
                    act.wait_ge(mx_done, 6 * l + n + 1)
                    if n == 2:
                        act.wait_ge(zr_done, 8 * l + 8)
                    heads, width = (4, P) if n < 2 else (2, T)
                    at = 4 * n if n < 2 else 8 + 2 * (n - 2)
                    for h in range(heads):
                        dst = P0[:, at + h, :] if n < 2 else P1[:, at + h - 8, :]
                        t = nc.scalar.activation(dst, bank[SCORE_BANK[n]][:, h * width:(h + 1) * width], ACT.Exp,
                                                 bias=MX[:, at + h:at + h + 1], accum_out=SUM[:, at + h:at + h + 1])
                    t.then_inc(ex_done, 1)

                for n in range(4):
                    numerators(n)
                for n, bk in enumerate((7, 4)):
                    act.wait_ge(slabs_used, base + 8)
                    nc.scalar.copy(V[:, n, :], bank[bk][:, :]).then_inc(qkv_done, 1)
                nc.scalar.activation(SQ[:, 4:6, :], MT[:, 4:6, :], ACT.Square).then_inc(bsq, 1)
                act.wait_ge(ys_done, l + 1)
                nc.scalar.activation(GY[:, :, :], YS[:, :, :], ACT.Gelu_apprx_tanh).then_inc(gy_done, 1)
                for n in (4, 5):
                    numerators(n)
                def gate():
                    act.wait_ge(glu_ps, l + 1)
                    bg = par(l, "b_glu")
                    for m in range(2):
                        t = nc.scalar.activation(SG[:, m, :], bank[5][:, m * T:(m + 1) * T], ACT.Sigmoid, bias=bg[:, m:m + 1])
                    t.then_inc(sg_done, 1)

                def branch_rstd(n):
                    act.wait_ge(bvar, 3 * l + n + 1)
                    nc.scalar.activation(RB[:, n, :], RB[:, n, :], ACT.Sqrt).then_inc(brs, 1)

                for h in range(HEADS):
                    if h in (4, 7):
                        branch_rstd((h - 4) // 3)
                    act.wait_ge(pt_ps, 8 * l + h + 1)
                    nc.scalar.copy(PTS[:, h % 2, :], bank[PT_BANK[h % 2]][:, 0:3 * P]).then_inc(pt_done, 1)
                    if h == 1:
                        gate()
                    if h == 3:
                        act.wait_ge(mt_ssm, l + 1)
                        nc.scalar.activation(SQ[:, 6:8, :], MT[:, 6:8, :], ACT.Square).then_inc(bsq, 1)
                for m in range(2):
                    act.wait_ge(ot_done, 2 * l + m + 1)
                    t = nc.scalar.activation(SQ[:, 2 * m:2 * m + 2, :], MT[:, 2 * m:2 * m + 2, :], ACT.Square)
                t.then_inc(bsq, 1)
                branch_rstd(2)
                between(2 * l, MIX_BANKS, ((mix_ps, l + 1), (slabs_used, base + 12)), None if l else lambda: high(0))

            def dense():
                def silu_unit(u):
                    act.wait_ge(dm_used, AT_DENSE["b", u] + 1)
                    if u:
                        act.wait_ge(dal_d, u)
                    for j in range(2):
                        t = nc.scalar.activation(SA[:, j, :], bank[2 * (u % 2) + j][:, 0:T], ACT.Silu)
                    t.then_inc(silu_d, 1)

                high(1)
                gain = par(0, "g_ffn")
                for k in range(KT):
                    act.wait_ge(ht_tr, 4 + k // 2 + 1)
                    t = nc.scalar.activation(HTH[:, k, :], bank[k // 2][:, (k % 2) * T:(k % 2 + 1) * T], ACT.Identity,
                                             scale=gain[:, k:k + 1])
                    if k % 2:
                        t.then_inc(hth_done, 1)
                for m in range(2, DENSE_SLABS):
                    high(m)
                    if m >= 3 and m % 3 == 0:
                        silu_unit(m // 3 - 1)
                    if m == 5:
                        scan_tables(1, 0)
                    if m == 8:
                        scan_tables(1, 1)
                    if m in (14, 17):
                        scan_tables(1, 2 + (m == 17))
                silu_unit(DENSE_UNITS - 1)
                between(1, (4, 5, 6, 7), ((ffn_ps, 1), (ffn_ps, 2)))

            def silu(i, u):
                act.wait_ge(mm_used, i * MOE_SLABS + (AT_SLAB["b", u] + 3))
                nc.scalar.activation(SM[:, :], bank[u % 2][0:SLOTS, 0:W_COLS], ACT.Silu).then_inc(silu_m, 1)

            def high_part(i, m):
                moe_arrived(act, i, m)
                nc.scalar.copy(WH[:, m % NSPLIT, :], RING[:, (BASE_MOE + m) % NSLOT, :]).then_inc(wh_done, 1)

            def item(i, first, ahead):
                for m in range(first, MOE_SLABS):
                    act.wait_ge(mm_used, i * MOE_SLABS + m)
                    high_part(i, m)
                    if m >= 3 and m % 3 == 0:
                        silu(i, m // 3 - 1)
                silu(i, UNITS - 1)
                for m in range(AHEAD if ahead else 0):
                    act.wait_ge(mm_used, i * MOE_SLABS + (MOE_SLABS + m))
                    high_part(i + 1, m)
                act.wait_ge(mm_used, i * MOE_SLABS + (MOE_SLABS + 2))
                for c in range(2):
                    t = nc.scalar.copy(YE[:, c * 512:(c + 1) * 512], bank[2 + c][0:SLOTS, :])
                t.then_inc(ye_done, 1)

            def experts():
                tiles(3)
                load_gain(3)
                for m in range(NSPLIT):
                    high_part(0, m)
                act.wait_ge(gate_d, 1)
                nc.scalar.activation(GATE[:, :, 1:2], GATE[:, :, 0:1], ACT.Exp).then_inc(gate_e, 1)
                act.wait_ge(ye_done, 1)
                item(0, NSPLIT, True)
                with act.Fori(1, NE - 1) as e:
                    item(e, AHEAD, True)
                item(NE - 1, AHEAD, False)
                act.wait_ge(route_ok, 1)
                over = act.value_load(OVER[0:1, 0:1], min_val=0, max_val=T)
                with act.If(over > CAP):
                    for p in range(1, PASSES):
                        for m in range(AHEAD):
                            high_part(p * NE, m)
                        with act.Fori(0, NE - 1) as e:
                            item(e + p * NE, AHEAD, True)
                        item(p * NE + NE - 1, AHEAD, False)
                    act.wait_ge(acc_ps, TB * PASSES * NE)
                for b in range(TB):
                    square_out(3, (4, 5, 6, 7), b, (acc_ps, TB * (NE - 1) + b + 1))

            act.wait_ge(vec_in, 16)
            scan_tables(0, 0)
            scan_tables(0, 1)
            mixer(0)
            dense()
            mixer(1)
            experts()

        @block.gpsimd
        def _(pool):
            steps = [0]

            def rstd(blocks):
                for post, i, b in blocks:
                    pool.wait_ge(sq_done, norm_count(post, i, b))
                    v = STAT[:, 2 * b:2 * b + 1]
                    if post:
                        nc.gpsimd.tensor_tensor(STAT[:, 4 + b:5 + b], v, STAT[:, 2 * b + 1:2 * b + 2], ALU.add)\
                            .then_inc(var_done, 1)
                        steps[0] += 1
                        pool.wait_ge(var_done, steps[0])
                        v = STAT[:, 4 + b:5 + b]
                    nc.gpsimd.tensor_scalar(STAT[:, 6 + b:7 + b], v, 1.0 / D, EPS, ALU.mult, ALU.add).then_inc(var_done, 1)
                    steps[0] += 1
                    pool.wait_ge(var_done, steps[0])
                    if post:
                        pool.wait_ge(xn_done, TB * i + b + 1)
                    elif i:
                        pool.wait_ge(x_done, 4 * (i - 1) + 2 * b + 2)
                    nc.gpsimd.tensor_tensor(RSTD[:, b:b + 1], STAT[:, 6 + b:7 + b], EXPO[:, 0:1], ALU.pow).then_inc(rstd_done, 1)

            def mixer(l):
                if l == 0:
                    rstd(norm_order[0:2])
                for j in range(SJ):
                    pool.wait_ge(z_done, 8 * l + j + 1)
                    if j >= 2:
                        pool.wait_ge(y_done, 8 * l + j - 1)
                    z = Z[:, j % 2, :].rearrange("p (c t) -> p c t", c=2)
                    for dst, tab in ((ZC, COS), (ZS, SIN)):
                        t = nc.gpsimd.tensor_tensor(dst[:, j % 2, :].rearrange("p (c t) -> p c t", c=2), z,
                                                    tab[:, j, :].unsqueeze(1).to_broadcast([P, 2, T]), ALU.mult)
                    t.then_inc(zr_done, 1)
                    if j == 2:
                        pool.wait_ge(fz_v, 4 * l + 4)
                        pool.dma_start(c_dram[l, :, :, :], FG[:, 4:6, :]).then_inc(c_out, 16)
                    if j == 4:
                        pool.wait_ge(c_out, 16 * (l + 1))
                        for n, dst in enumerate((QA[DH:DH + 1, :, :], KA[DH + 1:DH + 2, :, :])):
                            pool.dma_start(dst, c_dram[l, :, n, :].unsqueeze(0)).then_inc(c_rows, 16)
                rstd(boundary[2 * l])

            def ones_rows(l):
                for n, m in enumerate((QA, KA)):
                    if n or l:
                        pool.wait_ge(aug_ones, 2 * l + n)
                    nc.gpsimd.memset(m[DH:DH + 2, :, :], 1.0).then_inc(aug_ones, 1)
                pool.wait_ge(aug_ones, 2 * l + 2)

            nc.gpsimd.memset(EXPO[:, :], -0.5).then_inc(expo_set, 1)
            pool.wait_ge(expo_set, 1)
            ones_rows(0)
            mixer(0)
            rstd(boundary[1])
            pool.wait_ge(rstd_done, norm_count(False, 2, 1))
            ones_rows(1)
            mixer(1)
            pool.wait_ge(rstd_done, norm_count(False, 3, 1))
            nc.gpsimd.memset(GT[:, :], 0.0).then_inc(gt_done, 1)
            pool.wait_ge(gt_done, 1)
            nc.gpsimd.memset(YE[:, :], 0.0).then_inc(ye_done, 1)
            rstd(norm_order[-2:])

        @block.vector
        def _(dve):
            links = [0]

            def link(t):
                t.then_inc(chain, 1)
                links[0] += 1
                dve.wait_ge(chain, links[0])

            TT, TS, STT = nc.vector.tensor_tensor, nc.vector.tensor_scalar, nc.vector.scalar_tensor_tensor

            def norm_rows(i, b):
                if i == 0:
                    dve.wait_ge(x_in[b], 16)
                else:
                    dve.wait_ge(ht_tr, 4 * i)
                dve.wait_ge(rstd_done, norm_count(False, i, b))
                TS(XN[:, b, :], X[:, b, :], RSTD[:, b:b + 1], None, ALU.mult).then_inc(xn_done, 1)

            def tiles(i, ks=(0, 1, 4, 5)):
                gain = par(i // 2, "g_ffn" if i % 2 else "g_mix")
                for k in ks:
                    dve.wait_ge(ht_tr, 4 * i + k // 2 + 1)
                    TS(HT[:, k, :], bank[k // 2][:, (k % 2) * T:(k % 2 + 1) * T], gain[:, k:k + 1], None, ALU.mult)\
                        .then_inc(ht_v, 1)

            def add_out(i, banks, b):
                dve.wait_ge(gb_in, 16 * (i + 1))
                dve.wait_ge(rstd_done, norm_count(True, i, b))
                for h in range(2):
                    if b:
                        dve.wait_ge(x_done, 4 * i + h + 1)
                    STT(TMP[:, h * 512:(h + 1) * 512], bank[banks[2 * b + h]][:, :], RSTD[:, b:b + 1],
                        GB[:, h * 512:(h + 1) * 512], ALU.mult, ALU.mult).then_inc(post_tmp, 1)
                for h in range(2):
                    dve.wait_ge(post_tmp, 4 * i + 2 * b + h + 1)
                    TT(X[:, b, h * 512:(h + 1) * 512], X[:, b, h * 512:(h + 1) * 512],
                       TMP[:, h * 512:(h + 1) * 512], ALU.add).then_inc(x_done, 1)

            def between(i, banks, meanwhile=None):
                for post, _, b in boundary[i]:
                    if post:
                        add_out(i, banks, b)
                    else:
                        if b and meanwhile:
                            meanwhile()
                        norm_rows(i + 1, b)

            def s(n):
                return SV[:, n, :]

            def scan_steps(l):
                a_re = par(l, "a_re")
                dve.wait_ge(trig_a, 4 * l + 1)
                if l:
                    dve.wait_ge(y_done, 8 * l)
                link(TS(s(1), s(0), 1.0, None, ALU.add))
                link(TS(s(2), s(0), -1.0, 1.0, ALU.mult, ALU.add))
                link(nc.vector.reciprocal(s(2), s(2)))
                link(TT(s(3), s(1), s(2), ALU.mult))
                for _ in range(3):
                    link(TT(s(3), s(3), s(3), ALU.mult))
                TT(s(5), a_re, s(3), ALU.mult).then_inc(trig_v, 1)

            def scan_phases(l, part):
                if part == 1:
                    link(TS(COS, COS, -ROUND, None, ALU.add))
                    for j in range(SJ):
                        t = STT(SIN[:, j, :], iota, s(10)[:, j:j + 1], COS[:, j, :], ALU.mult, ALU.subtract)
                    t.then_inc(trig_v, 1)
                    return
                a_im = par(l, "a_im")
                link(TT(s(9), a_im, s(3), ALU.mult))
                link(TS(s(10), s(9), 1.0 / (2.0 * math.pi), None, ALU.mult))
                link(TS(s(11), s(10), ROUND, None, ALU.add))
                link(TS(s(11), s(11), -ROUND, None, ALU.add))
                link(TT(s(10), s(10), s(11), ALU.subtract))
                for j in range(SJ):
                    t = TS(COS[:, j, :], iota, s(10)[:, j:j + 1], ROUND, ALU.mult, ALU.add)
                link(t)

            def scan_decay(l):
                dve.wait_ge(trig_a, 4 * l + 2)
                link(TS(s(7), s(6), -1.0, 1.0, ALU.mult, ALU.add))
                link(nc.vector.reciprocal(s(7), s(7)))
                link(STT(s(7), s(7), 2.0, s(6), ALU.mult, ALU.mult))
                link(TS(s(8), s(7), 1.0, None, ALU.add))
                dve.wait_ge(trig_a, 4 * l + 3)
                for h in range(2):
                    c = COS[:, 4 * h:4 * h + 4, :]
                    link(TT(c, c, c, ALU.mult))

            def scan_coefs(l):
                a_re, a_im = par(l, "a_re"), par(l, "a_im")
                dve.wait_ge(trig_a, 4 * l + 4)
                sin1 = SIN[:, :, 1]
                link(TS(s(12), COS[:, :, 1], -2.0, None, ALU.mult))
                link(TS(s(13), s(12), 1.0, None, ALU.add))
                link(TT(s(13), s(13), s(7), ALU.mult))
                link(TT(s(13), s(13), s(12), ALU.add))
                link(TT(s(14), s(8), sin1, ALU.mult))
                link(TT(s(15), a_re, a_re, ALU.mult))
                link(TT(s(16), a_im, a_im, ALU.mult))
                link(TT(s(15), s(15), s(16), ALU.add))
                link(nc.vector.reciprocal(s(15), s(15)))
                link(TT(s(16), s(13), a_re, ALU.mult))
                link(TT(s(17), s(14), a_im, ALU.mult))
                link(TT(s(16), s(16), s(17), ALU.add))
                link(TT(s(16), s(16), s(15), ALU.mult))
                link(TT(s(17), s(14), a_re, ALU.mult))
                link(TT(s(18), s(13), a_im, ALU.mult))
                link(TT(s(17), s(17), s(18), ALU.subtract))
                link(TT(s(17), s(17), s(15), ALU.mult))

            def scan_outputs(l):
                for h in range(2):
                    c = COS[:, 4 * h:4 * h + 4, :]
                    link(TS(c, c, -2.0, 1.0, ALU.mult, ALU.add))
                cr = par(l, "c_re").rearrange("p (j c) -> p j c", j=SJ)
                ci = par(l, "c_im").rearrange("p (j c) -> p j c", j=SJ)
                re = s(16).unsqueeze(2).to_broadcast([P, SJ, SCH])
                im = s(17).unsqueeze(2).to_broadcast([P, SJ, SCH])
                link(TT(CT[:, 0, :, :], cr, re, ALU.mult))
                link(TT(CT[:, 1, :, :], ci, im, ALU.mult))
                link(TT(CC[:, 0, :, :], CT[:, 0, :, :], CT[:, 1, :, :], ALU.subtract))
                link(TT(CT[:, 0, :, :], cr, im, ALU.mult))
                link(TT(CT[:, 1, :, :], ci, re, ALU.mult))
                link(TT(CT[:, 0, :, :], CT[:, 0, :, :], CT[:, 1, :, :], ALU.add))
                link(TS(CC[:, 2, :, :], CT[:, 0, :, :], -1.0, None, ALU.mult))
                TS(CC[:, 1, :, :], CC[:, 0, :, :], -1.0, None, ALU.mult).then_inc(tab_ok, 1)

            def scan_tile(l, j):
                dve.wait_ge(bu_done, 8 * l + j + 1)
                bu = bank[4 + j % 2][:, :].rearrange("p (c t) -> p c t", c=2)
                for n, tab in enumerate((COS, SIN)):
                    t = TT(ROT[:, n, :].rearrange("p (c t) -> p c t", c=2), bu,
                           tab[:, j, :].unsqueeze(1).to_broadcast([P, 2, T]), ALU.mult)
                t.then_inc(rot_done, 1)
                dve.wait_ge(rot_done, 8 * l + j + 1)
                TT(ZIN[:, 0:T], ROT[:, 0, 0:T], ROT[:, 1, T:2 * T], ALU.add)
                TT(ZIN[:, T:2 * T], ROT[:, 0, T:2 * T], ROT[:, 1, 0:T], ALU.subtract).then_inc(zin_done, 1)
                dve.wait_ge(zin_done, 8 * l + j + 1)
                if j >= 2:
                    dve.wait_ge(zr_done, 8 * l + j - 1)
                r = SV[:, 8, j:j + 1].to_broadcast([P, T])
                for c in range(2):
                    t = nc.vector.tensor_tensor_scan(Z[:, j % 2, c * T:(c + 1) * T], r, ZIN[:, c * T:(c + 1) * T], 0.0,
                                                     ALU.mult, ALU.add)
                t.then_inc(z_done, 1)

            def branch_norm(l, n, src, width):
                dve.wait_ge(bss_ps, 3 * l + n + 1)
                link(TS(RB[:, n, :], src, 1.0 / width, EPS, ALU.mult, ALU.add))
                nc.vector.reciprocal(RB[:, n, :], RB[:, n, :]).then_inc(bvar, 1)

            def branch_scale(l, n, tiles):
                dve.wait_ge(brs, 3 * l + n + 1)
                dve.wait_ge(bsq, 3 * l + n + 1)
                g = par(l, "g_br")
                for k in tiles:
                    STT(MT[:, k, :], MT[:, k, :], g[:, k:k + 1], RB[:, n, :], ALU.mult, ALU.mult).then_inc(mtn, 1)

            def softmax_max(l, n):
                dve.wait_ge(sc_ps, 6 * l + n + 1)
                bk = bank[SCORE_BANK[n]]
                heads, width = (4, P) if n < 2 else (2, T)
                at = 4 * n if n < 2 else 8 + 2 * (n - 2)
                sc = bk[:, :].rearrange("p (h k) -> p h k", h=heads)
                diag = sc[:, :, width - P:width]
                TT(diag, diag, mask.unsqueeze(1).to_broadcast([P, heads, P]), ALU.add).then_inc(msk_done, 1)
                dve.wait_ge(msk_done, 6 * l + n + 1)
                nc.vector.tensor_reduce(MX[:, at:at + heads], sc, AX, ALU.max, negate=True).then_inc(mx_done, 1)

            def softmax_scale(l, n):
                dve.wait_ge(ex_done, 6 * l + n + 1)
                heads, width = (4, P) if n < 2 else (2, T)
                at = 4 * n if n < 2 else 8 + 2 * (n - 2)
                nc.vector.reciprocal(RS[:, at:at + heads], SUM[:, at:at + heads]).then_inc(rs_done, 1)
                dve.wait_ge(rs_done, 6 * l + n + 1)
                p = P0[:, at:at + heads, :] if n < 2 else P1[:, at - 8:at - 8 + heads, :]
                TT(p, p, RS[:, at:at + heads].unsqueeze(2).to_broadcast([P, heads, width]), ALU.mult).then_inc(pn_done, 1)

            def mixer(l):
                if l == 0:
                    norm_rows(0, 0)
                    norm_rows(0, 1)
                tiles(2 * l)
                if l == 0:
                    scan_phases(0, 0)
                    scan_phases(0, 1)
                    dve.wait_ge(par_in, 16)
                    dve.wait_ge(cst_in, 16)
                    scan_decay(0)
                    scan_coefs(0)
                    scan_outputs(0)
                scan_tile(l, 0)
                dve.wait_ge(fz_a, 3 * l + 1)
                TS(FG[:, 3, :], bank[6][0:HEADS, 0:T], par(l, "b_forget")[0:HEADS, :], 0.0, ALU.add, ALU.min)\
                    .then_inc(fz_v, 1)
                scan_tile(l, 1)
                dve.wait_ge(fz_a, 3 * l + 3)
                dve.wait_ge(fz_v, 4 * l + 1)
                TT(FG[:, 3, :], FG[:, 3, :], FG[:, 2, :], ALU.subtract).then_inc(fz_v, 1)
                dve.wait_ge(fz_v, 4 * l + 2)
                nc.vector.tensor_tensor_scan(FG[:, 4, :], ones[0:HEADS, 0:1].to_broadcast([HEADS, T]), FG[:, 3, :], 0.0,
                                             ALU.mult, ALU.add).then_inc(fz_v, 1)
                dve.wait_ge(fz_v, 4 * l + 3)
                TS(FG[:, 5, :], FG[:, 4, :], -1.0, None, ALU.mult).then_inc(fz_v, 1)
                for j in range(2, SJ):
                    scan_tile(l, j)
                for n in range(4):
                    softmax_max(l, n)
                dve.wait_ge(y_done, 8 * (l + 1))
                d = par(l, "ssm_d")
                for a in range(2):
                    t = STT(YS[:, a, :], UT[:, a, :], d[:, a:a + 1], bank[6][:, a * T:(a + 1) * T], ALU.mult, ALU.add)
                t.then_inc(ys_done, 1)
                for n in (4, 5):
                    softmax_max(l, n)
                for n in range(6):
                    softmax_scale(l, n)
                dve.wait_ge(sg_done, l + 1)
                TT(MT[:, 6:8, :], GY[:, :, :], SG[:, :, :], ALU.mult).then_inc(mt_ssm, 1)
                branch_norm(l, 0, bank[6][:, 0:T], NG * GC)
                branch_scale(l, 0, (4, 5))
                for m in range(2):
                    if m == 1:
                        branch_norm(l, 1, bank[6][:, T:2 * T], SJ * SCH)
                        branch_scale(l, 1, (6, 7))
                    dve.wait_ge(ot_ps, 2 * l + m + 1)
                    nc.vector.tensor_copy(MT[:, 2 * m:2 * m + 2, :], bank[2 + m][:, :].rearrange("p (a t) -> p a t", a=2))\
                        .then_inc(ot_done, 1)
                branch_norm(l, 2, bank[5][:, 0:T], HEADS * DH)
                branch_scale(l, 2, (0, 1, 2, 3))

            def dense():
                def rest(m):
                    dve.wait_ge(dh_done, m + 1)
                    TT(WL[:, m % NSPLIT, :], RING[:, (BASE_DENSE + m) % NSLOT, :], WH[:, m % NSPLIT, :].bitcast(F32),
                       ALU.subtract).then_inc(slabs_used, 1)

                def activations_unit(u):
                    dve.wait_ge(silu_d, u + 1)
                    for j in range(2):
                        t = TT(SA[:, j, :], SA[:, j, :], bank[2 * (u % 2) + j][:, T:2 * T], ALU.mult)
                    t.then_inc(prod_d, 1)
                    dve.wait_ge(prod_d, u + 1)
                    if u:
                        dve.wait_ge(dm_used, AT_DENSE["d", u - 1] + 1)
                    nc.vector.tensor_copy(DAH[:, :, :], SA[:, :, :]).then_inc(dah_d, 1)
                    dve.wait_ge(dah_d, u + 1)
                    TT(DAL[:, :, :], SA[:, :, :], DAH[:, :, :].bitcast(F32), ALU.subtract).then_inc(dal_d, 1)

                between(0, MIX_BANKS, lambda: rest(0))
                rest(1)
                gain = par(0, "g_ffn")
                for k in range(KT):
                    dve.wait_ge(hth_done, k // 2 + 1)
                    t = STT(HTL[:, k, :], bank[k // 2][:, (k % 2) * T:(k % 2 + 1) * T], gain[:, k:k + 1],
                            HTH[:, k, :].bitcast(F32), ALU.mult, ALU.subtract)
                    if k % 2:
                        t.then_inc(htl_done, 1)
                for m in range(2, DENSE_SLABS):
                    rest(m)
                    if m >= 4 and m % 3 == 1:
                        activations_unit((m - 4) // 3)
                    if m == 6:
                        scan_steps(1)
                    if m in (9, 10):
                        scan_phases(1, m - 9)
                    if m == 18:
                        scan_decay(1)
                    if m == 21:
                        scan_coefs(1)
                    if m == 24:
                        scan_outputs(1)
                activations_unit(DENSE_UNITS - 1)
                between(1, (4, 5, 6, 7))

            def routing():
                dve.wait_ge(lg_ps, 1)
                link(nc.vector.tensor_copy(LG[:, :, :], bank[0][:, 0:TB * NE].rearrange("p (b e) -> p b e", b=TB)))
                for b in range(TB):
                    link(nc.vector.max(M8[:, b, :], LG[:, b, :]))
                    link(nc.vector.max_index(I8[:, b, :], M8[:, b, :], LG[:, b, :]))
                TT(GATE[:, :, 0:1], M8[:, :, 1:2], M8[:, :, 0:1], ALU.subtract).then_inc(gate_d, 1)
                link(nc.vector.tensor_copy(IF8[:, :, :], I8[:, :, :]))
                for c in range(2):
                    for b in range(TB):
                        link(TS(OH[:, c, b, :], iota[:, 0:NE], IF8[:, b, c:c + 1], None, ALU.is_equal))
                TT(SEL[:, :, :], OH[:, 0, :, :], OH[:, 1, :, :], ALU.add).then_inc(sel_done, 1)
                dve.wait_ge(gate_e, 1)
                link(TS(GATE[:, :, 2:3], GATE[:, :, 1:2], 1.0, None, ALU.add))
                link(nc.vector.reciprocal(GATE[:, :, 2:3], GATE[:, :, 2:3]))
                link(TT(GATE[:, :, 3:4], GATE[:, :, 1:2], GATE[:, :, 2:3], ALU.mult))
                for b in range(TB):
                    link(TS(CMB[:, b, 0:NE], OH[:, 0, b, :], GATE[:, b, 2:3], None, ALU.mult))
                    link(STT(CMB[:, b, 0:NE], OH[:, 1, b, :], GATE[:, b, 3:4], CMB[:, b, 0:NE], ALU.mult, ALU.add))
                dve.wait_ge(pos_ps, 1)
                dve.wait_ge(sel_done, 1)
                link(STT(POS[:, :, 0:NE], bank[3][:, 0:TB * NE].rearrange("p (b e) -> p b e", b=TB), 1.0, SEL[:, :, :],
                         ALU.add, ALU.mult))
                link(TS(POS[:, :, 0:NE], POS[:, :, 0:NE], -1.0, None, ALU.add))
                for p in range(1, PASSES):
                    TS(POS[:, :, p * NE:(p + 1) * NE], POS[:, :, 0:NE], -float(p * CAP), None, ALU.add)
                    nc.vector.tensor_copy(CMB[:, :, p * NE:(p + 1) * NE], CMB[:, :, 0:NE])
                link(nc.vector.tensor_reduce(CNT[:, 0:1], bank[3][:, 2 * NE:3 * NE], AX, ALU.max))
                nc.vector.tensor_copy(OVER[:, :], CNT[:, 0:1]).then_inc(route_ok, 1)

            def one_hot(dst, i, weighted):
                for b in range(TB):
                    pos = POS[:, b, bass.ds(i, 1)]
                    if weighted:
                        t = TS(dst[:, b, :], slots, pos, CMB[:, b, bass.ds(i, 1)], ALU.is_equal, ALU.mult)
                    else:
                        t = TS(dst[:, b, :], slots, pos, None, ALU.is_equal)
                return t

            def gathered(i, h):
                gain = par(1, "g_ffn")
                src = bank[h][:, 0:4 * SLOTS].rearrange("p (k s) -> p k s", k=4)
                dve.wait_ge(ga_ps, i * 2 + (h + 1))
                TT(XGH[:, 4 * h:4 * h + 4, :], src, gain[:, 4 * h:4 * h + 4].unsqueeze(2).to_broadcast([P, 4, SLOTS]),
                   ALU.mult).then_inc(xgh_done, 1)
                dve.wait_ge(xgh_done, i * 2 + (h + 1))
                for k in range(4):
                    kt = 4 * h + k
                    t = STT(XGL[:, kt, :], src[:, k, :], gain[:, kt:kt + 1], XGH[:, kt, :].bitcast(F32),
                            ALU.mult, ALU.subtract)
                t.then_inc(xg_done, 1)

            def product(i, u):
                dve.wait_ge(silu_m, i * UNITS + (u + 1))
                TT(HM[:, :], SM[:, :], bank[u % 2][0:SLOTS, W_COLS:2 * W_COLS], ALU.mult).then_inc(h_done, 1)

            def activations(i, u):
                dve.wait_ge(t_ps, i * UNITS + (u + 1))
                src = bank[u % 2][:, 0:2 * SLOTS].rearrange("p (j s) -> p j s", j=2)
                nc.vector.tensor_copy(ATH[:, :, :], src).then_inc(ath_done, 1)
                dve.wait_ge(ath_done, i * UNITS + (u + 1))
                TT(ATL[:, :, :], src, ATH[:, :, :].bitcast(F32), ALU.subtract).then_inc(at_done, 1)

            def rest_part(i, m):
                dve.wait_ge(wh_done, i * MOE_SLABS + (m + 1))
                TT(WL[:, m % NSPLIT, :], RING[:, (BASE_MOE + m) % NSLOT, :], WH[:, m % NSPLIT, :].bitcast(F32),
                   ALU.subtract).then_inc(slabs_used, 1)

            def item(i, first, ahead):
                for m in range(MOE_SLABS):
                    if m >= first:
                        rest_part(i, m)
                    if m >= 3 and m % 3 == 0:
                        product(i, m // 3 - 1)
                    if m >= 4 and m % 3 == 1:
                        activations(i, (m - 4) // 3)
                    if m == 11:
                        if ahead:
                            one_hot(GM, i + 1, False).then_inc(g_done, 1)
                        one_hot(GW, i, True).then_inc(gw_done, 1)
                product(i, UNITS - 1)
                activations(i, UNITS - 1)
                nc.vector.tensor_copy(GT[:, :], bank[(UNITS - 1) % 2][0:SLOTS, T:2 * T]).then_inc(gt_done, 1)
                if ahead:
                    gathered(i + 1, 0)
                    rest_part(i + 1, 0)
                    gathered(i + 1, 1)
                    for m in range(1, AHEAD):
                        rest_part(i + 1, m)

            def experts():
                between(2, MIX_BANKS)
                tiles(3)
                rest_part(0, 0)
                routing()
                dve.wait_ge(route_ok, 1)
                one_hot(GM, 0, False).then_inc(g_done, 1)
                rest_part(0, 1)
                gathered(0, 0)
                gathered(0, 1)
                rest_part(0, 2)
                item(0, NSPLIT, True)
                with dve.Fori(1, NE - 1) as e:
                    item(e, AHEAD, True)
                item(NE - 1, AHEAD, False)
                over = dve.value_load(OVER[0:1, 0:1], min_val=0, max_val=T)
                with dve.If(over > CAP):
                    for p in range(1, PASSES):
                        one_hot(GM, p * NE, False).then_inc(g_done, 1)
                        gathered(p * NE, 0)
                        gathered(p * NE, 1)
                        for m in range(AHEAD):
                            rest_part(p * NE, m)
                        with dve.Fori(0, NE - 1) as e:
                            item(e + p * NE, AHEAD, True)
                        item(p * NE + NE - 1, AHEAD, False)
                    dve.wait_ge(acc_ps, TB * PASSES * NE)
                for b in range(TB):
                    add_out(3, (4, 5, 6, 7), b)

            dve.wait_ge(vec_in, 16)
            dve.wait_ge(id_in, 16)
            scan_steps(0)
            mixer(0)
            dense()
            mixer(1)
            experts()


def shape_constants():
    c = np.zeros((P, NCONST), np.float32)
    c[:, C_ID:C_ID + P] = np.eye(P)
    c[:, C_MASK:C_MASK + P] = np.triu(np.full((P, P), NEG), 1)
    c[:, C_TRI:C_TRI + P] = np.triu(np.ones((P, P)), 1)
    c[:, C_ONES:C_ONES + P] = 1.0
    c[:, C_IOTA:C_IOTA + T] = np.arange(T)
    c[:, C_SLOT:C_SLOT + SLOTS] = np.where(np.arange(SLOTS) < CAP, np.arange(SLOTS), -9.0 * T)
    t = np.arange(T)
    for g, w in enumerate(WINDOWS):
        inside = (t[None, :] >= t[:, None]) & (t[None, :] - t[:, None] < w)
        a = inside / np.minimum(t + 1.0, w)[None, :] - np.eye(T)
        for n, (s, u) in enumerate(((0, 0), (0, 1), (1, 1))):
            at = C_BAND + (3 * g + n) * P
            c[:, at:at + P] = a[s * P:(s + 1) * P, u * P:(u + 1) * P]
    return c


def pack_params(a):
    out = np.zeros((P, LAYERS, NPAR), np.float32)
    for l in range(LAYERS):
        def put(name, v):
            lo, hi = _off[name]
            out[:v.shape[0], l, lo:hi] = v

        def columns(v):
            return v.reshape(-1, P).T

        put("g_mix", columns(a["norm_mix_pre"][l]))
        put("g_ffn", columns(a["norm_ffn_pre"][l]))
        put("g_br", columns(np.concatenate([a["branch_norm_attn"][l], a["branch_norm_pool"][l], a["branch_norm_ssm"][l]])))
        put("pool_scale", columns(a["pool_scale"][l]))
        put("ssm_d", columns(a["ssm_d"][l].reshape(-1)))
        put("b_glu", columns(a["ssm_b_glu"][l]))
        put("b_forget", a["b_forget"][l].reshape(HEADS, 1))
        put("a_re", columns(a["ssm_a_re"][l].reshape(-1)))
        put("a_im", columns(a["ssm_a_im"][l].reshape(-1)))
        put("log_dt", columns(np.repeat(a["ssm_log_dt"][l], 64)))
        put("w_f", a["w_in"][l][:, F_OFF:P_OFF].reshape(KT, P, HEADS).transpose(1, 0, 2).reshape(P, -1))
        put("router", a["moe_router"][l // 2].reshape(KT, P, NE).transpose(1, 0, 2).reshape(P, -1))
        for name, key in (("b_re", "ssm_b_re"), ("b_im", "ssm_b_im")):
            m = np.zeros((P, 2, P), np.float32)
            for g in range(16):
                j, o = g // 2, g % 2
                r = SCH * (j % 4) + 16 * o
                m[r:r + 16, j // 4, 64 * o:64 * o + 64] = a[key][l, g].T
            put(name, m.reshape(P, -1))
        for name, key in (("c_re", "ssm_c_re"), ("c_im", "ssm_c_im")):
            m = np.zeros((P, SJ, SCH), np.float32)
            for g in range(16):
                j, o = g // 2, g % 2
                m[64 * o:64 * o + 64, j, 16 * o:16 * o + 16] = a[key][l, g].T
            put(name, m.reshape(P, -1))
        m = np.zeros((P, 2, P), np.float32)
        for g in range(NG):
            o = GC * (g % 2)
            m[o:o + GC, g // 2, o:o + GC] = a["pool_w"][l, g]
        put("pool_w", m.reshape(P, -1))
        put("w_glu", a["ssm_w_glu"][l].reshape(2, P, T).transpose(1, 0, 2).reshape(P, -1))
    return out


def kernel(**inputs):
    from concourse import bacc
    from concourse.bass_utils import run_bass_kernel_spmd

    a = {k: np.asarray(v) for k, v in inputs.items()}
    post = np.stack([a["norm_mix_post"][0], a["norm_ffn_post"][0], a["norm_mix_post"][1], a["norm_ffn_post"][1]])
    arrays = {
        "x": a["x"][0], "w_in": a["w_in"], "w_out": a["w_out"],
        "ffn_gate": a["ffn_w_gate"][0], "ffn_up": a["ffn_w_up"][0], "ffn_down": a["ffn_w_down"][0],
        "moe_gate": a["moe_w_gate"][0], "moe_up": a["moe_w_up"][0], "moe_down": a["moe_w_down"][0],
        "g_post": np.broadcast_to(post[:, None, :], (4, P, D)),
        "params": pack_params(a), "consts": shape_constants(),
    }
    arrays = {k: np.ascontiguousarray(v) for k, v in arrays.items()}
    nc = bacc.Bacc("TRN2", target_bir_lowering=False, num_devices=1)
    args = [nc.dram_tensor(k, v.shape, F32, kind="ExternalInput").ap() for k, v in arrays.items()]
    args.append(nc.dram_tensor("c_scratch", (LAYERS, HEADS, 2, T), F32, kind="Internal").ap())
    out = nc.dram_tensor("out", (T, D), F32, kind="ExternalOutput").ap()
    build(nc, *args, out)
    r = run_bass_kernel_spmd(nc, [arrays], core_ids=[0])
    return r.results[0]["out"].reshape(1, T, D)
```
